# Optimizing a Trainium2 kernel written in Bass

```python
import jax, jax.numpy as jnp
from jax import lax
import numpy as np

D_MODEL = 1024
BATCH = 1
SEQ = 512
DEPTH = 2
DEC_BATCH = 1
DEC_SEQ = 32
PAST_LEN = 256

CHUNK = 64
QBLOCK = 128
NORM_EPS = 1e-6
MLA_HEADS = 8
Q_LORA = 384
KV_LORA = 256
NOPE_DIM = 64
ROPE_DIM = 32
V_HEAD = 64
ROPE_THETA = 10000.0
SM_SCALE = (NOPE_DIM + ROPE_DIM) ** -0.5
RWKV_HEADS = 4
RWKV_HEAD = 64
RWKV_DIM = RWKV_HEADS * RWKV_HEAD
W_LORA = 64
A_LORA = 64
G_LORA = 128
RWKV_IN = 3 * RWKV_DIM + W_LORA + A_LORA + G_LORA
GN_EPS = 64e-5
CONV_DIM = 256
CONV_WIDTH = 31
LN_EPS = 1e-5
N_BRANCH = 3
MLA_IN = Q_LORA + KV_LORA + ROPE_DIM
IN_COLS = MLA_IN + RWKV_IN + 2 * CONV_DIM + N_BRANCH * D_MODEL
N_MOD = 6
N_GROUPS = 4
EXPERTS_PER_GROUP = 4
N_EXPERTS = N_GROUPS * EXPERTS_PER_GROUP
TOP_K = 2
D_EXPERT = 256

kernel_name = "hybrid_mla_rwkv7_conformer_hmoe_stream_step"

def rmsnorm(x, g):
    xf = x.astype(jnp.float32)
    y = xf * lax.rsqrt(jnp.mean(xf * xf, axis=-1, keepdims=True) + NORM_EPS)
    return (y * g.astype(jnp.float32)).astype(x.dtype)

def layernorm(x, g, b):
    xf = x.astype(jnp.float32)
    mu = jnp.mean(xf, axis=-1, keepdims=True)
    var = jnp.mean(jnp.square(xf - mu), axis=-1, keepdims=True)
    y = (xf - mu) * lax.rsqrt(var + LN_EPS) * g.astype(jnp.float32) + b.astype(jnp.float32)
    return y.astype(x.dtype)

def rope(x, pos):
    half = ROPE_DIM // 2
    inv = ROPE_THETA ** (-jnp.arange(half, dtype=jnp.float32) / half)
    ang = pos.astype(jnp.float32)[:, None] * inv[None, :]
    shape = (1, pos.shape[0]) + (1,) * (x.ndim - 3) + (half,)
    cos, sin = jnp.cos(ang).reshape(shape), jnp.sin(ang).reshape(shape)
    xf = x.astype(jnp.float32)
    x1, x2 = xf[..., :half], xf[..., half:]
    return jnp.concatenate([x1 * cos - x2 * sin, x1 * sin + x2 * cos], axis=-1).astype(x.dtype)

def chunk_causal_attend(q_lat, q_rope, q_pos, k_lat, k_rope, k_pos):
    B, T, H, C = q_lat.shape
    qb = min(QBLOCK, T)
    nb = T // qb
    k_chunk = k_pos // CHUNK

    def block(args):
        ql, qr, qp = args
        s = (jnp.einsum('bqhc,bkc->bhqk', ql, k_lat).astype(jnp.float32)
             + jnp.einsum('bqhr,bkr->bhqk', qr, k_rope).astype(jnp.float32)) * SM_SCALE
        visible = k_chunk[None, :] <= (qp // CHUNK)[:, None]
        s = jnp.where(visible[None, None], s, -jnp.inf)
        p = jax.nn.softmax(s, axis=-1).astype(k_lat.dtype)
        return jnp.einsum('bhqk,bkc->bqhc', p, k_lat)

    split = lambda t: jnp.moveaxis(t.reshape((B, nb, qb) + t.shape[2:]), 1, 0)
    out = lax.map(block, (split(q_lat), split(q_rope), q_pos.reshape(nb, qb)))
    return jnp.moveaxis(out, 0, 1).reshape(B, T, H, C)

def mla_branch(p_q, p_kv, p_kr, cache_lat, cache_rope, lp):
    B, T, _ = p_q.shape
    P = cache_lat.shape[1]
    pos = P + jnp.arange(T)
    q = (rmsnorm(p_q, lp['q_norm_g']) @ lp['q_up']).reshape(B, T, MLA_HEADS, NOPE_DIM + ROPE_DIM)
    q_nope, q_rope = q[..., :NOPE_DIM], rope(q[..., NOPE_DIM:], pos)
    lat = rmsnorm(p_kv, lp['kv_norm_g'])
    kr = rope(p_kr, pos)
    k_lat = jnp.concatenate([cache_lat.astype(lat.dtype), lat], axis=1)
    k_rope = jnp.concatenate([cache_rope.astype(kr.dtype), kr], axis=1)
    q_lat = jnp.einsum('bthn,chn->bthc', q_nope, lp['w_uk'])
    o_lat = chunk_causal_attend(q_lat, q_rope, pos, k_lat, k_rope, jnp.arange(P + T))
    o = jnp.einsum('bthc,chv->bthv', o_lat, lp['w_uv']).reshape(B, T, MLA_HEADS * V_HEAD)
    return o @ lp['proj_a'], lat, kr

def wkv_scan(S0, r, w, k, v, kk, a):
    def step(S, inp):
        r_t, w_t, k_t, v_t, kk_t, a_t = inp
        sa = jnp.einsum('bhij,bhj->bhi', S, -kk_t)
        S = (S * w_t[:, :, None, :] + sa[..., None] * (kk_t * a_t)[:, :, None, :]
             + v_t[..., None] * k_t[:, :, None, :])
        return S, jnp.einsum('bhij,bhj->bhi', S, r_t)
    xs = tuple(jnp.moveaxis(t, 1, 0) for t in (r, w, k, v, kk, a))
    S, ys = lax.scan(step, S0, xs)
    return S, jnp.moveaxis(ys, 0, 1)

def rwkv_branch(pr, shift_st, wkv_st, lp):
    B, T, _ = pr.shape
    f32 = jnp.float32
    prev = jnp.concatenate([shift_st[:, None, :].astype(pr.dtype), pr[:, :-1]], axis=1)
    xs = pr + (prev - pr) * lp['rwkv_mu']
    o1 = RWKV_DIM
    r, k, v, wl, al, gl = jnp.split(xs, [o1, 2 * o1, 3 * o1, 3 * o1 + W_LORA, 3 * o1 + W_LORA + A_LORA], axis=-1)
    heads = lambda t: t.astype(f32).reshape(B, T, RWKV_HEADS, RWKV_HEAD)
    z = (lp['rwkv_w0'] + jnp.tanh(wl) @ lp['rwkv_w2']).astype(f32)
    decay = jnp.exp(-jnp.exp(-jax.nn.softplus(-z) - 0.5))
    a = jax.nn.sigmoid((lp['rwkv_a0'] + al @ lp['rwkv_a2']).astype(f32))
    g = (jax.nn.sigmoid(gl) @ lp['rwkv_g2']).astype(f32)
    kf = k.astype(f32)
    kk = heads(kf * lp['rwkv_k_k'])
    kk = kk * lax.rsqrt(jnp.sum(kk * kk, axis=-1, keepdims=True) + 1e-12)
    kf = kf * (1.0 + (a - 1.0) * lp['rwkv_k_a'])
    rh, kh, vh, ah, wh = heads(r), heads(kf), heads(v), heads(a), heads(decay)
    S, y = wkv_scan(wkv_st.astype(f32), rh, wh, kh, vh, kk, ah)
    mu = jnp.mean(y, axis=-1, keepdims=True)
    var = jnp.mean(jnp.square(y - mu), axis=-1, keepdims=True)
    y = ((y - mu) * lax.rsqrt(var + GN_EPS)).reshape(B, T, RWKV_DIM)
    y = y * lp['rwkv_ln_g'].astype(f32) + lp['rwkv_ln_b'].astype(f32)
    bonus = jnp.sum(rh * kh * lp['rwkv_r_k'].astype(f32), axis=-1, keepdims=True) * vh
    y = (y + bonus.reshape(B, T, RWKV_DIM)) * g
    return y.astype(pr.dtype) @ lp['proj_b'], pr[:, -1], S.astype(pr.dtype)

def conv_branch(pc, conv_st, lp):
    glu = pc[..., :CONV_DIM] * jax.nn.sigmoid(pc[..., CONV_DIM:])
    buf = jnp.concatenate([conv_st.astype(glu.dtype), glu], axis=1)
    y = lax.conv_general_dilated(buf, lp['conv_dw'][:, None, :], window_strides=(1,), padding='VALID',
                                 dimension_numbers=('NWC', 'WIO', 'NWC'), feature_group_count=CONV_DIM)
    y = jax.nn.silu(layernorm(y + lp['conv_dw_b'], lp['conv_ln_g'], lp['conv_ln_b']))
    return y @ lp['proj_c'], buf[:, -(CONV_WIDTH - 1):]

def hier_moe(h, lp):
    f32 = jnp.float32
    B, T, _ = h.shape
    g_prob = jax.nn.softmax((h @ lp['router_group_w'] + lp['router_group_b']).astype(f32), axis=-1)
    g_val, g_idx = lax.top_k(g_prob, 1)
    e_logits = (h @ lp['router_expert_w'] + lp['router_expert_b']).astype(f32)
    e_logits = e_logits.reshape(B, T, N_GROUPS, EXPERTS_PER_GROUP)
    in_group = jnp.einsum('btg,btge->bte', jax.nn.one_hot(g_idx[..., 0], N_GROUPS, dtype=f32), e_logits)
    e_val, e_idx = lax.top_k(in_group, TOP_K)
    weights = g_val * jax.nn.softmax(e_val, axis=-1)
    expert_id = g_idx * EXPERTS_PER_GROUP + e_idx
    combine = jnp.einsum('btk,btke->bte', weights, jax.nn.one_hot(expert_id, N_EXPERTS, dtype=f32)).astype(h.dtype)
    gate = jnp.einsum('btd,edf->btef', h, lp['moe_w_gate'])
    up = jnp.einsum('btd,edf->btef', h, lp['moe_w_up'])
    act = jax.nn.silu(gate) * up * combine[..., None]
    return jnp.einsum('btef,efd->btd', act, lp['moe_w_down'])

def trunk_layer(x, c, cache_lat, cache_rope, shift_st, wkv_st, conv_st, lp):
    B, T, D = x.shape
    mod = (jax.nn.silu(c) @ lp['ada_w'] + lp['ada_b']).reshape(B, N_MOD, D)
    sh1, sc1, gt1, sh2, sc2, gt2 = [mod[:, i, None, :] for i in range(N_MOD)]
    h = rmsnorm(x, lp['norm1_g']) * (1 + sc1) + sh1
    p = h @ lp['w_in']
    cuts = [Q_LORA, Q_LORA + KV_LORA, MLA_IN, MLA_IN + RWKV_IN, MLA_IN + RWKV_IN + 2 * CONV_DIM]
    p_q, p_kv, p_kr, p_rw, p_cv, p_gate = jnp.split(p, cuts, axis=-1)
    o_a, lat, kr = mla_branch(p_q, p_kv, p_kr, cache_lat, cache_rope, lp)
    o_b, shift_new, wkv_new = rwkv_branch(p_rw, shift_st, wkv_st, lp)
    o_c, conv_new = conv_branch(p_cv, conv_st, lp)
    gates = jax.nn.sigmoid(p_gate).reshape(B, T, N_BRANCH, D)
    merged = gates[:, :, 0] * o_a + gates[:, :, 1] * o_b + gates[:, :, 2] * o_c
    x = x + gt1 * (merged @ lp['w_out'])
    h2 = rmsnorm(x, lp['norm2_g']) * (1 + sc2) + sh2
    x = x + gt2 * hier_moe(h2, lp)
    return x, (lat, kr, shift_new, wkv_new, conv_new)

def setup_inputs(seed: int = 0) -> dict:
    key = jax.random.key(seed)
    ks = iter(jax.random.split(key, 64))
    nrm = lambda shape, std: std * jax.random.normal(next(ks), shape, jnp.float32)
    L, D = DEPTH, D_MODEL
    return {
        'x_prompt': nrm((BATCH, SEQ, D), 1.0),
        'x_sample': nrm((DEC_BATCH, DEC_SEQ, D), 1.0),
        'c_prompt': nrm((BATCH, D), 1.0),
        'c_sample': nrm((DEC_BATCH, D), 1.0),
        'cache_kv_latent': nrm((L, DEC_BATCH, PAST_LEN, KV_LORA), 1.0),
        'cache_k_rope': nrm((L, DEC_BATCH, PAST_LEN, ROPE_DIM), 1.0),
        'state_rwkv_shift': nrm((L, DEC_BATCH, RWKV_IN), 1.0),
        'state_rwkv_wkv': nrm((L, DEC_BATCH, RWKV_HEADS, RWKV_HEAD, RWKV_HEAD), 0.5),
        'state_conv': nrm((L, DEC_BATCH, CONV_WIDTH - 1, CONV_DIM), 0.5),
        'ada_w': nrm((L, D, N_MOD * D), 0.5 * D ** -0.5),
        'ada_b': nrm((L, N_MOD * D), 0.02),
        'norm1_g': 1.0 + nrm((L, D), 0.05),
        'norm2_g': 1.0 + nrm((L, D), 0.05),
        'w_in': nrm((L, D, IN_COLS), D ** -0.5),
        'q_norm_g': 1.0 + nrm((L, Q_LORA), 0.05),
        'q_up': nrm((L, Q_LORA, MLA_HEADS * (NOPE_DIM + ROPE_DIM)), Q_LORA ** -0.5),
        'kv_norm_g': 1.0 + nrm((L, KV_LORA), 0.05),
        'w_uk': nrm((L, KV_LORA, MLA_HEADS, NOPE_DIM), KV_LORA ** -0.5),
        'w_uv': nrm((L, KV_LORA, MLA_HEADS, V_HEAD), KV_LORA ** -0.5),
        'proj_a': nrm((L, MLA_HEADS * V_HEAD, D), (MLA_HEADS * V_HEAD) ** -0.5),
        'rwkv_mu': jax.random.uniform(next(ks), (L, RWKV_IN), jnp.float32),
        'rwkv_w0': nrm((L, RWKV_DIM), 1.0),
        'rwkv_w2': nrm((L, W_LORA, RWKV_DIM), 0.5 * W_LORA ** -0.5),
        'rwkv_a0': nrm((L, RWKV_DIM), 0.5),
        'rwkv_a2': nrm((L, A_LORA, RWKV_DIM), 0.5 * A_LORA ** -0.5),
        'rwkv_g2': nrm((L, G_LORA, RWKV_DIM), G_LORA ** -0.5),
        'rwkv_k_k': 0.85 + nrm((L, RWKV_DIM), 0.1),
        'rwkv_k_a': 1.0 + nrm((L, RWKV_DIM), 0.1),
        'rwkv_r_k': nrm((L, RWKV_HEADS, RWKV_HEAD), 0.1),
        'rwkv_ln_g': 1.0 + nrm((L, RWKV_DIM), 0.05),
        'rwkv_ln_b': nrm((L, RWKV_DIM), 0.02),
        'proj_b': nrm((L, RWKV_DIM, D), RWKV_DIM ** -0.5),
        'conv_dw': nrm((L, CONV_WIDTH, CONV_DIM), CONV_WIDTH ** -0.5),
        'conv_dw_b': nrm((L, CONV_DIM), 0.02),
        'conv_ln_g': 1.0 + nrm((L, CONV_DIM), 0.05),
        'conv_ln_b': nrm((L, CONV_DIM), 0.02),
        'proj_c': nrm((L, CONV_DIM, D), CONV_DIM ** -0.5),
        'w_out': nrm((L, D, D), D ** -0.5),
        'router_group_w': nrm((L, D, N_GROUPS), D ** -0.5),
        'router_group_b': nrm((L, N_GROUPS), 0.01),
        'router_expert_w': nrm((L, D, N_EXPERTS), D ** -0.5),
        'router_expert_b': nrm((L, N_EXPERTS), 0.01),
        'moe_w_gate': nrm((L, N_EXPERTS, D, D_EXPERT), D ** -0.5),
        'moe_w_up': nrm((L, N_EXPERTS, D, D_EXPERT), D ** -0.5),
        'moe_w_down': nrm((L, N_EXPERTS, D_EXPERT, D), D_EXPERT ** -0.5),
        'final_g': 1.0 + nrm((D,), 0.05),
    }

def reference(x_prompt, x_sample, c_prompt, c_sample, cache_kv_latent, cache_k_rope, state_rwkv_shift,
              state_rwkv_wkv, state_conv, ada_w, ada_b, norm1_g, norm2_g, w_in, q_norm_g, q_up, kv_norm_g,
              w_uk, w_uv, proj_a, rwkv_mu, rwkv_w0, rwkv_w2, rwkv_a0, rwkv_a2, rwkv_g2, rwkv_k_k, rwkv_k_a,
              rwkv_r_k, rwkv_ln_g, rwkv_ln_b, proj_b, conv_dw, conv_dw_b, conv_ln_g, conv_ln_b, proj_c, w_out,
              router_group_w, router_group_b, router_expert_w, router_expert_b, moe_w_gate, moe_w_up,
              moe_w_down, final_g):
    bp = x_prompt.shape[0]
    dt = x_prompt.dtype
    lat0 = jnp.zeros((bp, 0, KV_LORA), dt)
    rope0 = jnp.zeros((bp, 0, ROPE_DIM), dt)
    shift0 = jnp.zeros((bp, RWKV_IN), dt)
    wkv0 = jnp.zeros((bp, RWKV_HEADS, RWKV_HEAD, RWKV_HEAD), dt)
    conv0 = jnp.zeros((bp, CONV_WIDTH - 1, CONV_DIM), dt)
    hp, hs = x_prompt, x_sample
    new_p, new_s = [], []
    for l in range(DEPTH):
        lp = dict(ada_w=ada_w[l], ada_b=ada_b[l], norm1_g=norm1_g[l], norm2_g=norm2_g[l], w_in=w_in[l],
                  q_norm_g=q_norm_g[l], q_up=q_up[l], kv_norm_g=kv_norm_g[l], w_uk=w_uk[l], w_uv=w_uv[l],
                  proj_a=proj_a[l], rwkv_mu=rwkv_mu[l], rwkv_w0=rwkv_w0[l], rwkv_w2=rwkv_w2[l],
                  rwkv_a0=rwkv_a0[l], rwkv_a2=rwkv_a2[l], rwkv_g2=rwkv_g2[l], rwkv_k_k=rwkv_k_k[l],
                  rwkv_k_a=rwkv_k_a[l], rwkv_r_k=rwkv_r_k[l], rwkv_ln_g=rwkv_ln_g[l], rwkv_ln_b=rwkv_ln_b[l],
                  proj_b=proj_b[l], conv_dw=conv_dw[l], conv_dw_b=conv_dw_b[l], conv_ln_g=conv_ln_g[l],
                  conv_ln_b=conv_ln_b[l], proj_c=proj_c[l], w_out=w_out[l], router_group_w=router_group_w[l],
                  router_group_b=router_group_b[l], router_expert_w=router_expert_w[l],
                  router_expert_b=router_expert_b[l], moe_w_gate=moe_w_gate[l], moe_w_up=moe_w_up[l],
                  moe_w_down=moe_w_down[l])
        hp, st_p = trunk_layer(hp, c_prompt, lat0, rope0, shift0, wkv0, conv0, lp)
        hs, st_s = trunk_layer(hs, c_sample, cache_kv_latent[l], cache_k_rope[l], state_rwkv_shift[l],
                               state_rwkv_wkv[l], state_conv[l], lp)
        new_p.append(st_p)
        new_s.append(st_s)
    y_prompt = rmsnorm(hp, final_g)
    y_sample = rmsnorm(hs, final_g)
    stack = lambda states, i: jnp.stack([s[i] for s in states], axis=0)
    p_lat, p_rope, p_shift, p_wkv, p_conv = [stack(new_p, i) for i in range(5)]
    s_lat, s_rope, s_shift, s_wkv, s_conv = [stack(new_s, i) for i in range(5)]
    return (y_prompt, y_sample, p_lat, p_rope, p_shift, p_wkv, p_conv, s_lat, s_rope, s_shift, s_wkv, s_conv)


_drawn_inputs = setup_inputs


def setup_inputs(seed=0):
    import zlib

    import numpy as np

    out = dict(_drawn_inputs(seed))
    spreads = {}
    factors = {'cache_k_rope': 3.489,
     'state_rwkv_shift': 2.804,
     'q_norm_g': 8.0,
     'rwkv_ln_g': 6.422,
     'rwkv_ln_b': 8.0,
     'conv_dw_b': 7.991,
     'conv_ln_g': 3.758,
     'conv_ln_b': 8.0,
     'router_group_b': 24.62,
     'router_expert_b': 26.258,
     'norm2_g': 2.701}
    for name, (base, spread) in spreads.items():
        noise = np.random.default_rng([zlib.crc32(name.encode()), seed]).standard_normal(out[name].shape)
        drawn = base * np.exp(spread * noise) if base else spread * noise
        out[name] = __import__('jax').numpy.asarray(drawn.astype(out[name].dtype))
    for name, factor in factors.items():
        out[name] = (out[name] * factor).astype(out[name].dtype)
    return out
```

```python
from contextlib import ExitStack

import numpy as np

import concourse.bass as bass
from concourse import mybir

F32 = mybir.dt.float32
ALU = mybir.AluOpType
ACT = mybir.ActivationFunctionType
AX_X = mybir.AxisListType.X

P = 128
DM, DEPTH = 1024, 2
TP, TS = 512, 32
T = TP + TS
HALF = T // 2
DT = DM // P
TT = 5
PAST = 256
HEADS, NOPE, ROPE, VH = 8, 64, 32, 64
QL, KVL = 384, 256
QK = NOPE + ROPE
SCALE = float(QK) ** -0.5
RH = 4
CW, CD = 31, 256
NE, FE = 16, 256
CHUNK = 64
DECAY = float(np.exp(-0.5))
PADT = TT * P

U_ADA, U_CV, U_RW, U_MLA, U_UK, U_UV = 0, 48, 52, 60, 66, 67
U_MERGE = 68
U_OUT = U_MERGE + 4 * DT
UNITS = U_OUT + DT
RING = 6
UW = DT * P

PARAM = {}
_at = 0
for _name, _n in (("ada_b", 48), ("norm1_g", 8), ("norm2_g", 8), ("q_norm_g", 3), ("kv_norm_g", 2), ("mu", 8),
                  ("w0", 2), ("a0", 2), ("k_k", 2), ("k_a", 2), ("r_k", 2), ("ln_g", 2), ("ln_b", 2),
                  ("dw", 2 * CW), ("dw_b", 2), ("cln_g", 2), ("cln_b", 2)):
    PARAM[_name] = (_at, _n)
    _at += _n
NPARAM = _at

CONST = {}
_at = 0
for _name, _n in (("ident", P), ("ones", P), ("blk", P), ("gram", 4 * P), ("first", P), ("first_t", P),
                  ("levels", 5 * P), ("rot", ROPE), ("cos", T), ("sin", T), ("scan", T),
                  ("falling", 4)):
    CONST[_name] = (_at, _n)
    _at += _n
NCONST = _at
"""Offsets in the arena, in words of a partition."""
ARENA = 29568


class Chain:

    def __init__(self, eng, sem):
        self.eng, self.sem, self.n = eng, sem, 0

    def mark(self, ins):
        ins.then_inc(self.sem, 1)
        self.n += 1
        return self.n

    def link(self, ins):
        self.eng.wait_ge(self.sem, self.mark(ins))

    def wait(self, n):
        self.eng.wait_ge(self.sem, n)


def build(nc, d):
    ctx = ExitStack()
    with ctx:
        def sb(name, shape):
            return ctx.enter_context(nc.sbuf_tensor("s_" + name, shape, F32))

        sems = []

        def sem(name):
            s = ctx.enter_context(nc.semaphore(name))
            sems.append(s)
            return s

        PS = ctx.enter_context(nc.psum_tensor("PS", [P, 8, 512], F32))
        xT = sb("xT", [P, DT, T])
        hT = sb("hT", [P, DT, T])
        ring = sb("ring", [P, RING, UW])
        cst = sb("cst", [P, NCONST])
        prm = sb("prm", [P, NPARAM])
        fin_g = sb("fin_g", [P, DT])
        silu_c = sb("silu_c", [P, DT, 2])
        c_tmp = sb("c_tmp", [P, DT, 2])
        mod = sb("mod", [P, 6 * DT, 2])
        gain1 = sb("gain1", [P, DT, 2])
        gain2 = sb("gain2", [P, DT, 2])
        half_gt1 = sb("half_gt1", [P, DT, 2])
        half_gt2 = sb("half_gt2", [P, DT, 2])
        lora = sb("lora", [P, 3, RH * 64])
        router_w = sb("router_w", [P, DT, 20])
        router_b = sb("router_b", [P, 20])
        row = sb("row", [1, 2, 604])
        rs_in = sb("rs_in", [P, 20])
        rs = sb("rs", [P, 20])
        minus_half = sb("minus_half", [P, 20])
        rb = sb("rb", [P, TT, 2, P])
        half_w0a0 = sb("half_w0a0", [P, 4])
        keep = sb("keep", [P, 2, DT])
        arena = sb("arena", [P, ARENA])

        def a_(off, *shape):
            n = int(np.prod(shape))
            v = arena[:, off:off + n]
            if len(shape) == 1:
                return v
            names = "abcd"[:len(shape)]
            return v.rearrange(f"p ({' '.join(names)}) -> p {' '.join(names)}",
                               **{k: s for k, s in zip(names, shape)})

        def c_(name):
            o, n = CONST[name]
            return cst[:, o:o + n]

        def p_(name, i=None):
            o, n = PARAM[name]
            return prm[:, o:o + n] if i is None else prm[:, o + i:o + i + 1]

        ident, ones, blk = c_("ident"), c_("ones"), c_("blk")
        cos, sin = c_("cos"), c_("sin")

        cT = a_(0, 2, T)
        yT = a_(1088, 2, T)
        oT = a_(2176, 4, T)
        mod_row = a_(4352, 6 * DM)
        CBW = 2 * (CW - 1) + T
        CYW = CBW - (CW - 1)
        cb = a_(4352, 2, CBW)
        cy = a_(5568, 2, CYW)
        cth = a_(6720, 2, T)
        csq = a_(7808, 2, CYW)
        xs = a_(2176, 8, PADT)
        pr = a_(7296, 8, T + 2)
        logw = a_(11664, 2, T)
        aa = a_(12752, 2, T)
        kk = a_(13840, 2, T)
        cum = a_(14928, 2, T)
        rtmp = a_(16016, 2, T)
        gg = a_(17104, 2, T)
        bonus = a_(18192, 2, T)
        bf = a_(19280, 2, PADT)
        kf = a_(20560, 2, PADT)
        ar = a_(21840, 2, 4, PADT)
        et = a_(26960, TT, 2, 2 * P)
        zp = a_(2176, TT, 4, P)
        yv = a_(2176 + 6 * PADT, TT, RH * 64)
        vtok = a_(7296, 2 * P)
        btm = a_(7552, 2, 2 * P)
        ktm = a_(8064, 2, 2 * P)
        wr = a_(8576, 4, P)
        gb = a_(9088, 2, 4, P)
        gk = a_(10112, 2, 4, P)
        xx = a_(11136, 4, P)
        xt = a_(11648, 4, P)
        tm = a_(12160, 4, P)
        mo = a_(12672, 4, P)
        wn = a_(13184, 2, 4, 64)
        st = a_(13696, 11, 2, P)
        ytok = a_(7296, TT, RH, 64)
        ysq = a_(8576, TT, RH, 64)
        pexp, pneg, pm = a_(7296, 2, T), a_(8384, 2, T), a_(9472, 2, T)
        pmT = a_(4352, 5, T)
        latT = a_(7072, 2, TP + PAST + TS)
        msq = a_(8672, 5, T)
        vv = a_(8672, 7, HEADS * VH)
        krt, krr = a_(12256, T), a_(12800, T)
        krc = a_(13344, PAST)
        qup = a_(13888, 3, HEADS * QK)
        QT = a_(16192, HEADS, T)
        KT = a_(20544, HEADS, TP)
        KTs = a_(24640, HEADS, PAST + TS)
        sin_q = [a_(4352, 4, T), a_(13888, 4, T)]
        prob = [a_(26944, 4, TP), a_(4352, 4, TP)]
        probT = [a_(13888, 4, 4, P), a_(6400, 4, 4, P)]
        diag = [a_(12256 + 512 * i, 4, P) for i in range(2)]
        mx = sb("mx", [P, 2, 4, 4])
        mg = a_(4352, DT, T)
        th = [a_(8704 + 1632 * i, 3, T) for i in range(2)]
        mtmp = [a_(11968 + 544 * i, T) for i in range(2)]
        gu_w = [a_(13056 + 6144 * i, DT, 2 * FE) for i in range(2)]
        dn_w = [a_(13056 + 6144 * i + 4096, 2, DM) for i in range(2)]
        eact = a_(25344, 3, 2, T)
        eth = [a_(28608 + HALF * i, HALF) for i in range(3)]
        yacc = a_(8704, DT, T)
        lg = a_(0, TT, 20)
        ra = a_(100, 4, TT, 4)
        rm = a_(180, 8, TT)
        cmb = a_(220, TT, 4, 4)
        grp = a_(300, TT, 4, 4)
        cmbT = a_(400, T)
        pend = sb("pend", [P, TT, 2, 2])
        shift_in = sb("shift_in", [P, DT])

        s_const = sem("const_loaded")
        s_prm = sem("params_loaded")
        s_lora = sem("lora_loaded")
        s_wkv = sem("wkv_loaded")
        ring_full = [sem(f"ring_full{i}") for i in range(RING)]
        unit_done = sem("unit_done")
        s_c = sem("silu_c_ready")
        dch, pch = sem("dve_chain"), sem("pool_chain")
        ada_row = sem("ada_row")
        ada_tp = sem("ada_transposed")
        mod_ready = sem("mod_ready")
        nm = {k: {s: sem(f"norm_{k}_{s}") for s in ("sq", "row", "srow", "col", "ms", "rs", "rb", "bc", "g", "out")[lo:hi]}
              for k, lo, hi in (("n1", 0, 10), ("cv", 0, 8), ("kk", 4, 8))}
        cv_th, cv_glu, cv_init, cv_state = sem("cv_th"), sem("cv_glu"), sem("cv_init"), sem("cv_state")
        cv_y, cv_mu, cv_cent, cv_zh, cv_t2, cv_out = (sem(f"cv_{s}") for s in ("y", "mu", "cent", "zh", "t2", "out"))
        rw_pr, rw_init, rw_shift, rw_xs, rw_act, rw_lora, rw_wag, rw_fin = (
            sem(f"rw_{s}") for s in ("pr", "init", "shift", "xs", "act", "lora", "wag", "fin"))

        def norm_pe_tail(pe, s, r=0):
            pe.wait_ge(s["rb"], r + 1)
            for i in range(4):
                nc.tensor.transpose(PS[:, 3, i * P:(i + 1) * P], rb[:, i, 0, :], ident)
            nc.tensor.transpose(PS[:, 4, 0:TS], rb[0:TS, 4, 0, :], ident[0:TS, 0:TS]).then_inc(s["bc"], 1)

        def norm_cols_pe(pe, s, sample_at, r=0):
            pe.wait_ge(s["srow"], 2 * r + 2)
            for i in range(4):
                nc.tensor.matmul(PS[:, 2, i:i + 1], row[0:1, 0, i * P:(i + 1) * P], ones[0:1, 0:1],
                                 start=True, stop=True)
            nc.tensor.matmul(PS[0:TS, 2, 4:5], row[0:1, 0, sample_at:sample_at + TS], ones[0:1, 0:1],
                             start=True, stop=True).then_inc(s["col"], 1)

        def norm_cols_dve(dve, s, n, eps, r=0):
            dve.wait_ge(s["col"], r + 1)
            nc.vector.tensor_scalar(rs_in[:, 0:4], PS[:, 2, 0:4], 1.0 / n, eps, ALU.mult, ALU.add).then_inc(s["ms"], 1)
            nc.vector.tensor_scalar(rs_in[0:TS, 4:5], PS[0:TS, 2, 4:5], 1.0 / n, eps, ALU.mult, ALU.add)\
                .then_inc(s["ms"], 1)
            dve.wait_ge(s["rs"], r + 1)
            nc.vector.tensor_copy(rb[:, :, 0, :], rs[:, 0:TT].unsqueeze(2).to_broadcast([P, TT, P]))\
                .then_inc(s["rb"], 1)

        def norm_pow(pool, s, n=TT, r=0):
            pool.wait_ge(s["ms"], 2 * r + 2)
            nc.gpsimd.tensor_tensor(rs[:, 0:n], rs_in[:, 0:n], minus_half[:, 0:n], ALU.pow).then_inc(s["rs"], 1)

        def norm_x_act(act, s):
            for k in range(DT):
                nc.scalar.activation(hT[:, k, :], xT[:, k, :], ACT.Square).then_inc(s["sq"], 1)

        def norm_x_pe(pe, s, r=0):
            for k in range(DT):
                pe.wait_ge(s["sq"], DT * r + k + 1)
                for h in range(2):
                    ins = nc.tensor.matmul(PS[0:1, h, 0:HALF], ones[:, 0:1], hT[:, k, h * HALF:(h + 1) * HALF],
                                           start=(k == 0), stop=(k == DT - 1))
            ins.then_inc(s["row"], 1)
            norm_cols_pe(pe, s, TP, r)
            norm_pe_tail(pe, s, r)

        def norm_x_dve(dve, s, gain, r=0):
            dve.wait_ge(s["row"], r + 1)
            for h in range(2):
                nc.vector.tensor_copy(row[0:1, 0, h * HALF:(h + 1) * HALF], PS[0:1, h, 0:HALF]).then_inc(s["srow"], 1)
            norm_cols_dve(dve, s, DM, 1e-6, r)
            dve.wait_ge(s["bc"], r + 1)
            for k in range(DT):
                nc.vector.scalar_tensor_tensor(hT[:, k, 0:TP], xT[:, k, 0:TP], gain(k, 0), PS[:, 3, :],
                                               ALU.mult, ALU.mult).then_inc(s["g"], 1)
                nc.vector.scalar_tensor_tensor(hT[:, k, TP:T], xT[:, k, TP:T], gain(k, 1), PS[:, 4, 0:TS],
                                               ALU.mult, ALU.mult).then_inc(s["g"], 1)

        def norm_shift_act(act, s, chunk, r=0):
            for k in range(DT):
                act.wait_ge(s["g"], 2 * DT * r + 2 * k + 2)
                nc.scalar.activation(hT[:, k, 0:TP], hT[:, k, 0:TP], ACT.Identity,
                                     bias=mod[:, chunk * DT + k, 0:1]).then_inc(s["out"], 1)
                nc.scalar.activation(hT[:, k, TP:T], hT[:, k, TP:T], ACT.Identity,
                                     bias=mod[:, chunk * DT + k, 1:2]).then_inc(s["out"], 1)

        def unit_wait(pe, n):
            pe.wait_ge(ring_full[n % RING], 16 * (n // RING + 1))
            return ring[:, n % RING, :].rearrange("p (k m) -> p k m", k=DT)

        def unit_mm(pe, n, pair, rows=P):
            w = unit_wait(pe, n)
            if rows < P:
                w = ring[:, n % RING, 0:DT * rows].rearrange("p (k m) -> p k m", k=DT)
            for k in range(DT):
                for h in range(2):
                    ins = nc.tensor.matmul(PS[0:rows, 2 * pair + h, 0:HALF], w[:, k, :],
                                           hT[:, k, h * HALF:(h + 1) * HALF], start=(k == 0), stop=(k == DT - 1))
            ins.then_inc(unit_done, 1)

        lay = [None]
        L_ = lambda name: lay[0](name)

        names = ("act", "gl", "sq", "n2", "cumd", "exp", "der", "bon", "bon_mm", "tp", "tpe", "gram", "gm", "x0",
                 "mo", "t", "te", "x", "xe", "nv", "nve", "wu", "wue", "lin", "line", "st_init", "st_mm", "st",
                 "y_mm", "y", "ytp", "out", "clr", "ms2", "rs2")
        q = {n: sem(f"q_{n}") for n in names}
        cv_done = sem("cv_done")

        def by4(v):
            return v.unsqueeze(1).to_broadcast([P, 4, P])

        def bank4(b):
            return PS[:, b, :].rearrange("p (h n) -> p h n", h=4)

        def rwkv_pe(pe):
            pe.wait_ge(cv_done, 1)
            for i in range(8):
                if i >= 4:
                    pe.wait_ge(rw_pr, 3 * (i - 3))
                unit_mm(pe, U_RW + i, i % 4)
            pe.wait_ge(rw_pr, 24)
            pe.wait_ge(s_lora, 64)
            pe.wait_ge(q["act"], 1)
            for j in range(4):
                for h in range(2):
                    ins = nc.tensor.matmul(PS[:, 2 * j + h, 0:HALF], lora[:, j // 2, (j % 2) * P:(j % 2 + 1) * P],
                                           xs[:, 6, h * HALF:(h + 1) * HALF], start=True, stop=True)
                ins.then_inc(rw_lora, 1)
            pe.wait_ge(q["gl"], 1)
            pe.wait_ge(rw_wag, 4)
            for j in range(2):
                for h in range(2):
                    ins = nc.tensor.matmul(PS[:, 2 * j + h, 0:HALF], lora[:, 2, j * P:(j + 1) * P],
                                           xs[:, 7, h * HALF:(h + 1) * HALF], start=True, stop=True)
                ins.then_inc(rw_lora, 1)
            pe.wait_ge(q["sq"], 1)
            pe.wait_ge(rw_wag, 12)
            for t in range(2):
                for i in range(TT):
                    m = P if i < 4 else TS
                    ins = nc.tensor.matmul(PS[0:m, 2, 4 * i + 2 * t:4 * i + 2 * t + 2], rtmp[:, t, i * P:i * P + m],
                                           blk[:, 0:P:64], start=True, stop=True)
            ins.then_inc(q["n2"], 1)
            turn_rb(pe, nm["kk"], lambda i, t: rb[:, i, t, :])
            pe.wait_ge(q["bon"], 2)
            for t in range(2):
                for h in range(2):
                    ins = nc.tensor.matmul(PS[:, (0, 1, 2, 7)[2 * t + h], 0:HALF], blk,
                                           bonus[:, t, h * HALF:(h + 1) * HALF], start=True, stop=True)
            ins.then_inc(q["bon_mm"], 1)
            pe.wait_ge(q["der"], 8)
            for p in range(TT):
                co = slice(p * P, (p + 1) * P)
                if p:
                    pe.wait_ge(q["wue"], p)
                    pe.wait_ge(q["line"], 5 * p)
                for t in range(2):
                    nc.tensor.transpose(PS[:, 0, t * P:(t + 1) * P], xs[:, 4 + t, co], ident)
                    nc.tensor.transpose(PS[:, 0, (2 + t) * P:(3 + t) * P], bf[:, t, co], ident)
                    nc.tensor.transpose(PS[:, 1, t * P:(t + 1) * P], kf[:, t, co], ident)
                    for e in range(2):
                        ins = nc.tensor.matmul(PS[:, 1, (2 + t) * P:(3 + t) * P], ar[:, t, e, co], ident,
                                               start=(e == 0), stop=(e == 1))
                ins.then_inc(q["tp"], 1)
                for o, src in ((2, bf), (4, kf)):
                    for t in range(2):
                        nc.tensor.matmul(PS[:, o + t, :].rearrange("p (k n) -> p k n", k=4), src[:, t, co],
                                         ar[:, t, :, co], start=True, stop=True).then_inc(q["gram"], 1)
                for h in range(4):
                    ins = nc.tensor.matmul(PS[:, 6, h * P:(h + 1) * P], ar[:, h // 2, h % 2, co], bf[:, h // 2, co],
                                           start=True, stop=True)
                ins.then_inc(q["gram"], 1)
                for lv in range(5):
                    n = 5 * p + lv
                    pe.wait_ge(q["mo"], n + 1)
                    pe.wait_ge(q["x0"], 2 * (p + 1))
                    if lv:
                        pe.wait_ge(q["xe"], 9 * p + 2 * lv)
                    for h in range(4):
                        ins = nc.tensor.matmul(PS[:, 7, h * P:(h + 1) * P], mo[:, h, :], xx[:, h, :],
                                               start=True, stop=True)
                    ins.then_inc(q["t"], 1)
                    pe.wait_ge(q["te"], n + 1)
                    for h in range(4):
                        ins = nc.tensor.matmul(PS[:, 5, h * P:(h + 1) * P], tm[:, h, :], xt[:, h, :],
                                               start=True, stop=True)
                    ins.then_inc(q["x"], 1)
                    if lv < 4:
                        for h in range(4):
                            ins = nc.tensor.matmul(PS[:, 6, h * P:(h + 1) * P], xt[:, h, :], tm[:, h, :],
                                                   start=True, stop=True)
                        ins.then_inc(q["x"], 1)
                pe.wait_ge(q["tpe"], 6 * (p + 1))
                for h in range(4):
                    ins = nc.tensor.matmul(PS[:, 0, h * 64:(h + 1) * 64], gk[:, 0, h, :], vtok[:, h * 64:(h + 1) * 64],
                                           start=True, stop=True)
                ins.then_inc(q["nv"], 1)
                pe.wait_ge(q["nve"], p + 1)
                pe.wait_ge(q["xe"], 9 * (p + 1))
                for h in range(4):
                    ins = nc.tensor.matmul(PS[:, 1, h * P:(h + 1) * P], xt[:, h, :], wr[:, h, :],
                                           start=True, stop=True)
                ins.then_inc(q["wu"], 1)
                pe.wait_ge(q["wue"], p + 1)
                for t in range(2):
                    ins = nc.tensor.matmul(PS[:, 2, t * 256:(t + 1) * 256].rearrange("p (a n) -> p a n", a=2),
                                           wn[:, 0, 2 * t:2 * t + 2, :].rearrange("p h n -> p (h n)"), btm[:, :, t * P:(t + 1) * P],
                                           start=True, stop=True)
                ins.then_inc(q["lin"], 1)
                for t in range(2):
                    for e in range(2):
                        o = PS[:, 3, (2 * t + e) * P:(2 * t + e + 1) * P]
                        nc.tensor.matmul(o, btm[:, e, t * P:(t + 1) * P], wn[:, 1, 2 * t:2 * t + 2, :].rearrange("p h n -> p (h n)"),
                                         start=True, stop=False)
                        ins = nc.tensor.matmul(o, ktm[:, e, t * P:(t + 1) * P], vtok[:, t * P:(t + 1) * P],
                                               start=False, stop=True)
                ins.then_inc(q["lin"], 1)
                for h in range(4):
                    e = h % 2
                    ins = nc.tensor.matmul(PS[64 * e:64 * e + 64, 4, (h // 2) * P:(h // 2 + 1) * P], wn[:, 0, h, :],
                                           gb[:, 1, h, :], start=True, stop=True)
                ins.then_inc(q["lin"], 1)
                for h in range(4):
                    nc.tensor.matmul(PS[:, 5, h * 64:(h + 1) * 64], gb[:, 1, h, :], wn[:, 1, h, :],
                                     start=True, stop=False)
                    ins = nc.tensor.matmul(PS[:, 5, h * 64:(h + 1) * 64], gk[:, 1, h, :],
                                           vtok[:, h * 64:(h + 1) * 64], start=False, stop=True)
                ins.then_inc(q["lin"], 1)
            pe.wait_ge(q["st_init"], 1)
            pe.wait_ge(s_wkv, 64)
            pe.wait_ge(q["line"], 5 * TT)
            for c in range(9):
                if c and c < 8:
                    pe.wait_ge(q["st"], 2 * c)
                for t in range(2):
                    ins = nc.tensor.matmul(PS[:, 6 + c % 2, t * P:(t + 1) * P], et[:, c // 2, t, (c % 2) * P:(c % 2 + 1) * P],
                                           st[:, c if c < 8 else 9, t, :], start=True, stop=True)
                ins.then_inc(q["st_mm"], 1)
            pe.wait_ge(q["st"], 14)
            for c in range(9):
                p, e = c // 2, c % 2
                for t in range(2):
                    for r in range(2):
                        ins = nc.tensor.matmul(PS[64 * e:64 * e + 64, p, t * P:(t + 1) * P],
                                               ar[:, t, 2 + r, c * 64:(c + 1) * 64], st[:, c if c < 8 else 9, t, :],
                                               start=(r == 0), stop=(r == 1))
                ins.then_inc(q["y_mm"], 1)
            turn_rb(pe, None, lambda i, t: ytok[:, i, 2 * t:2 * t + 2, :].rearrange("p h n -> p (h n)"), (q["y"], 20), q["ytp"])

        def turn_rb(pe, s, src, wait=None, done=None):
            if s is not None:
                wait, done = (s["rb"], 1), s["bc"]
            pe.wait_ge(*wait)
            for t in range(2):
                for i in range(4):
                    nc.tensor.transpose(PS[:, 3 + 2 * t, i * P:(i + 1) * P], src(i, t), ident)
                ins = nc.tensor.transpose(PS[:, 4, TS * t:TS * (t + 1)], src(4, t)[0:TS], ident[0:TS, 0:TS])
            ins.then_inc(done, 1)

        def rwkv_act(act):
            act.wait_ge(cv_done, 1)
            for i in range(8):
                act.wait_ge(unit_done, U_RW + i + 1)
                b = 2 * (i % 4)
                nc.scalar.copy(pr[:, i, 1:1 + HALF], PS[:, b, 0:HALF]).then_inc(rw_pr, 1)
                nc.scalar.copy(pr[:, i, 1 + HALF:1 + TP], PS[:, b + 1, 0:TP - HALF]).then_inc(rw_pr, 1)
                nc.scalar.copy(pr[:, i, 2 + TP:2 + T], PS[:, b + 1, TP - HALF:HALF]).then_inc(rw_pr, 1)
            act.wait_ge(rw_shift, 2)
            act.dma_start(L_("out_shift").rearrange("l p g n -> p (l g) n"), keep[:, :, :]).then_inc(rw_fin, 16)
            act.wait_ge(rw_xs, 14)
            nc.scalar.activation(xs[0:64, 6, 0:T], xs[0:64, 6, 0:T], ACT.Tanh).then_inc(q["act"], 1)
            act.wait_ge(rw_xs, 16)
            nc.scalar.activation(xs[:, 7, 0:T], xs[:, 7, 0:T], ACT.Tanh, scale=0.5).then_inc(q["act"], 1)
            act.wait_ge(rw_init, 7)
            for j in range(4):
                act.wait_ge(rw_lora, j + 1)
                dst = (logw, aa)[j // 2]
                for h in range(2):
                    nc.scalar.activation(dst[:, j % 2, h * HALF:(h + 1) * HALF], PS[:, 2 * j + h, 0:HALF], ACT.Tanh,
                                         bias=half_w0a0[:, j:j + 1], scale=0.5).then_inc(rw_wag, 1)
            for j in range(2):
                act.wait_ge(rw_lora, 5 + j)
                for h in range(2):
                    nc.scalar.copy(gg[:, j, h * HALF:(h + 1) * HALF], PS[:, 2 * j + h, 0:HALF]).then_inc(rw_wag, 1)
            act.wait_ge(q["cumd"], 2)
            nc.scalar.activation(pexp[:, :, :], cum[:, :, :], ACT.Exp).then_inc(q["exp"], 1)
            nc.scalar.activation(pneg[:, :, :], cum[:, :, :], ACT.Exp, scale=-1.0).then_inc(q["exp"], 1)
            act.wait_ge(q["cumd"], 3)
            nc.scalar.activation(pm[:, :, :], logw[:, :, :], ACT.Exp).then_inc(q["exp"], 1)
            act.wait_ge(q["clr"], 1)
            for h in range(4):
                e = h % 2
                act.dma_start(st[64 * e:64 * e + 64, 9, h // 2, 64 * e:64 * e + 64],
                              L_("wkv")[:, h].rearrange("l j i -> (l j) i")).then_inc(s_wkv, 16)
            for p in range(TT):
                act.wait_ge(q["tp"], p + 1)
                nc.scalar.copy(vtok[:, :], PS[:, 0, 0:256]).then_inc(q["tpe"], 1)
                for dst, b, o in ((btm, 0, 256), (ktm, 1, 0)):
                    for e in range(2):
                        nc.scalar.copy(dst[64 * e:64 * e + 64, e, :], PS[64 * e:64 * e + 64, b, o:o + 256])\
                            .then_inc(q["tpe"], 1)
                nc.scalar.copy(wr[:, :, 0:64], PS[:, 1, 256:512].rearrange("p (h n) -> p h n", h=4))\
                    .then_inc(q["tpe"], 1)
                for lv in range(5):
                    act.wait_ge(q["t"], 5 * p + lv + 1)
                    nc.scalar.copy(tm[:, :, :], bank4(7)).then_inc(q["te"], 1)
                act.wait_ge(q["nv"], p + 1)
                nc.scalar.copy(wr[:, :, 64:128], PS[:, 0, 0:256].rearrange("p (h n) -> p h n", h=4))\
                    .then_inc(q["nve"], 1)
                act.wait_ge(q["wu"], p + 1)
                nc.scalar.activation(wn[:, :, :, :].rearrange("p a h n -> p h a n"),
                                     PS[:, 1, :].rearrange("p (h a n) -> p h a n", h=4, a=2), ACT.Copy, scale=-1.0).then_inc(q["wue"], 1)
                act.wait_ge(q["lin"], 4 * p + 4)
                nc.scalar.copy(yv[:, p, :], PS[:, 5, 0:256]).then_inc(q["line"], 1)
            act.wait_ge(q["st"], 18)
            for g, c in ((0, 8), (1, 10)):
                for h in range(4):
                    e = h % 2
                    act.dma_start(L_("out_wkv")[:, g, h].rearrange("l j i -> (l j) i"),
                                  st[64 * e:64 * e + 64, c, h // 2, 64 * e:64 * e + 64]).then_inc(rw_fin, 16)
            act.wait_ge(rw_fin, 16 * 9)

        def rwkv_pool(pool):
            pool.wait_ge(cv_done, 1)
            pool.wait_ge(s_lora, 64)
            nc.gpsimd.memset(pr[:, :, 0:1], 0.0).then_inc(rw_init, 1)
            nc.gpsimd.tensor_copy(pr[:, :, TP + 1:TP + 2], shift_in[:, :].unsqueeze(2)).then_inc(rw_init, 1)
            nc.gpsimd.memset(xs[:, :, T:PADT], 0.0).then_inc(rw_init, 1)
            nc.gpsimd.memset(bf[:, :, T:PADT], 0.0).then_inc(rw_init, 1)
            nc.gpsimd.memset(kf[:, :, T:PADT], 0.0).then_inc(rw_init, 1)
            nc.gpsimd.memset(ar[:, :, :, :], 0.0).then_inc(rw_init, 1)
            nc.gpsimd.tensor_scalar(half_w0a0[:, :], prm[:, PARAM["w0"][0]:PARAM["w0"][0] + 4], 0.5, None, ALU.mult)\
                .then_inc(rw_init, 1)
            pool.wait_ge(rw_pr, 24)
            nc.gpsimd.tensor_copy(keep[:, 0, :], pr[:, :, TP:TP + 1].squeeze(2)).then_inc(rw_shift, 1)
            nc.gpsimd.tensor_copy(keep[:, 1, :], pr[:, :, T + 1:T + 2].squeeze(2)).then_inc(rw_shift, 1)
            norm_pow(pool, nm["kk"], 4 * TT)
            pool.wait_ge(q["der"], 8)
            nc.gpsimd.memset(btm[:, :, :], 0.0).then_inc(pch, 1)
            nc.gpsimd.memset(ktm[:, :, :], 0.0).then_inc(pch, 1)
            nc.gpsimd.memset(st[:, 0, :, :], 0.0).then_inc(pch, 1)
            pool.wait_ge(pch, 3)
            nc.gpsimd.memset(st[:, 9, :, :], 0.0).then_inc(q["clr"], 1)
            pool.wait_ge(q["line"], 5 * TT)
            nc.gpsimd.memset(ytok[64:128, 4, :, :], 0.0).then_inc(q["st_init"], 1)
            norm_pow(pool, {"ms": q["ms2"], "rs": q["rs2"]}, 4 * TT)

        def rwkv_dve(dve, ch):
            dve.wait_ge(rw_init, 3)
            for i in range(8):
                dve.wait_ge(rw_pr, 3 * (i + 1))
                tmp = a_((11664, 12752)[i % 2], T + 1)
                if i >= 2:
                    dve.wait_ge(rw_xs, 2 * (i - 1))
                ch.link(nc.vector.tensor_tensor(tmp, pr[:, i, 0:T + 1], pr[:, i, 1:T + 2], ALU.subtract))
                nc.vector.scalar_tensor_tensor(xs[:, i, 0:TP], tmp[:, 0:TP], p_("mu", i), pr[:, i, 1:TP + 1],
                                               ALU.mult, ALU.add).then_inc(rw_xs, 1)
                nc.vector.scalar_tensor_tensor(xs[:, i, TP:T], tmp[:, TP + 1:T + 1], p_("mu", i),
                                               pr[:, i, TP + 2:T + 2], ALU.mult, ALU.add).then_inc(rw_xs, 1)
            dve.wait_ge(rw_xs, 16)
            for t in range(2):
                ch.mark(nc.vector.tensor_scalar(kk[:, t, :], xs[:, 2 + t, 0:T], p_("k_k", t), None, ALU.mult))
            dve.wait_ge(q["act"], 2)
            nc.vector.tensor_scalar(xs[:, 7, 0:T], xs[:, 7, 0:T], 0.5, 0.5, ALU.mult, ALU.add).then_inc(q["gl"], 1)
            ch.wait(ch.n)
            nc.vector.tensor_tensor(rtmp[:, :, :], kk[:, :, :], kk[:, :, :], ALU.mult).then_inc(q["sq"], 1)
            dve.wait_ge(rw_wag, 4)
            ch.link(nc.vector.tensor_scalar(logw[:, :, :], logw[:, :, :], -0.5 * DECAY, -0.5 * DECAY,
                                            ALU.mult, ALU.add))
            for t in range(2):
                nc.vector.tensor_tensor_scan(cum[:, t, :], c_("scan"), logw[:, t, :], 0.0, ALU.mult, ALU.add)\
                    .then_inc(q["cumd"], 1)
            dve.wait_ge(q["cumd"], 2)
            nc.vector.tensor_tensor(logw[:, :, :], cum[:, :, :], logw[:, :, :], ALU.subtract).then_inc(q["cumd"], 1)
            dve.wait_ge(rw_wag, 8)
            ch.link(nc.vector.tensor_scalar(aa[:, :, :], aa[:, :, :], 0.5, 0.5, ALU.mult, ALU.add))
            s = nm["kk"]
            dve.wait_ge(q["n2"], 1)
            nc.vector.tensor_scalar(rs_in[:, 0:16], PS[:, 2, 0:16], 1e-12, None, ALU.add).then_inc(s["ms"], 1)
            nc.vector.tensor_scalar(rs_in[0:TS, 16:20], PS[0:TS, 2, 16:20], 1e-12, None, ALU.add)\
                .then_inc(s["ms"], 1)
            for t in range(2):
                ch.link(nc.vector.tensor_scalar(rtmp[:, t, :], aa[:, t, :], 1.0, p_("k_a", t),
                                                ALU.subtract, ALU.mult))
                ch.link(nc.vector.scalar_tensor_tensor(rtmp[:, t, :], rtmp[:, t, :], 1.0, xs[:, 2 + t, 0:T],
                                                       ALU.add, ALU.mult))
                nc.vector.scalar_tensor_tensor(bonus[:, t, :], xs[:, t, 0:T], p_("r_k", t), rtmp[:, t, :],
                                               ALU.mult, ALU.mult).then_inc(q["bon"], 1)
            dve.wait_ge(s["rs"], 1)
            nc.vector.tensor_copy(rb[:, :, :, :].rearrange("p i t (h n) -> p (i t h) n", h=2),
                                  rs[:, 0:20].unsqueeze(2).to_broadcast([P, 20, 64])).then_inc(s["rb"], 1)
            dve.wait_ge(q["exp"], 3)
            dve.wait_ge(rw_init, 7)
            dve.wait_ge(q["bon"], 2)
            nc.vector.tensor_tensor(kf[:, :, 0:T], rtmp[:, :, :], pneg[:, :, :], ALU.mult).then_inc(q["der"], 1)
            for e in range(2):
                r = slice(64 * e, 64 * e + 64)
                nc.vector.tensor_tensor(ar[r, :, 2 + e, 0:T], xs[r, 0:2, 0:T], pexp[r, :, :], ALU.mult)\
                    .then_inc(q["der"], 1)
            for t in range(2):
                ch.mark(nc.vector.tensor_copy(pend[:, 0:4, t, :], pexp[:, t, 63:TP:64]
                                              .rearrange("p (a b) -> p a b", b=2)))
            ch.mark(nc.vector.tensor_copy(pend[:, 4, :, 0:1], pexp[:, :, T - 1:T]))
            ch.mark(nc.vector.tensor_copy(pend[:, 4, :, 1:2], pexp[:, :, T - 1:T]))
            dve.wait_ge(s["bc"], 1)
            for t in range(2):
                ch.mark(nc.vector.tensor_tensor(kk[:, t, 0:TP], kk[:, t, 0:TP], PS[:, 3 + 2 * t, :], ALU.mult))
                ch.link(nc.vector.tensor_tensor(kk[:, t, TP:T], kk[:, t, TP:T], PS[:, 4, TS * t:TS * t + TS],
                                                ALU.mult))
            ch.link(nc.vector.tensor_tensor(aa[:, :, :], aa[:, :, :], kk[:, :, :], ALU.mult))
            nc.vector.tensor_tensor(bf[:, :, 0:T], aa[:, :, :], pneg[:, :, :], ALU.mult).then_inc(q["der"], 1)
            for e in range(2):
                r = slice(64 * e, 64 * e + 64)
                nc.vector.tensor_tensor(ar[r, :, e, 0:T], kk[r, :, :], pm[r, :, :], ALU.mult).then_inc(q["der"], 1)
            dve.wait_ge(q["bon_mm"], 1)
            for t in range(2):
                for h in range(2):
                    ins = nc.vector.tensor_tensor(bonus[:, t, h * HALF:(h + 1) * HALF],
                                                  PS[:, (0, 1, 2, 7)[2 * t + h], 0:HALF],
                                                  xs[:, 4 + t, h * HALF:(h + 1) * HALF], ALU.mult)
                    ins.then_inc(q["der"], 1) if h else ch.mark(ins)
            ch.wait(ch.n)
            dve.wait_ge(q["der"], 8)
            for p in range(TT):
                co = slice(p * P, (p + 1) * P)
                for i in range(4):
                    dve.wait_ge(q["gram"], 5 * p + i + 1)
                    dst, t = (gb, gk)[i // 2], i % 2
                    nc.vector.tensor_tensor(dst[:, :, 2 * t:2 * t + 2, :].rearrange("p k h n -> p k (h n)"),
                                            PS[:, 2 + i, :].rearrange("p (k n) -> p k n", k=2),
                                            c_("gram").rearrange("p (k n) -> p k n", k=2), ALU.mult)\
                        .then_inc(q["gm"], 1)
                dve.wait_ge(q["gram"], 5 * p + 5)
                dve.wait_ge(q["gm"], 4 * p + 4)
                ch.mark(nc.vector.scalar_tensor_tensor(xx[:, :, :], bank4(6), -1.0, by4(c_("first")),
                                                       ALU.mult, ALU.mult))
                ch.link(nc.vector.scalar_tensor_tensor(xt[:, :, :], gb[:, 0, :, :], -1.0, by4(c_("first_t")),
                                                       ALU.mult, ALU.mult))
                nc.vector.tensor_tensor(xx[:, :, :], xx[:, :, :], by4(ident), ALU.add).then_inc(q["x0"], 1)
                nc.vector.tensor_tensor(xt[:, :, :], xt[:, :, :], by4(ident), ALU.add).then_inc(q["x0"], 1)
                for lv in range(5):
                    n = 5 * p + lv
                    if n:
                        dve.wait_ge(q["t"], n)
                    nc.vector.tensor_tensor(mo[:, :, :], gb[:, 0, :, :], by4(c_("levels")[:, lv * P:(lv + 1) * P]),
                                            ALU.mult).then_inc(q["mo"], 1)
                    dve.wait_ge(q["x0"], 2 * p + 2)
                    nx = 9 * p + 2 * lv + (2 if lv < 4 else 1)
                    dve.wait_ge(q["x"], nx)
                    if lv:
                        dve.wait_ge(q["xe"], 9 * p + 2 * lv)
                    nc.vector.tensor_tensor(xt[:, :, :], xt[:, :, :], bank4(5), ALU.add).then_inc(q["xe"], 1)
                    if lv < 4:
                        nc.vector.tensor_tensor(xx[:, :, :], xx[:, :, :], bank4(6), ALU.add).then_inc(q["xe"], 1)
                dve.wait_ge(q["lin"], 4 * p + 3)
                four = lambda v: v.rearrange("p (a n) -> p a n", n=P)
                e4 = et[:, p, :, :].rearrange("p t n -> p (t n)").rearrange("p (a n) -> p a n", n=P)
                ch.mark(nc.vector.tensor_tensor(e4, bank4(2), by4(blk), ALU.mult))
                ch.link(nc.vector.tensor_tensor(zp[:, p, :, :], bank4(3), by4(blk), ALU.mult))
                nc.vector.tensor_tensor(e4, e4, by4(ident), ALU.add).then_inc(q["line"], 1)
                nc.vector.tensor_tensor(zp[:, p, :, :], zp[:, p, :, :],
                                        pend[:, p, :, :].rearrange("p a b -> p (a b)").unsqueeze(2)
                                        .to_broadcast([P, 4, P]), ALU.mult).then_inc(q["line"], 1)
                for e in range(2):
                    r = slice(64 * e, 64 * e + 64)
                    ins = nc.vector.tensor_tensor(ar[r, :, 2 + e, co], ar[r, :, 2 + e, co],
                                                  PS[r, 4, 0:256].rearrange("p (t n) -> p t n", t=2), ALU.add)
                    ins.then_inc(q["line"], 1)
            dve.wait_ge(q["line"], 5 * TT)
            for c in range(9):
                dve.wait_ge(q["st_mm"], c + 1)
                p, e = c // 2, c % 2
                for t in range(2):
                    nc.vector.scalar_tensor_tensor(st[:, c + 1 if c < 8 else 10, t, :], PS[:, 6 + c % 2, t * P:(t + 1) * P],
                                                   pend[:, p, t, e:e + 1], zp[:, p, 2 * t + e, :],
                                                   ALU.mult, ALU.add).then_inc(q["st"], 1)
            dve.wait_ge(q["st_init"], 1)
            for p in range(TT):
                m = P if p < 4 else 64
                dve.wait_ge(q["y_mm"], min(2 * p + 2, 9))
                ch.mark(nc.vector.tensor_tensor(ytok[0:m, p, :, :].rearrange("p h n -> p (h n)"), PS[0:m, p, 0:256],
                                                yv[0:m, p, :], ALU.add))
            ch.wait(ch.n)
            y20 = ytok[:, :, :, :].rearrange("p i h n -> p (i h) n")
            s20 = ysq[:, :, :, :].rearrange("p i h n -> p (i h) n")
            ch.link(nc.vector.tensor_reduce(rs_in[:, :], y20, AX_X, ALU.add))
            ch.link(nc.vector.tensor_scalar(rs[:, :], rs_in[:, :], -1.0 / 64, None, ALU.mult))
            ch.link(nc.vector.tensor_tensor(y20, y20, rs[:, :].unsqueeze(2).to_broadcast([P, 20, 64]), ALU.add))
            ch.link(nc.vector.tensor_tensor(s20, y20, y20, ALU.mult))
            ch.link(nc.vector.tensor_reduce(rs_in[:, :], s20, AX_X, ALU.add))
            nc.vector.tensor_scalar(rs_in[:, :], rs_in[:, :], 1.0 / 64, 64e-5, ALU.mult, ALU.add).then_inc(q["ms2"], 2)
            dve.wait_ge(q["rs2"], 1)
            nc.vector.tensor_tensor(y20, y20, rs[:, :].unsqueeze(2).to_broadcast([P, 20, 64]), ALU.mult)\
                .then_inc(q["y"], 20)
            dve.wait_ge(q["ytp"], 1)
            for t in range(2):
                ch.mark(nc.vector.tensor_scalar(yT[:, t, 0:TP], PS[:, 3 + 2 * t, :], p_("ln_g", t), p_("ln_b", t),
                                                ALU.mult, ALU.add))
                ch.mark(nc.vector.tensor_scalar(yT[:, t, TP:T], PS[:, 4, TS * t:TS * t + TS], p_("ln_g", t),
                                                p_("ln_b", t), ALU.mult, ALU.add))
            ch.wait(ch.n)
            ch.link(nc.vector.tensor_tensor(yT[:, :, :], yT[:, :, :], bonus[:, :, :], ALU.add))
            nc.vector.tensor_tensor(yT[:, :, :], yT[:, :, :], gg[:, :, :], ALU.mult).then_inc(q["out"], 1)

        at = {n: sem(f"at_{n}") for n in
              ("in", "lat_in", "pm", "sq", "kr", "row", "srow", "col", "ms", "rs", "rb", "bc", "krot", "kcos", "ksin",
               "krr", "kb", "lat", "qn", "k_mm", "ka", "kd", "v_mm", "v", "q_mm", "rot", "sin", "cos",
               "q", "s", "mx", "exp", "dg", "t", "ta", "td", "o_mm", "o", "out", "init")}
        groups = [(b, g) for b in range(TT) for g in range(2)]
        extent = lambda b: (b + 1) * P if b < 4 else PAST + TS
        ktiles = [(i, k) for i, (b, g) in enumerate(groups) for k in range(-(-extent(b) // P))]
        first_tile = [next(n for n, x in enumerate(ktiles) if x[0] == i) for i in range(len(groups))] + [len(ktiles)]

        def k_or_unit(eng, name, i, last, unit):
            if i < last:
                eng.wait_ge(at[name], i + 1)
            else:
                eng.wait_ge(unit_done, unit + 1)

        def att_sp(sp):
            sp.wait_ge(q["out"], 1)
            sp.wait_ge(rw_fin, 16 * 9)
            sp.dma_start(qup[:, :, :].rearrange("p k n -> p (k n)"), L_("qup").rearrange("l p n -> p (l n)"))\
                .then_inc(at["in"], 16)
            sp.dma_start(latT[:, :, TP:TP + PAST], L_("cache_lat").rearrange("l p k n -> p (l k) n"))\
                .then_inc(at["lat_in"], 16)
            sp.dma_start(krc[NOPE:QK, :], L_("cache_rope").rearrange("l p n -> p (l n)")).then_inc(at["lat_in"], 16)

        def att_out_sp(sp):
            sp.wait_ge(at["out"], 48)

        def att_pe(pe):
            pe.wait_ge(q["out"], 1)
            for i in range(6):
                if i == 4:
                    pe.wait_ge(at["pm"], 2)
                    pe.wait_ge(at["sq"], 2)
                if i < 5:
                    unit_mm(pe, U_MLA + i, i % 4)
            pe.wait_ge(at["pm"], 4)
            pe.wait_ge(at["sq"], 4)
            unit_wait(pe, U_MLA + 5)
            w = ring[:, (U_MLA + 5) % RING, 0:DT * ROPE].rearrange("p (k m) -> p k m", k=DT)
            for k in range(DT):
                for h in range(2):
                    ins = nc.tensor.matmul(PS[NOPE:QK, 2 + h, 0:HALF], w[:, k, :], hT[:, k, h * HALF:(h + 1) * HALF],
                                           start=(k == 0), stop=(k == DT - 1))
            ins.then_inc(unit_done, 1)
            pe.wait_ge(at["pm"], 10)
            pe.wait_ge(at["sq"], 10)
            for t in range(5):
                o, first, last = (4, t == 0, t == 2) if t < 3 else (6, t == 3, t == 4)
                for h in range(2):
                    ins = nc.tensor.matmul(PS[0:1, o + h, 0:HALF], ones[:, 0:1], msq[:, t, h * HALF:(h + 1) * HALF],
                                           start=first, stop=last)
            ins.then_inc(at["row"], 1)
            pe.wait_ge(at["kr"], 2)
            pe.wait_ge(at["init"], 1)
            for h in range(2):
                ins = nc.tensor.matmul(PS[NOPE:QK, h, 0:HALF], c_("rot")[0:QK], krt[0:QK, h * HALF:(h + 1) * HALF],
                                       start=True, stop=True)
            ins.then_inc(at["krot"], 1)
            pe.wait_ge(at["srow"], 4)
            for j in range(2):
                for i in range(TT):
                    m = P if i < 4 else TS
                    ins = nc.tensor.matmul(PS[0:m, 2, 5 * j + i:5 * j + i + 1], row[0:1, j, i * P:i * P + m],
                                           ones[0:1, 0:1], start=True, stop=True)
            ins.then_inc(at["col"], 1)
            turn_rb(pe, at, lambda i, t: rb[:, i, t, :])
            pe.wait_ge(at["lat"], 4)
            pe.wait_ge(at["lat_in"], 32)
            wk = unit_wait(pe, U_UK).rearrange("p k m -> p (k m)").rearrange("p (k m) -> p k m", k=2)
            for h in range(HEADS):
                b = 2 * ((h + 3) % 4)
                if h == 1:
                    pe.wait_ge(at["ksin"], 2)
                if h == 2:
                    pe.wait_ge(at["qn"], 6)
                if h >= 4:
                    pe.wait_ge(at["ka"], h - 3)
                    pe.wait_ge(at["kd"], h - 3)
                for o, n, lo in ((0, TP, 0), (1, PAST + TS, TP)):
                    for k in range(2):
                        ins = nc.tensor.matmul(PS[0:NOPE, b + o, 0:n], wk[:, k, h * NOPE:(h + 1) * NOPE],
                                               latT[:, k, lo:lo + n], start=(k == 0), stop=(k == 1))
                ins.then_inc(at["k_mm"] if h < 7 else unit_done, 1)
            wv = unit_wait(pe, U_UV).rearrange("p k m -> p (k m)").rearrange("p (k m) -> p k m", k=2)
            for i in range(7):
                m = P if i < 6 else TS
                if i % 2 == 0:
                    pe.wait_ge(at["ka"], 5 + i // 2)
                    pe.wait_ge(at["kd"], 5 + i // 2)
                for k in range(2):
                    ins = nc.tensor.matmul(PS[0:m, (6 + i) % 8, :], latT[:, k, i * P:i * P + m], wv[:, k, :],
                                           start=(k == 0), stop=(k == 1))
                ins.then_inc(at["v_mm"] if i < 6 else unit_done, 1)
            pe.wait_ge(at["qn"], 6)
            pe.wait_ge(at["in"], 16)
            for h in range(HEADS):
                b = 2 * ((h + 3) % 4)
                if h < 4:
                    pe.wait_ge(at["v"], min(2 * h + 2, 7))
                else:
                    pe.wait_ge(at["ka"], 8 + h - 3)
                    pe.wait_ge(at["kd"], 8 + h - 3)
                for k in range(3):
                    for o in range(2):
                        ins = nc.tensor.matmul(PS[0:QK, b + o, 0:HALF], qup[:, k, h * QK:(h + 1) * QK],
                                               pmT[:, k, o * HALF:(o + 1) * HALF], start=(k == 0), stop=(k == 2))
                ins.then_inc(at["q_mm"], 1)
            pe.wait_ge(at["ka"], 16)
            pe.wait_ge(at["kd"], 16)
            for h in range(HEADS):
                b = 2 * ((h + 3) % 4)
                if h >= 4:
                    pe.wait_ge(at["sin"], 2 * (h - 3))
                for o in range(2):
                    ins = nc.tensor.matmul(PS[NOPE:QK, b + o, 0:HALF], c_("rot")[0:QK],
                                           QT[0:QK, h, o * HALF:(o + 1) * HALF], start=True, stop=True)
                ins.then_inc(at["rot"], 1)
            pe.wait_ge(at["q"], 2)
            pe.wait_ge(at["kb"], 5)

            def scores(i):
                b, g = groups[i]
                n, m = extent(b), (P if b < 4 else TS)
                keys, rows = (KT, QK + 4) if b < 4 else (KTs, QK)
                if i:
                    pe.wait_ge(at["exp"], 4 * i)
                for j in range(4):
                    h = 4 * g + j
                    ins = nc.tensor.matmul(PS[0:m, j, 0:n], QT[0:rows, h, b * P:b * P + m], keys[0:rows, h, 0:n],
                                           start=True, stop=True)
                ins.then_inc(at["s"], 1)

            scores(0)
            for i, (b, g) in enumerate(groups):
                m = P if b < 4 else TS
                if i + 1 < len(groups):
                    scores(i + 1)
                pe.wait_ge(at["dg"], i + 1)
                for n in range(first_tile[i], first_tile[i + 1]):
                    k = ktiles[n][1]
                    if n >= 3:
                        pe.wait_ge(at["td" if (n - 3) % 2 else "ta"], (n - 3) // 2 + 1)
                    rows = min(P, extent(b) - k * P)
                    for j in range(4):
                        ins = nc.tensor.matmul(PS[0:rows, 4 + n % 3, j * P:j * P + m],
                                               prob[i % 2][0:m, j, k * P:k * P + rows], diag[i % 2][0:m, j, 0:m],
                                               start=True, stop=True)
                    ins.then_inc(at["t"], 1)
                last = first_tile[i + 1] - 1
                for n in (last, last - 1):
                    if n >= first_tile[i]:
                        pe.wait_ge(at["td" if n % 2 else "ta"], n // 2 + 1)
                if i:
                    pe.wait_ge(at["o"], i)
                tiles = range(first_tile[i], first_tile[i + 1])
                for j in range(4):
                    h = 4 * g + j
                    for n in tiles:
                        k = ktiles[n][1]
                        rows = min(P, extent(b) - k * P)
                        o = (i % 2) * 256 + (j // 2) * P
                        ins = nc.tensor.matmul(PS[64 * (j % 2):64 * (j % 2) + 64, 7, o:o + m],
                                               vv[0:rows, k + (4 if b == 4 else 0), h * VH:(h + 1) * VH],
                                               probT[i % 2][0:rows, k, j, 0:m], start=(n == tiles[0]),
                                               stop=(n == tiles[-1]), skip_group_check=True)
                ins.then_inc(at["o_mm"], 1)

        def att_act(act):
            for t in range(5):
                act.wait_ge(at["pm"], 2 * t + 2)
                nc.scalar.activation(msq[:, t, :], pmT[:, t, :], ACT.Square).then_inc(at["sq"], 2)
            act.wait_ge(unit_done, U_MLA + 6)
            for h in range(2):
                nc.scalar.copy(krt[NOPE:QK, h * HALF:(h + 1) * HALF], PS[NOPE:QK, 2 + h, 0:HALF])\
                    .then_inc(at["kr"], 1)
            for h in range(HEADS):
                k_or_unit(act, "k_mm", h, 7, U_UK)
                nc.scalar.copy(KT[0:NOPE, h, :], PS[0:NOPE, 2 * ((h + 3) % 4), :]).then_inc(at["ka"], 1)
            act.dma_start(L_("out_lat")[:, :, :, 0:TP].rearrange("l p k n -> p (l k) n"), latT[:, :, 0:TP])\
                .then_inc(at["out"], 16)
            act.dma_start(L_("out_lat")[:, :, :, TP:T].rearrange("l p k n -> p (l k) n"),
                          latT[:, :, TP + PAST:TP + PAST + TS]).then_inc(at["out"], 16)
            act.wait_ge(at["krr"], 1)
            act.dma_start(L_("out_rope").rearrange("l p n -> p (l n)"), krr[NOPE:QK, :]).then_inc(at["out"], 16)
            for i in range(7):
                m = P if i < 6 else TS
                k_or_unit(act, "v_mm", i, 6, U_UV)
                nc.scalar.copy(vv[0:m, i, :], PS[0:m, (6 + i) % 8, :]).then_inc(at["v"], 1)
            for h in range(HEADS):
                act.wait_ge(at["q_mm"], h + 1)
                nc.scalar.copy(QT[0:QK, h, 0:HALF], PS[0:QK, 2 * ((h + 3) % 4), 0:HALF]).then_inc(at["ka"], 1)

            def exps(i):
                b, g = groups[i]
                n, m = extent(b), (P if b < 4 else TS)
                act.wait_ge(at["mx"], i + 1)
                if i == 1:
                    act.wait_ge(at["out"], 48)
                if i >= 2:
                    act.wait_ge(at["t"], first_tile[i - 1])
                for j in range(4):
                    nc.scalar.activation(prob[i % 2][0:m, j, 0:n], PS[0:m, j, 0:n], ACT.Exp, scale=SCALE,
                                         bias=mx[0:m, i % 2, 1, j:j + 1], accum_out=mx[0:m, i % 2, 2, j:j + 1])\
                        .then_inc(at["exp"], 1)

            exps(0)
            for i, (b, g) in enumerate(groups):
                m = P if b < 4 else TS
                if i + 1 < len(groups):
                    exps(i + 1)
                for n in range(first_tile[i], first_tile[i + 1]):
                    if n % 2 == 0:
                        turned(act, nc.scalar.copy, i, n)
                act.wait_ge(at["o_mm"], i + 1)
                nc.scalar.copy(oT[:, 2 * g:2 * g + 2, b * P:b * P + m],
                               PS[:, 7, (i % 2) * 256:(i % 2) * 256 + 256].rearrange("p (t n) -> p t n", t=2)[:, :, 0:m])\
                    .then_inc(at["o"], 1)

        def turned(eng, copy, i, n):
            b, k = groups[i][0], ktiles[n][1]
            m, rows = (P if b < 4 else TS), min(P, extent(b) - k * P)
            eng.wait_ge(at["t"], n + 1)
            if i >= 2:
                eng.wait_ge(at["o_mm"], i - 1)
            copy(probT[i % 2][0:rows, k, :, 0:m], PS[0:rows, 4 + n % 3, :].rearrange("p (j n) -> p j n", j=4)[:, :, 0:m])\
                .then_inc(at["td" if n % 2 else "ta"], 1)

        def att_pool(pool):
            pool.wait_ge(q["out"], 1)
            nc.gpsimd.memset(krt[0:NOPE, :], 0.0).then_inc(at["init"], 1)
            pool.wait_ge(at["init"], 1)
            pool.wait_ge(rw_fin, 16 * 9)
            nc.gpsimd.tensor_copy(QT[QK:QK + 4, :, 0:TP], cos[QK:QK + 4, 0:TP].unsqueeze(1).to_broadcast([4, HEADS, TP]))\
                .then_inc(at["kb"], 1)
            pool.wait_ge(at["kb"], 1)
            nc.gpsimd.tensor_copy(KT[QK:QK + 4, :, :], sin[QK:QK + 4, 0:TP].unsqueeze(1).to_broadcast([4, HEADS, TP]))\
                .then_inc(at["kb"], 1)
            pool.wait_ge(at["kb"], 2)
            pool.wait_ge(at["krot"], 1)
            nc.gpsimd.tensor_tensor(krt[NOPE:QK, :], krt[NOPE:QK, :], cos[NOPE:QK, :], ALU.mult).then_inc(at["kcos"], 1)
            pool.wait_ge(at["kcos"], 1)
            norm_pow(pool, at, 10)
            pool.wait_ge(at["rs"], 1)
            pool.wait_ge(at["lat_in"], 32)
            nc.gpsimd.tensor_copy(KTs[NOPE:QK, :, 0:PAST], krc[NOPE:QK, :].unsqueeze(1).to_broadcast([ROPE, HEADS, PAST]))\
                .then_inc(at["kb"], 1)
            pool.wait_ge(at["krr"], 1)
            pool.wait_ge(at["kb"], 3)
            nc.gpsimd.tensor_copy(KT[NOPE:QK, :, :], krr[NOPE:QK, 0:TP].unsqueeze(1).to_broadcast([ROPE, HEADS, TP]))\
                .then_inc(at["kb"], 1)
            pool.wait_ge(at["kb"], 4)
            nc.gpsimd.tensor_copy(KTs[NOPE:QK, :, PAST:PAST + TS],
                                  krr[NOPE:QK, TP:T].unsqueeze(1).to_broadcast([ROPE, HEADS, TS])).then_inc(at["kb"], 1)
            pool.wait_ge(at["kb"], 5)
            for g in range(2):
                pool.wait_ge(at["rot"], 4 * g + 4)
                if g:
                    pool.wait_ge(at["cos"], 1)
                nc.gpsimd.tensor_tensor(QT[NOPE:QK, 4 * g:4 * g + 4, :], QT[NOPE:QK, 4 * g:4 * g + 4, :],
                                        cos[NOPE:QK, :].unsqueeze(1).to_broadcast([ROPE, 4, T]), ALU.mult)\
                    .then_inc(at["cos"], 1)
            pool.wait_ge(at["cos"], 2)

        def att_dve(dve, ch):
            for t in range(5):
                dve.wait_ge(unit_done, U_MLA + t + 1)
                for h in range(2):
                    nc.vector.tensor_copy(pmT[:, t, h * HALF:(h + 1) * HALF], PS[:, 2 * (t % 4) + h, 0:HALF])\
                        .then_inc(at["pm"], 1)
            dve.wait_ge(at["row"], 1)
            for j in range(2):
                for h in range(2):
                    nc.vector.tensor_copy(row[0:1, j, h * HALF:(h + 1) * HALF], PS[0:1, 4 + 2 * j + h, 0:HALF])\
                        .then_inc(at["srow"], 1)
            dve.wait_ge(at["krot"], 1)
            for h in range(2):
                nc.vector.tensor_tensor(krr[NOPE:QK, h * HALF:(h + 1) * HALF], PS[NOPE:QK, h, 0:HALF],
                                        sin[NOPE:QK, h * HALF:(h + 1) * HALF], ALU.mult).then_inc(at["ksin"], 1)
            dve.wait_ge(at["col"], 1)
            for j, n in ((0, QL), (1, KVL)):
                ins = nc.vector.tensor_scalar(rs_in[:, 5 * j:5 * j + 4], PS[:, 2, 5 * j:5 * j + 4], 1.0 / n, 1e-6,
                                              ALU.mult, ALU.add)
                ch.mark(ins)
                ins = nc.vector.tensor_scalar(rs_in[0:TS, 5 * j + 4:5 * j + 5], PS[0:TS, 2, 5 * j + 4:5 * j + 5],
                                              1.0 / n, 1e-6, ALU.mult, ALU.add)
                ins.then_inc(at["ms"], 2) if j else ch.mark(ins)
            dve.wait_ge(at["kcos"], 1)
            dve.wait_ge(at["ksin"], 2)
            nc.vector.tensor_tensor(krr[NOPE:QK, :], krr[NOPE:QK, :], krt[NOPE:QK, :], ALU.add).then_inc(at["krr"], 1)
            dve.wait_ge(at["rs"], 1)
            for j in range(2):
                ins = nc.vector.tensor_copy(rb[:, :, j, :], rs[:, 5 * j:5 * j + 5].unsqueeze(2).to_broadcast([P, TT, P]))
                if j:
                    ins.then_inc(at["rb"], 1)
                else:
                    ch.link(ins)
            dve.wait_ge(at["bc"], 1)
            for t in range(2):
                nc.vector.scalar_tensor_tensor(latT[:, t, 0:TP], pmT[:, 3 + t, 0:TP], p_("kv_norm_g", t), PS[:, 5, :],
                                               ALU.mult, ALU.mult).then_inc(at["lat"], 1)
                nc.vector.scalar_tensor_tensor(latT[:, t, TP + PAST:], pmT[:, 3 + t, TP:T], p_("kv_norm_g", t),
                                               PS[:, 4, TS:2 * TS], ALU.mult, ALU.mult).then_inc(at["lat"], 1)
            for t in range(3):
                nc.vector.scalar_tensor_tensor(pmT[:, t, 0:TP], pmT[:, t, 0:TP], p_("q_norm_g", t), PS[:, 3, :],
                                               ALU.mult, ALU.mult).then_inc(at["qn"], 1)
                nc.vector.scalar_tensor_tensor(pmT[:, t, TP:T], pmT[:, t, TP:T], p_("q_norm_g", t), PS[:, 4, 0:TS],
                                               ALU.mult, ALU.mult).then_inc(at["qn"], 1)
            for h in range(HEADS):
                k_or_unit(dve, "k_mm", h, 7, U_UK)
                nc.vector.tensor_copy(KTs[0:NOPE, h, :], PS[0:NOPE, 2 * ((h + 3) % 4) + 1, 0:PAST + TS])\
                    .then_inc(at["kd"], 1)
            for h in range(HEADS):
                dve.wait_ge(at["q_mm"], h + 1)
                nc.vector.tensor_copy(QT[0:QK, h, HALF:T], PS[0:QK, 2 * ((h + 3) % 4) + 1, 0:HALF]).then_inc(at["kd"], 1)
            for h in range(HEADS):
                dve.wait_ge(at["rot"], h + 1)
                for o in range(2):
                    nc.vector.tensor_tensor(sin_q[h // 4][NOPE:QK, h % 4, o * HALF:(o + 1) * HALF],
                                            PS[NOPE:QK, 2 * ((h + 3) % 4) + o, 0:HALF],
                                            sin[NOPE:QK, o * HALF:(o + 1) * HALF], ALU.mult).then_inc(at["sin"], 1)
                if h % 4 == 3:
                    g = h // 4
                    dve.wait_ge(at["cos"], g + 1)
                    dve.wait_ge(at["sin"], 2 * h + 2)
                    nc.vector.tensor_tensor(QT[NOPE:QK, 4 * g:4 * g + 4, :], QT[NOPE:QK, 4 * g:4 * g + 4, :],
                                            sin_q[g][NOPE:QK, :, :], ALU.add).then_inc(at["q"], 1)

            def maxima(i):
                b, g = groups[i]
                n, m = extent(b), (P if b < 4 else TS)
                dve.wait_ge(at["s"], i + 1)
                ch.link(nc.vector.tensor_reduce(mx[0:m, i % 2, 0, :], PS[0:m, 0:4, 0:n], AX_X, ALU.max))
                nc.vector.tensor_scalar(mx[0:m, i % 2, 1, :], mx[0:m, i % 2, 0, :], -SCALE, None, ALU.mult)\
                    .then_inc(at["mx"], 1)

            maxima(0)
            for i, (b, g) in enumerate(groups):
                m = P if b < 4 else TS
                dve.wait_ge(at["exp"], 4 * i + 4)
                if i >= 2:
                    dve.wait_ge(at["t"], first_tile[i - 1])
                elif i == 1:
                    dve.wait_ge(at["out"], 48)
                ch.link(nc.vector.reciprocal(mx[0:m, i % 2, 3, :], mx[0:m, i % 2, 2, :]))
                nc.vector.tensor_tensor(diag[i % 2][0:m, :, :], ident[0:m].unsqueeze(1).to_broadcast([m, 4, P]),
                                        mx[0:m, i % 2, 3, :].unsqueeze(2).to_broadcast([m, 4, P]), ALU.mult)\
                    .then_inc(at["dg"], 1)
                if i + 1 < len(groups):
                    maxima(i + 1)
                for n in range(first_tile[i], first_tile[i + 1]):
                    if n % 2:
                        turned(dve, nc.vector.tensor_copy, i, n)

        g_ = {n: sem(f"mg_{n}") for n in ("th", "o_mm", "u", "done", "out")}
        src_k = ((0, 4), (4, 6), (6, 8))

        def branch(b, k):
            return (oT, yT, cT)[b][:, k - src_k[b][0], :]

        def freed(pe, n):
            d_, j = divmod(n, 6)
            if j < 3:
                pe.wait_ge(g_["th"], 2 * (3 * d_ + j + 1))
            else:
                pe.wait_ge(g_["u"], 2 * (3 * d_ + j - 2))

        def merge_pe(pe):
            pe.wait_ge(at["o"], len(groups))
            for t in range(DT):
                for j in range(6):
                    n = 6 * t + j
                    if n >= 4:
                        freed(pe, n - 4)
                    if j < 3:
                        unit_mm(pe, U_MERGE + 4 * t + j, n % 4)
                        continue
                    w = unit_wait(pe, U_MERGE + 4 * t + 3)
                    lo, hi = src_k[j - 3]
                    for k in range(lo, hi):
                        for h in range(2):
                            ins = nc.tensor.matmul(PS[:, 2 * (n % 4) + h, 0:HALF], w[:, k, :],
                                                   branch(j - 3, k)[:, h * HALF:(h + 1) * HALF],
                                                   start=(k == lo), stop=(k == hi - 1))
                    ins.then_inc(unit_done if j == 5 else g_["o_mm"], 1)
            for t in range(DT):
                n = 6 * DT + t
                pe.wait_ge(g_["done"], DT)
                if t >= 4:
                    pe.wait_ge(g_["out"], 3 * (t - 3))
                else:
                    freed(pe, n - 4)
                w = unit_wait(pe, U_OUT + t)
                for k in range(DT):
                    for h in range(2):
                        ins = nc.tensor.matmul(PS[:, 2 * (n % 4) + h, 0:HALF], w[:, k, :],
                                               mg[:, k, h * HALF:(h + 1) * HALF], start=(k == 0), stop=(k == DT - 1))
                ins.then_inc(unit_done, 1)
            pe.wait_ge(g_["out"], 3 * DT)
            norm_x_pe(pe, nm["n1"], 1)

        def merge_act(act):
            for t in range(DT):
                for b in range(3):
                    n = 6 * t + b
                    act.wait_ge(unit_done, U_MERGE + 4 * t + b + 1)
                    if t >= 2:
                        act.wait_ge(g_["u"], 2 * (3 * (t - 2) + b + 1))
                    for h in range(2):
                        nc.scalar.activation(th[t % 2][:, b, h * HALF:(h + 1) * HALF], PS[:, 2 * (n % 4) + h, 0:HALF],
                                             ACT.Tanh, scale=0.5).then_inc(g_["th"], 1)
            for k in range(DT):
                act.wait_ge(g_["out"], 3 * k + 3)
                if k == 0:
                    act.wait_ge(unit_done, U_OUT)
                nc.scalar.activation(hT[:, k, :], xT[:, k, :], ACT.Square).then_inc(nm["n1"]["sq"], 1)
            norm_shift_act(act, nm["n1"], 3, 1)

        def merge_pool(pool):
            norm_pow(pool, nm["n1"], r=1)

        def merge_dve(dve, ch):
            for t in range(DT):
                for b in range(3):
                    n = 6 * t + 3 + b
                    dve.wait_ge(g_["th"], 2 * (3 * t + b + 1))
                    if b < 2:
                        dve.wait_ge(g_["o_mm"], 2 * t + b + 1)
                    else:
                        dve.wait_ge(unit_done, U_MERGE + 4 * t + 4)
                    dst = mg[:, t, :] if b == 0 else mtmp[b - 1]
                    if b == 0 and t == 0:
                        dve.wait_ge(at["o"], len(groups))
                    for h in range(2):
                        nc.vector.scalar_tensor_tensor(dst[:, h * HALF:(h + 1) * HALF],
                                                       th[t % 2][:, b, h * HALF:(h + 1) * HALF], 1.0,
                                                       PS[:, 2 * (n % 4) + h, 0:HALF], ALU.add, ALU.mult)\
                            .then_inc(g_["u"], 1)
                    dve.wait_ge(g_["u"], 2 * (3 * t + b + 1))
                    if b:
                        ins = nc.vector.tensor_tensor(mg[:, t, :], mg[:, t, :], mtmp[b - 1], ALU.add)
                        if b == 1:
                            ch.link(ins)
                        else:
                            ins.then_inc(g_["done"], 1)
            dve.wait_ge(g_["done"], DT)
            for t in range(DT):
                n = 6 * DT + t
                dve.wait_ge(unit_done, U_OUT + t + 1)
                for bank, src, lo, hi, g in ((0, 0, 0, HALF, 0), (1, 0, HALF, TP, 0), (1, TP - HALF, TP, T, 1)):
                    nc.vector.scalar_tensor_tensor(xT[:, t, lo:hi], PS[:, 2 * (n % 4) + bank, src:src + hi - lo],
                                                   half_gt1[:, t, g:g + 1], xT[:, t, lo:hi], ALU.mult, ALU.add)\
                        .then_inc(g_["out"], 1)
            norm_x_dve(dve, nm["n1"], lambda k, g: gain2[:, k, g:g + 1], 1)

        e_ = {n: sem(f"moe_{n}") for n in ("w0", "w1", "wd", "logit", "shift", "gexp", "diff", "eexp", "comb", "combT", 
                                           "mm", "th", "use", "x", "clr", "ctp")}
        order = [("gu", 0), ("gu", 1)]
        for e in range(2, NE, 2):
            order += [("gu", e), ("dn", e // 2 - 1), ("gu", e + 1)]
        order.append(("dn", NE // 2 - 1))
        start = {}
        _n = 0
        for kind, i in order:
            start[kind, i] = _n
            _n += 5 if kind == "gu" else DT

        def moe_sp(sp):
            sp.wait_ge(at["o"], len(groups))
            for p in range(NE // 2):
                for e in (2 * p, 2 * p + 1):
                    if e >= 2:
                        sp.wait_ge(e_["mm"], start["gu", e - 2] + 4)
                    sp.dma_start(gu_w[e % 2][:, :, :].rearrange("p k n -> p (k n)"),
                                 L_("moe_gu")[:, e].rearrange("l p n -> p (l n)")).then_inc(e_[f"w{e % 2}"], 16)
                if p:
                    sp.wait_ge(e_["mm"], start["dn", p - 1] + DT)
                for e in (2 * p, 2 * p + 1):
                    sp.dma_start(dn_w[e % 2][:, :, :].rearrange("p k n -> p (k n)"),
                                 L_("moe_dn")[:, e].rearrange("l p n -> p (l n)")).then_inc(e_["wd"], 16)

        def moe_pe(pe):
            pe.wait_ge(nm["n1"]["out"], 4 * DT)
            for i in range(TT):
                m = P if i < 4 else TS
                for k in range(DT):
                    ins = nc.tensor.matmul(PS[0:m, 0, 20 * i:20 * i + 20], hT[:, k, i * P:i * P + m], router_w[:, k, :],
                                           start=(k == 0), stop=(k == DT - 1))
            ins.then_inc(e_["logit"], 1)
            pe.wait_ge(e_["comb"], 1)
            for i in range(4):
                nc.tensor.transpose(PS[0:NE, 1, i * P:(i + 1) * P], cmb[:, i, :, :].rearrange("p g e -> p (g e)"), ident)
            nc.tensor.transpose(PS[0:NE, 2, 0:TS], cmb[0:TS, 4, :, :].rearrange("p g e -> p (g e)"), ident[0:TS, 0:TS])\
                .then_inc(e_["ctp"], 1)
            pe.wait_ge(e_["combT"], 2)
            for kind, i in order:
                if kind == "gu":
                    pe.wait_ge(e_[f"w{i % 2}"], 16 * (i // 2 + 1))
                    for j in range(4):
                        n = start[kind, i] + j
                        if n >= 4:
                            pe.wait_ge(e_["use"], n - 3)
                        o = (j % 2) * FE + (j // 2) * P
                        for k in range(DT):
                            for h in range(2):
                                ins = nc.tensor.matmul(PS[:, 2 * (n % 4) + h, 0:HALF], gu_w[i % 2][:, k, o:o + P],
                                                       hT[:, k, h * HALF:(h + 1) * HALF],
                                                       start=(k == 0), stop=(k == DT - 1))
                        ins.then_inc(e_["mm"], 1)
                    n = start[kind, i] + 4
                    pe.wait_ge(e_["use"], n - 3)
                    for h in range(2):
                        ins = nc.tensor.matmul(PS[:, 2 * (n % 4) + h, 0:HALF], ident[0:NE, i:i + 1].to_broadcast([NE, P]),
                                               cmbT[0:NE, h * HALF:(h + 1) * HALF], start=True, stop=True)
                    ins.then_inc(e_["mm"], 1)
                else:
                    pe.wait_ge(e_["use"], start["gu", 2 * i + 1] + 5)
                    pe.wait_ge(e_["wd"], 32 * (i + 1))
                    for t in range(DT):
                        n = start[kind, i] + t
                        pe.wait_ge(e_["use"], n - 3)
                        for e in range(2):
                            for k in range(2):
                                for h in range(2):
                                    ins = nc.tensor.matmul(PS[:, 2 * (n % 4) + h, 0:HALF],
                                                           dn_w[e][:, k, t * P:(t + 1) * P],
                                                           eact[:, (2 * i + e) % 3, k, h * HALF:(h + 1) * HALF],
                                                           start=(e == 0 and k == 0), stop=(e == 1 and k == 1))
                        ins.then_inc(e_["mm"], 1)

        def moe_act(act):
            act.wait_ge(e_["shift"], 1)
            nc.scalar.activation(ra[:, 0, :, :], ra[:, 0, :, :], ACT.Exp).then_inc(e_["gexp"], 1)
            act.wait_ge(e_["diff"], 1)
            nc.scalar.activation(rm[:, 3, :], rm[:, 3, :], ACT.Exp).then_inc(e_["eexp"], 1)
            act.wait_ge(e_["ctp"], 1)
            nc.scalar.copy(cmbT[0:NE, 0:TP], PS[0:NE, 1, :]).then_inc(e_["combT"], 1)
            nc.scalar.copy(cmbT[0:NE, TP:T], PS[0:NE, 2, 0:TS]).then_inc(e_["combT"], 1)
            c = 0
            for i in range(NE):
                for f in range(2):
                    n = start["gu", i] + 2 * f
                    act.wait_ge(e_["mm"], n + 1)
                    for h in range(2):
                        if c >= 2:
                            pc = c - 2
                            pi, pf = pc // 4, (pc // 2) % 2
                            act.wait_ge(e_["use"], start["gu", pi] + 2 * pf + 1)
                        nc.scalar.activation(eth[c % 2], PS[:, 2 * (n % 4) + h, 0:HALF], ACT.Tanh, scale=0.5)\
                            .then_inc(e_["th"], 1)
                        c += 1

        def moe_pool(pool):
            pool.wait_ge(g_["done"], DT)
            nc.gpsimd.memset(lg[:, 4, :], 0.0).then_inc(e_["clr"], 1)
            pool.wait_ge(unit_done, U_OUT)
            nc.gpsimd.memset(yacc[:, :, :], 0.0).then_inc(e_["clr"], 1)

        def moe_dve(dve, ch):
            V = nc.vector
            A, B, C, D_ = (ra[:, i, :, :] for i in range(4))
            col = lambda i: rm[:, i, :]
            wide = lambda i: rm[:, i, :].unsqueeze(2).to_broadcast([P, TT, 4])
            fall = c_("falling").unsqueeze(1).to_broadcast([P, TT, 4])
            glog = lg[:, :, 0:4]
            dve.wait_ge(e_["logit"], 1)
            dve.wait_ge(e_["clr"], 1)
            ch.mark(V.tensor_tensor(lg[:, 0:4, :], PS[:, 0, 0:80].rearrange("p (i n) -> p i n", i=4),
                                    router_b[:, :].unsqueeze(1).to_broadcast([P, 4, 20]), ALU.add))
            ch.link(V.tensor_tensor(lg[0:TS, 4, :], PS[0:TS, 0, 80:100], router_b[0:TS, :], ALU.add))

            def first_max(src, at_col, dst, tmp):
                ch.link(V.tensor_reduce(col(at_col), src, AX_X, ALU.max))
                ch.link(V.tensor_tensor(dst, src, wide(at_col), ALU.is_equal))
                ch.link(V.tensor_tensor(dst, dst, fall, ALU.mult))
                ch.link(V.tensor_reduce(col(7), dst, AX_X, ALU.max))
                ch.link(V.tensor_tensor(dst, dst, wide(7), ALU.is_equal))
            first_max(glog, 0, B, None)
            V.tensor_tensor(A, glog, wide(0), ALU.subtract).then_inc(e_["shift"], 1)
            ch.link(V.tensor_tensor(grp[:, :, :, :], lg[:, :, 4:20].rearrange("p i (g e) -> p i g e", g=4),
                                    B.unsqueeze(3).to_broadcast([P, TT, 4, 4]), ALU.mult))
            ch.link(V.tensor_reduce(C, grp[:, :, :, :].rearrange("p i g e -> p i e g"), AX_X, ALU.add))
            dve.wait_ge(e_["gexp"], 1)
            ch.link(V.tensor_reduce(col(1), A, AX_X, ALU.add))
            ch.link(V.reciprocal(col(1), col(1)))
            first_max(C, 2, D_, None)
            ch.link(V.scalar_tensor_tensor(C, D_, -1e30, C, ALU.mult, ALU.add))
            first_max(C, 4, A, None)
            V.tensor_tensor(col(3), col(4), col(2), ALU.subtract).then_inc(e_["diff"], 1)
            dve.wait_ge(e_["eexp"], 1)
            ch.link(V.tensor_scalar(col(5), col(3), 1.0, None, ALU.add))
            ch.link(V.reciprocal(col(5), col(5)))
            ch.link(V.tensor_tensor(col(5), col(5), col(1), ALU.mult))
            ch.link(V.tensor_tensor(col(6), col(5), col(3), ALU.mult))
            ch.link(V.tensor_tensor(D_, D_, wide(5), ALU.mult))
            ch.link(V.tensor_tensor(A, A, wide(6), ALU.mult))
            ch.link(V.tensor_tensor(A, A, D_, ALU.add))
            V.tensor_tensor(cmb[:, :, :, :], B.unsqueeze(3).to_broadcast([P, TT, 4, 4]),
                            A.unsqueeze(2).to_broadcast([P, TT, 4, 4]), ALU.mult).then_inc(e_["comb"], 1)
            dve.wait_ge(e_["clr"], 2)
            c = 0
            for kind, i in order:
                if kind == "gu":
                    dst = eact[:, i % 3, :, :]
                    if i >= 3:
                        dve.wait_ge(e_["mm"], start["dn", (i - 3) // 2] + DT)
                    for f in range(2):
                        n = start[kind, i] + 2 * f
                        for h in range(2):
                            c += 1
                            dve.wait_ge(e_["th"], c)
                            ins = V.scalar_tensor_tensor(dst[:, f, h * HALF:(h + 1) * HALF], eth[(c - 1) % 2], 1.0,
                                                         PS[:, 2 * (n % 4) + h, 0:HALF], ALU.add, ALU.mult)
                            ins.then_inc(e_["use"], 1) if h else ch.mark(ins)
                        ch.wait(ch.n)
                        dve.wait_ge(e_["use"], n + 1)
                        dve.wait_ge(e_["mm"], n + 2)
                        for h in range(2):
                            ins = V.tensor_tensor(dst[:, f, h * HALF:(h + 1) * HALF], dst[:, f, h * HALF:(h + 1) * HALF],
                                                  PS[:, 2 * ((n + 1) % 4) + h, 0:HALF], ALU.mult)
                            ins.then_inc(e_["use"], 1) if h else ch.mark(ins)
                    n = start[kind, i] + 4
                    ch.wait(ch.n)
                    dve.wait_ge(e_["use"], n)
                    dve.wait_ge(e_["mm"], n + 1)
                    for h in range(2):
                        ins = V.tensor_tensor(dst[:, :, h * HALF:(h + 1) * HALF], dst[:, :, h * HALF:(h + 1) * HALF],
                                              PS[:, 2 * (n % 4) + h, 0:HALF].unsqueeze(1).to_broadcast([P, 2, HALF]),
                                              ALU.mult)
                        if h:
                            ins.then_inc(e_["use"], 1)
                else:
                    for t in range(DT):
                        n = start[kind, i] + t
                        dve.wait_ge(e_["mm"], n + 1)
                        for h in range(2):
                            ins = V.tensor_tensor(yacc[:, t, h * HALF:(h + 1) * HALF], yacc[:, t, h * HALF:(h + 1) * HALF],
                                                  PS[:, 2 * (n % 4) + h, 0:HALF], ALU.add)
                            ins.then_inc(e_["use"], 1) if h else ch.mark(ins)
            ch.wait(ch.n)
            dve.wait_ge(e_["use"], start["dn", NE // 2 - 1] + DT)
            for t in range(DT):
                for g, lo, hi in ((0, 0, TP), (1, TP, T)):
                    V.scalar_tensor_tensor(xT[:, t, lo:hi], yacc[:, t, lo:hi], half_gt2[:, t, g:g + 1], xT[:, t, lo:hi],
                                           ALU.mult, ALU.add).then_inc(e_["x"], 1)

        def final_norm(block):
            s = nm["n1"]

            @block.scalar
            def _(act):
                norm_x_act(act, s)
                act.wait_ge(s["g"], 2 * DT)
                act.dma_start(d["out_y"], hT[:, :, :]).then_inc(s["out"], 16)
                act.wait_ge(s["out"], 16)

            @block.tensor
            def _(pe):
                norm_x_pe(pe, s)

            @block.gpsimd
            def _(pool):
                norm_pow(pool, s)

            @block.vector
            def _(dve):
                norm_x_dve(dve, s, lambda k, g: fin_g[:, k:k + 1])

        with nc.Block() as block:
            @block.sync
            def _(sp):
                sp.dma_start(xT[:, :, :], d["x"]).then_inc(s_const, 16)
                sp.dma_start(cst[:, :], d["const"]).then_inc(s_const, 16)
                sp.dma_start(c_tmp[:, :, :], d["c"]).then_inc(s_const, 16)
                sp.dma_start(fin_g[:, :], d["final_g"]).then_inc(s_const, 16)
                sp.wait_ge(s_const, 64)

            @block.gpsimd
            def _(pool):
                nc.gpsimd.memset(minus_half[:, :], -0.5)
                nc.gpsimd.memset(rs_in[:, :], 1.0)

            @block.scalar
            def _(act):
                act.wait_ge(s_const, 64)
                nc.scalar.activation(silu_c[:, :, :], c_tmp[:, :, :], ACT.Tanh, scale=0.5).then_inc(s_c, 1)

            @block.vector
            def _(dve):
                ch = Chain(dve, dch)
                dve.wait_ge(s_c, 1)
                ch.link(nc.vector.tensor_scalar(silu_c[:, :, :], silu_c[:, :, :], 0.5, 0.5, ALU.mult, ALU.add))
                ch.link(nc.vector.tensor_tensor(silu_c[:, :, :], silu_c[:, :, :], c_tmp[:, :, :], ALU.mult))

        nums = sorted(s.num for s in sems)
        assert nums[-1] - nums[0] == len(nums) - 1, "semaphores of the kernel are neighbours"
        clear = range(nums[0], nums[-1] + 1)
        nc.all_engine_barrier(sems_to_clear=clear)

        with nc.Fori(0, DEPTH) as layer:
            def L(name):
                return d[name][bass.ds(layer, 1)]

            lay[0] = L

            with nc.Block() as block:
                @block.sync
                def _(sp):
                    sp.dma_start(prm[:, :], L("params").rearrange("l p n -> p (l n)")).then_inc(s_prm, 16)
                    sp.dma_start(lora[:, :, :], L("lora").rearrange("l p a n -> p (l a) n")).then_inc(s_lora, 16)
                    sp.dma_start(shift_in[:, :], L("shift").rearrange("l p n -> p (l n)")).then_inc(s_lora, 16)
                    sp.dma_start(router_w[:, :, :], L("router").rearrange("l p k n -> p (l k) n")).then_inc(s_lora, 16)
                    sp.dma_start(router_b[:, :], L("router_b").rearrange("l p n -> p (l n)")).then_inc(s_lora, 16)
                    for n in range(UNITS):
                        if n == U_MLA:
                            att_sp(sp)
                        if n >= RING:
                            sp.wait_ge(unit_done, n - RING + 1)
                        sp.dma_start(ring[:, n % RING, :], L("wstream")[:, n].rearrange("l p w -> p (l w)"))\
                            .then_inc(ring_full[n % RING], 16)
                    att_out_sp(sp)
                    moe_sp(sp)

                @block.tensor
                def _(pe):
                    def turn(g):
                        pe.wait_ge(ada_row, g + 1)
                        for j in range(4 * g, 4 * g + 4):
                            ins = nc.tensor.transpose(PS[:, 4, 2 * j:2 * j + 2], mod_row[0:2, j * P:(j + 1) * P],
                                                      ident[0:2, 0:2])
                        return ins
                    for n in range(U_ADA, U_CV):
                        g, j = n // 4, n % 4
                        w = unit_wait(pe, n)
                        if j == 0 and g >= 4:
                            pe.wait_ge(ada_row, g - 3)
                        for k in range(DT):
                            ins = nc.tensor.matmul(PS[0:2, g % 4, j * P:(j + 1) * P], silu_c[:, k, :], w[:, k, :],
                                                   start=(k == 0), stop=(k == DT - 1))
                        ins.then_inc(unit_done, 1)
                        if j == 3 and g >= 1:
                            turn(g - 1)
                    turn(11).then_inc(ada_tp, 1)
                    pe.wait_ge(ada_row, 12)
                    norm_x_pe(pe, nm["n1"])
                    pe.wait_ge(mod_ready, 1)
                    pe.wait_ge(nm["n1"]["out"], 2 * DT)
                    for i in range(4):
                        unit_mm(pe, U_CV + i, i)
                    s = nm["cv"]
                    pe.wait_ge(cv_y, 2)
                    for t in range(2):
                        for h in range(2):
                            ins = nc.tensor.matmul(PS[:, h, 0:CYW // 2], ones, cy[:, t, h * 287:(h + 1) * 287],
                                                   start=(t == 0), stop=(t == 1))
                    ins.then_inc(cv_mu, 1)
                    pe.wait_ge(s["sq"], 2)
                    for t in range(2):
                        for h in range(2):
                            ins = nc.tensor.matmul(PS[0:1, 4 + h, 0:CYW // 2], ones[:, 0:1],
                                                   csq[:, t, h * 287:(h + 1) * 287], start=(t == 0), stop=(t == 1))
                    ins.then_inc(s["row"], 1)
                    norm_cols_pe(pe, s, CYW - TS)
                    norm_pe_tail(pe, s)
                    rwkv_pe(pe)
                    att_pe(pe)
                    merge_pe(pe)
                    moe_pe(pe)

                @block.scalar
                def _(act):
                    norm_x_act(act, nm["n1"])
                    act.wait_ge(mod_ready, 1)
                    act.dma_start(cb[:, :, CW - 1 + TP:CW - 1 + TP + CW - 1],
                                  L("state_conv").rearrange("l p a n -> p (l a) n")).then_inc(cv_state, 16)
                    norm_shift_act(act, nm["n1"], 0)
                    for i in range(2):
                        act.wait_ge(unit_done, U_CV + i + 1)
                        for h in range(2):
                            nc.scalar.activation(cth[:, i, h * HALF:(h + 1) * HALF], PS[:, 2 * i + h, 0:HALF],
                                                 ACT.Tanh, scale=0.5).then_inc(cv_th, 1)
                    act.wait_ge(cv_glu, 6)
                    act.wait_ge(cv_state, 16)
                    act.dma_start(L("out_conv")[:, 0].rearrange("l p a n -> p (l a) n"),
                                  cb[:, :, TP:TP + CW - 1]).then_inc(cv_out, 16)
                    act.dma_start(L("out_conv")[:, 1].rearrange("l p a n -> p (l a) n"),
                                  cb[:, :, CBW - (CW - 1):CBW]).then_inc(cv_out, 16)
                    act.wait_ge(cv_cent, 4)
                    for t in range(2):
                        nc.scalar.activation(csq[:, t, :], cy[:, t, :], ACT.Square).then_inc(nm["cv"]["sq"], 1)
                    act.wait_ge(cv_zh, 4)
                    nc.scalar.activation(cth[:, :, :], cT[:, :, :], ACT.Tanh).then_inc(cv_t2, 1)
                    act.wait_ge(cv_out, 32)
                    rwkv_act(act)
                    att_act(act)
                    merge_act(act)
                    moe_act(act)

                @block.gpsimd
                def _(pool):
                    norm_pow(pool, nm["n1"])
                    pool.wait_ge(mod_ready, 1)
                    nc.gpsimd.memset(cb[:, :, 0:CW - 1], 0.0).then_inc(cv_init, 1)
                    norm_pow(pool, nm["cv"])
                    rwkv_pool(pool)
                    att_pool(pool)
                    merge_pool(pool)
                    moe_pool(pool)

                @block.vector
                def _(dve):
                    ch = Chain(dve, dch)
                    for g in range(12):
                        dve.wait_ge(unit_done, 4 * g + 4)
                        nc.vector.tensor_copy(mod_row[0:2, 512 * g:512 * g + 512], PS[0:2, g % 4, :])\
                            .then_inc(ada_row, 1)
                    dve.wait_ge(ada_tp, 1)
                    dve.wait_ge(s_prm, 16)
                    nc.vector.tensor_tensor(mod[:, :, :], PS[:, 4, 0:96].rearrange("p (n g) -> p n g", g=2),
                                            p_("ada_b").unsqueeze(2).to_broadcast([P, 48, 2]), ALU.add)\
                        .then_inc(mod_ready, 1)
                    dve.wait_ge(mod_ready, 1)
                    for g in range(2):
                        ch.mark(nc.vector.scalar_tensor_tensor(gain1[:, :, g], mod[:, DT:2 * DT, g], 1.0,
                                                               p_("norm1_g"), ALU.add, ALU.mult))
                        ch.mark(nc.vector.scalar_tensor_tensor(gain2[:, :, g], mod[:, 4 * DT:5 * DT, g], 1.0,
                                                               p_("norm2_g"), ALU.add, ALU.mult))
                    ch.mark(nc.vector.tensor_scalar(half_gt1[:, :, :], mod[:, 2 * DT:3 * DT, :], 0.5, None, ALU.mult))
                    ch.link(nc.vector.tensor_scalar(half_gt2[:, :, :], mod[:, 5 * DT:6 * DT, :], 0.5, None, ALU.mult))
                    norm_x_dve(dve, nm["n1"], lambda k, g: gain1[:, k, g:g + 1])
                    for t in range(2):
                        dve.wait_ge(cv_th, 2 * t + 2)
                        ch.mark(nc.vector.tensor_scalar(cth[:, t, :], cth[:, t, :], 0.5, 0.5, ALU.mult, ALU.add))
                    ch.wait(ch.n)
                    for t in range(2):
                        dve.wait_ge(unit_done, U_CV + 3 + t)
                        b = 2 * (2 + t)
                        for o, lo, hi, bank in ((CW - 1, 0, HALF, b), (CW - 1 + HALF, HALF, TP, b + 1),
                                                (CBW - TS, TP, T, b + 1)):
                            src = lo - HALF * (bank - b)
                            nc.vector.tensor_tensor(cb[:, t, o:o + hi - lo], cth[:, t, lo:hi],
                                                    PS[:, bank, src:src + hi - lo], ALU.mult).then_inc(cv_glu, 1)
                    dve.wait_ge(cv_glu, 6)
                    dve.wait_ge(cv_init, 1)
                    dve.wait_ge(cv_state, 16)
                    for k in range(CW):
                        for t in range(2):
                            tap = p_("dw", t * CW + k)
                            if k == 0:
                                ins = nc.vector.tensor_scalar(cy[:, t, :], cb[:, t, 0:CYW], tap, p_("dw_b", t),
                                                              ALU.mult, ALU.add)
                            else:
                                ch.wait(ch.n if k == CW - 1 and t else ch.n - 1)
                                ins = nc.vector.scalar_tensor_tensor(cy[:, t, :], cb[:, t, k:k + CYW], tap,
                                                                     cy[:, t, :], ALU.mult, ALU.add)
                            if k == CW - 1:
                                ins.then_inc(cv_y, 1)
                            else:
                                ch.mark(ins)
                    dve.wait_ge(cv_mu, 1)
                    dve.wait_ge(cv_y, 2)
                    for t in range(2):
                        for h in range(2):
                            nc.vector.scalar_tensor_tensor(cy[:, t, h * 287:(h + 1) * 287], PS[:, h, 0:287],
                                                           -1.0 / CD, cy[:, t, h * 287:(h + 1) * 287],
                                                           ALU.mult, ALU.add).then_inc(cv_cent, 1)
                    s = nm["cv"]
                    dve.wait_ge(s["row"], 1)
                    for h in range(2):
                        nc.vector.tensor_copy(row[0:1, 0, h * 287:(h + 1) * 287], PS[0:1, 4 + h, 0:287])\
                            .then_inc(s["srow"], 1)
                    norm_cols_dve(dve, s, CD, 1e-5)
                    dve.wait_ge(s["bc"], 1)
                    dve.wait_ge(cv_cent, 4)
                    for t in range(2):
                        for src, lo, hi, bank in ((0, 0, TP, 3), (CYW - TS, TP, T, 4)):
                            ch.link(nc.vector.scalar_tensor_tensor(
                                cT[:, t, lo:hi], cy[:, t, src:src + hi - lo], p_("cln_g", t), PS[:, bank, 0:hi - lo],
                                ALU.mult, ALU.mult))
                            nc.vector.tensor_scalar(cT[:, t, lo:hi], cT[:, t, lo:hi], p_("cln_b", t), 0.5,
                                                    ALU.add, ALU.mult).then_inc(cv_zh, 1)
                    dve.wait_ge(cv_zh, 4)
                    dve.wait_ge(cv_t2, 1)
                    nc.vector.scalar_tensor_tensor(cT[:, :, :], cth[:, :, :], 1.0, cT[:, :, :],
                                                   ALU.add, ALU.mult).then_inc(cv_done, 1)
                    rwkv_dve(dve, ch)
                    att_dve(dve, ch)
                    merge_dve(dve, ch)
                    moe_dve(dve, ch)

            nc.all_engine_barrier(sems_to_clear=clear)

        with nc.Block() as block:
            final_norm(block)


def const_array():
    c = np.zeros((P, NCONST), np.float32)

    def put(name, v):
        o, n = CONST[name]
        c[:, o:o + n] = np.asarray(v, np.float32).reshape(P, n)
    i, j = np.indices((P, P))
    same = (i // 64 == j // 64)
    put("ident", i == j)
    put("ones", np.ones((P, P)))
    put("blk", same)
    strict, incl = same & (i < j), same & (i <= j)
    put("gram", np.stack([strict, strict, incl, incl], 1))
    up = lambda b: (i // (2 * b) == j // (2 * b)) & (i // b < j // b)
    put("first_t", up(1))
    put("first", up(1).T)
    put("levels", np.stack([-1.0 * up(b) for b in (2, 4, 8, 16, 32)], 1))
    rot = np.zeros((P, ROPE))
    for m in range(16):
        rot[NOPE + 16 + m, m] = -1.0
        rot[NOPE + m, 16 + m] = 1.0
    put("rot", rot)
    pos = np.concatenate([np.arange(TP), PAST + np.arange(TS)]).astype(np.float32)
    inv = (np.float32(10000.0) ** (-np.arange(16, dtype=np.float32) / 16)).astype(np.float32)
    ang = pos[None, :] * inv[:, None]
    tab = np.zeros((2, P, T), np.float32)
    for q in range(2):
        tab[0, NOPE + 16 * q:NOPE + 16 * q + 16] = np.cos(ang)
        tab[1, NOPE + 16 * q:NOPE + 16 * q + 16] = np.sin(ang)
    for b in range(4):
        tab[0, QK + b, 2 * b * CHUNK:(2 * b + 1) * CHUNK] = 1.0
        tab[1, QK + b, (2 * b + 1) * CHUNK:(2 * b + 2) * CHUNK] = -1e30
    put("cos", tab[0])
    put("sin", tab[1])
    put("falling", np.broadcast_to(4.0 - np.arange(4), (P, 4)))
    put("scan", np.broadcast_to((np.arange(T) % CHUNK != 0), (P, T)))
    return c


def host(inputs):
    g = {k: np.asarray(v) for k, v in inputs.items()}
    f32 = np.float32

    def rows(w):
        l, k, m = w.shape
        return w.reshape(l, k // P, P, m).transpose(0, 2, 1, 3)

    def cols(v):
        return v.reshape(v.shape[0], -1, P).transpose(0, 2, 1)

    units = np.zeros((DEPTH, UNITS, P, UW), f32)

    def put(n, w):
        units[:, n, :, :w.shape[2] * w.shape[3]] = w.reshape(DEPTH, P, -1)

    ada, w_in = rows(g["ada_w"]), rows(g["w_in"])
    for j in range(48):
        put(U_ADA + j, ada[..., j * P:(j + 1) * P])
    mla, rw = QL + KVL + ROPE, QL + KVL + ROPE + 1024
    cv, gates = rw, rw + 2 * CD
    for i, o in enumerate((2, 3, 0, 1)):
        put(U_CV + i, w_in[..., cv + o * P:cv + (o + 1) * P])
    for i in range(8):
        put(U_RW + i, w_in[..., mla + i * P:mla + (i + 1) * P])
    for i in range(5):
        put(U_MLA + i, w_in[..., i * P:(i + 1) * P])
    put(U_MLA + 5, w_in[..., QL + KVL:QL + KVL + ROPE])
    put(U_UK, rows(g["w_uk"].reshape(DEPTH, KVL, -1)))
    put(U_UV, rows(g["w_uv"].reshape(DEPTH, KVL, -1)))
    w_out = rows(g["w_out"])
    proj = np.concatenate([rows(g["proj_a"]), rows(g["proj_b"]), rows(g["proj_c"])], 2)
    for i in range(DT):
        for b in range(3):
            o = gates + b * DM + i * P
            put(U_MERGE + 4 * i + b, w_in[..., o:o + P])
        put(U_MERGE + 4 * i + 3, proj[..., i * P:(i + 1) * P])
        put(U_OUT + i, w_out[..., i * P:(i + 1) * P])
    dw = g["conv_dw"].reshape(DEPTH, CW, 2, P).transpose(0, 3, 2, 1).reshape(DEPTH, P, 2 * CW)
    par = {"ada_b": cols(g["ada_b"]), "norm1_g": cols(g["norm1_g"]), "norm2_g": cols(g["norm2_g"]),
           "q_norm_g": cols(g["q_norm_g"]), "kv_norm_g": cols(g["kv_norm_g"]), "mu": cols(g["rwkv_mu"]),
           "w0": cols(g["rwkv_w0"]), "a0": cols(g["rwkv_a0"]), "k_k": cols(g["rwkv_k_k"]), "k_a": cols(g["rwkv_k_a"]),
           "r_k": cols(g["rwkv_r_k"].reshape(DEPTH, -1)), "ln_g": cols(g["rwkv_ln_g"]), "ln_b": cols(g["rwkv_ln_b"]),
           "dw": dw, "dw_b": cols(g["conv_dw_b"]), "cln_g": cols(g["conv_ln_g"]), "cln_b": cols(g["conv_ln_b"])}
    params = np.concatenate([par[n] for n in PARAM], 2)
    lora = np.zeros((DEPTH, P, 3, RH * 64), f32)
    lora[:, 0:64, 0] = g["rwkv_w2"]
    lora[:, 64:128, 1] = g["rwkv_a2"]
    lora[:, :, 2] = g["rwkv_g2"]
    x = np.concatenate([g["x_prompt"][0], g["x_sample"][0]], 0)
    feat = lambda a: a.reshape(a.shape[0], DT, P).transpose(2, 1, 0)
    c = np.concatenate([g["c_prompt"], g["c_sample"]], 0)
    moe_gu = np.concatenate([g["moe_w_gate"], g["moe_w_up"]], 3).reshape(DEPTH, NE, DT, P, 2 * FE)\
        .transpose(0, 1, 3, 2, 4).reshape(DEPTH, NE, P, DT * 2 * FE)
    moe_dn = g["moe_w_down"].reshape(DEPTH, NE, 2, P, DM).transpose(0, 1, 3, 2, 4).reshape(DEPTH, NE, P, 2 * DM)
    router = np.concatenate([g["router_group_w"], g["router_expert_w"]], 2)
    router_b = np.concatenate([g["router_group_b"], g["router_expert_b"]], 1)
    conv = g["state_conv"][:, 0].reshape(DEPTH, CW - 1, 2, P).transpose(0, 3, 2, 1)
    arrays = dict(x=feat(x), c=feat(c), const=const_array(), params=params, lora=lora, wstream=units,
                  qup=rows(g["q_up"]).reshape(DEPTH, P, -1), moe_gu=moe_gu, moe_dn=moe_dn, router=rows(router),
                  router_b=np.broadcast_to(router_b[:, None], (DEPTH, P, 20)), final_g=g["final_g"].reshape(DT, P).T,
                  cache_lat=g["cache_kv_latent"][:, 0].reshape(DEPTH, PAST, 2, P).transpose(0, 3, 2, 1),
                  cache_rope=g["cache_k_rope"][:, 0].transpose(0, 2, 1),
                  shift=cols(g["state_rwkv_shift"][:, 0]), wkv=g["state_rwkv_wkv"][:, 0].transpose(0, 1, 3, 2),
                  state_conv=conv)
    return {k: np.ascontiguousarray(v) for k, v in arrays.items()}


OUTS = dict(out_y=(P, DT, T), out_lat=(DEPTH, P, 2, T), out_rope=(DEPTH, ROPE, T), out_shift=(DEPTH, P, 2, 8),
            out_wkv=(DEPTH, 2, RH, 64, 64), out_conv=(DEPTH, 2, P, 2, CW - 1))


def kernel(**inputs):
    import concourse.bacc as _bacc
    from concourse.bass_utils import run_bass_kernel_spmd as _run

    arrays = host(inputs)
    nc = _bacc.Bacc("TRN2", target_bir_lowering=False, num_devices=1)
    d = {k: nc.dram_tensor(k, v.shape, F32, kind="ExternalInput").ap() for k, v in arrays.items()}
    d |= {k: nc.dram_tensor(k, s, F32, kind="ExternalOutput").ap() for k, s in OUTS.items()}
    build(nc, d)
    r = _run(nc, [arrays], core_ids=[0])
    o = {k: r.results[0][k] for k in OUTS}
    y = o["out_y"].transpose(2, 1, 0).reshape(T, DM)
    lat = o["out_lat"].transpose(0, 3, 2, 1).reshape(DEPTH, T, KVL)
    rope = o["out_rope"].transpose(0, 2, 1)
    shift = o["out_shift"].transpose(0, 2, 3, 1).reshape(DEPTH, 2, 1024)
    wkv = o["out_wkv"].transpose(0, 1, 2, 4, 3)
    conv = o["out_conv"].transpose(0, 1, 4, 3, 2).reshape(DEPTH, 2, CW - 1, CD)
    res = (y[None, :TP], y[None, TP:], lat[:, None, :TP], rope[:, None, :TP], shift[:, 0:1], wkv[:, 0:1], conv[:, 0:1],
           lat[:, None, TP:], rope[:, None, TP:], shift[:, 1:2], wkv[:, 1:2], conv[:, 1:2])
    return tuple(np.ascontiguousarray(a) for a in res)
```

```python
from contextlib import ExitStack

import numpy as np

import concourse.bass as bass
from concourse import mybir

F32 = mybir.dt.float32
BF16 = mybir.dt.bfloat16
FAST = mybir.dt.float32r
ALU = mybir.AluOpType
ACT = mybir.ActivationFunctionType
AX_X = mybir.AxisListType.X

P = 128
DM, DEPTH = 1024, 2
TP, TS = 512, 32
T = TP + TS
HALF = T // 2
DT = DM // P
TT = 5
PAST = 256
HEADS, NOPE, ROPE, VH = 8, 64, 32, 64
QL, KVL = 384, 256
QK = NOPE + ROPE
SCALE = float(QK) ** -0.5
RH = 4
CW, CD = 31, 256
NE, FE = 16, 256
CHUNK = 64
DECAY = float(np.exp(-0.5))
PADT = TT * P

U_ADA, U_CV, U_RW, U_AD2, U_AD3, U_MLA, U_UK, U_UV = 0, 16, 20, 28, 40, 60, 66, 67
U_MERGE = 68
U_OUT = U_MERGE + 4 * DT
UNITS = U_OUT + DT
RING = 6
UW = DT * P

PARAM = {}
_at = 0
for _name, _n in (("ada_b", 48), ("norm1_g", 8), ("norm2_g", 8), ("q_norm_g", 3), ("kv_norm_g", 2), ("mu", 8),
                  ("w0", 2), ("a0", 2), ("k_k", 2), ("k_a", 2), ("r_k", 2), ("ln_g", 2), ("ln_b", 2),
                  ("dw", 2 * CW), ("dw_b", 2), ("cln_g", 2), ("cln_b", 2)):
    PARAM[_name] = (_at, _n)
    _at += _n
NPARAM = _at

CONST = {}
_at = 0
for _name, _n in (("ident", P), ("ones", P), ("blk", P), ("gram", 4 * P), ("first", P), ("first_t", P),
                  ("levels", 5 * P), ("rot", ROPE), ("cos", T), ("sin", T), ("scan", T), ("before", P),
                  ("falling", 4), ("valid", TT), ("slot0", NE)):
    CONST[_name] = (_at, _n)
    _at += _n
NCONST = _at
ARENA = 29568


class Chain:

    def __init__(self, eng, sem):
        self.eng, self.sem, self.n = eng, sem, 0

    def mark(self, ins):
        ins.then_inc(self.sem, 1)
        self.n += 1
        return self.n

    def link(self, ins):
        self.eng.wait_ge(self.sem, self.mark(ins))

    def wait(self, n):
        self.eng.wait_ge(self.sem, n)


def build(nc, d):
    ctx = ExitStack()
    with ctx:
        def sb(name, shape):
            return ctx.enter_context(nc.sbuf_tensor("s_" + name, shape, F32))

        sems = []

        def sem(name):
            s = ctx.enter_context(nc.semaphore(name))
            sems.append(s)
            return s

        PS = ctx.enter_context(nc.psum_tensor("PS", [P, 8, 512], F32))
        xT = sb("xT", [P, DT, T])
        hT = sb("hT", [P, DT, T])
        ring = sb("ring", [P, RING, UW])
        cst = sb("cst", [P, NCONST])
        prm = sb("prm", [P, NPARAM])
        fin_g = sb("fin_g", [P, DT])
        silu_c = sb("silu_c", [P, DT, 2])
        c_tmp = sb("c_tmp", [P, DT, 2])
        mod = sb("mod", [P, 6 * DT, 2])
        gain1 = sb("gain1", [P, DT, 2])
        gain2 = sb("gain2", [P, DT, 2])
        half_gt1 = sb("half_gt1", [P, DT, 2])
        half_gt2 = sb("half_gt2", [P, DT, 2])
        lora = sb("lora", [P, 3, RH * 64])
        router_w = sb("router_w", [P, DT, 20])
        router_b = sb("router_b", [P, 20])
        row = sb("row", [1, 2, 604])
        rs_in = sb("rs_in", [P, 20])
        rs = sb("rs", [P, 20])
        minus_half = sb("minus_half", [P, 20])
        rb = sb("rb", [P, TT, 2, P])
        half_w0a0 = sb("half_w0a0", [P, 4])
        keep = sb("keep", [P, 2, DT])
        with nc.sbuf_tensor("s_arena", [P, ARENA], F32) as arena:
            pass
        sb("arena_low", [P, 13056])
        x_hi, x_lo = (ctx.enter_context(nc.sbuf_tensor(n, [P, DT, T], FAST)) for n in ("s_x_hi", "s_x_lo"))
        w_hi, w_lo = (ctx.enter_context(nc.sbuf_tensor(n, [P, 2, DT, P], FAST)) for n in ("s_w_hi", "s_w_lo"))
        sb("arena_high", [P, ARENA - 13056 - 2 * DT * T - 4 * UW])

        def a_(off, *shape):
            n = int(np.prod(shape))
            v = arena[:, off:off + n]
            if len(shape) == 1:
                return v
            names = "abcd"[:len(shape)]
            return v.rearrange(f"p ({' '.join(names)}) -> p {' '.join(names)}",
                               **{k: s for k, s in zip(names, shape)})

        def c_(name):
            o, n = CONST[name]
            return cst[:, o:o + n]

        def p_(name, i=None):
            o, n = PARAM[name]
            return prm[:, o:o + n] if i is None else prm[:, o + i:o + i + 1]

        ident, ones, blk = c_("ident"), c_("ones"), c_("blk")
        cos, sin = c_("cos"), c_("sin")

        cT = a_(0, 2, T)
        yT = a_(1088, 2, T)
        oT = a_(2176, 4, T)
        mod_row = a_(4352, 2 * DM)
        CBW = 2 * (CW - 1) + T
        CYW = CBW - (CW - 1)
        cb = a_(4352, 2, CBW)
        cy = a_(5568, 2, CYW)
        cth = a_(12752, 2, T)
        csq = a_(14928, 2, CYW)
        ad_row, ad_row2 = a_(26960, 12 * P), a_(16512, 4 * P)
        xs = a_(2176, 8, PADT)
        pr = a_(7296, 8, T + 2)
        logw = a_(11664, 2, T)
        aa = a_(12752, 2, T)
        kk = a_(13840, 2, T)
        cum = a_(14928, 2, T)
        rtmp = a_(16016, 2, T)
        gg = a_(17104, 2, T)
        bonus = a_(18192, 2, T)
        bf = a_(19280, 2, PADT)
        kf = a_(20560, 2, PADT)
        ar = a_(21840, 2, 4, PADT)
        et = a_(26960, TT, 2, 2 * P)
        zp = a_(2176, TT, 4, P)
        yv = a_(2176 + 6 * PADT, TT, RH * 64)
        vtok = a_(7296, 2 * P)
        btm = a_(7552, 2, 2 * P)
        ktm = a_(8064, 2, 2 * P)
        wr = a_(8576, 4, P)
        gb = a_(9088, 2, 4, P)
        gk = a_(10112, 2, 4, P)
        xx = a_(11136, 4, P)
        xt = a_(11648, 4, P)
        tm = a_(12160, 4, P)
        mo = a_(12672, 4, P)
        wn = a_(13184, 2, 4, 64)
        st = a_(13696, 11, 2, P)
        ytok = a_(7296, TT, RH, 64)
        ysq = a_(8576, TT, RH, 64)
        pexp, pneg, pm = a_(7296, 2, T), a_(8384, 2, T), a_(9472, 2, T)
        pmT = a_(4352, 5, T)
        latT = a_(7072, 2, TP + PAST + TS)
        msq = a_(8672, 5, T)
        vv = a_(8672, 7, HEADS * VH)
        krt, krr = a_(12256, T), a_(12800, T)
        krc = a_(13344, PAST)
        qup = a_(13888, 3, HEADS * QK)
        QT = a_(16192, HEADS, T)
        KT = a_(20544, HEADS, TP)
        KTs = a_(24640, HEADS, PAST + TS)
        sin_q = [a_(26944, 4, T), a_(13888, 4, T)]
        prob = [a_(26944, 4, TP), a_(4352, 4, TP)]
        probT = [a_(13888, 4, 4, P), a_(6400, 4, 4, P)]
        diag = [a_(12256 + 512 * i, 4, P) for i in range(2)]
        mx = sb("mx", [P, 2, 4, 4])
        mg = a_(4352, DT, T)
        th = [a_(8704 + 1632 * i, 3, T) for i in range(2)]
        mtmp = [a_(11968 + 544 * i, T) for i in range(2)]
        gu_w = [a_(13056 + 6144 * i, DT, 2 * FE) for i in range(2)]
        dn_w = [a_(13056 + 6144 * i + 4096, 2, DM) for i in range(2)]
        eact = a_(25344, 3, 2, T)
        eth = [a_(28608 + HALF * i, HALF) for i in range(3)]
        yacc = a_(8704, DT, T)
        lg = a_(0, TT, 20)
        ra = a_(100, 4, TT, 4)
        rm = a_(180, 8, TT)
        cmb = a_(220, TT, 4, 4)
        grp = a_(300, TT, 4, 4)
        cmbT = a_(400, T)
        sel = sb("sel", [P, 2, TT, 4, 4])
        pos = sb("pos", [P, TT, NE])
        both = ctx.enter_context(nc.sbuf_tensor("s_both", [P, TT, NE], BF16))
        slot = sb("slot", [P, 2, TT])
        slot_i = ctx.enter_context(nc.sbuf_tensor("s_slot_i", [P, 2, TT], mybir.dt.uint32))
        most = sb("most", [P, 1])
        fits = ctx.enter_context(nc.sbuf_tensor("s_fits", [1, 1], mybir.dt.int32))
        both_f = sb("filler", [P, TT, NE])
        before = ctx.enter_context(nc.sbuf_tensor("s_before", [P, P], BF16))
        ones_b = ctx.enter_context(nc.sbuf_tensor("s_ones_b", [P, P], BF16))
        htok = a_(7936, TT, DM)
        pout = [a_(1024 + DM * i, DM) for i in range(2)]
        pth = [a_(3072 + FE * i, FE) for i in range(2)]
        pact = [a_(3584 + FE * i, FE) for i in range(2)]
        pactT = [a_(4096 + FE * i, 2, P) for i in range(2)]
        xe = [a_(25344 + DM * i, DM) for i in range(2)]
        xeT = [a_(27392 + DM * i, DT, P) for i in range(2)]
        yg = [a_(13056 + TT * DM * i, TT, DM) for i in range(2)]
        zeros = a_(21840, DM)
        pend = sb("pend", [P, TT, 2, 2])
        shift_in = sb("shift_in", [P, DT])

        s_const = sem("const_loaded")
        s_prm = sem("params_loaded")
        s_lora = sem("lora_loaded")
        s_wkv = sem("wkv_loaded")
        ring_full = [sem(f"ring_full{i}") for i in range(RING)]
        unit_done = sem("unit_done")
        s_c = sem("silu_c_ready")
        dch, pch = sem("dve_chain"), sem("pool_chain")
        ada_row = sem("ada_row")
        s_zero, zeros_set = sem("slots_zeroed"), sem("zeros_set")
        ada_tp = sem("ada_transposed")
        mod_ready = sem("mod_ready")
        nm = {k: {s: sem(f"norm_{k}_{s}") for s in ("sq", "row", "srow", "col", "ms", "rs", "rb", "bc", "g", "out")[lo:hi]}
              for k, lo, hi in (("n1", 0, 10), ("cv", 0, 8))}
        cv_th, cv_glu, cv_init, cv_state = sem("cv_th"), sem("cv_glu"), sem("cv_init"), sem("cv_state")
        cv_y, cv_mu, cv_cent, cv_zh, cv_t2, cv_out = (sem(f"cv_{s}") for s in ("y", "mu", "cent", "zh", "t2", "out"))
        rw_pr, rw_init, rw_shift, rw_xs, rw_act, rw_lora, rw_wag, rw_fin = (
            sem(f"rw_{s}") for s in ("pr", "init", "shift", "xs", "act", "lora", "wag", "fin"))

        def norm_pe_tail(pe, s, r=0):
            pe.wait_ge(s["rb"], r + 1)
            for i in range(4):
                nc.tensor.transpose(PS[:, 3, i * P:(i + 1) * P], rb[:, i, 0, :], ident)
            nc.tensor.transpose(PS[:, 4, 0:TS], rb[0:TS, 4, 0, :], ident[0:TS, 0:TS]).then_inc(s["bc"], 1)

        def norm_cols_pe(pe, s, sample_at, r=0):
            pe.wait_ge(s["srow"], 2 * r + 2)
            for i in range(4):
                nc.tensor.matmul(PS[:, 2, i:i + 1], row[0:1, 0, i * P:(i + 1) * P], ones[0:1, 0:1],
                                 start=True, stop=True)
            nc.tensor.matmul(PS[0:TS, 2, 4:5], row[0:1, 0, sample_at:sample_at + TS], ones[0:1, 0:1],
                             start=True, stop=True).then_inc(s["col"], 1)

        def norm_cols_dve(dve, s, n, eps, r=0):
            dve.wait_ge(s["col"], r + 1)
            nc.vector.tensor_scalar(rs_in[:, 0:4], PS[:, 2, 0:4], 1.0 / n, eps, ALU.mult, ALU.add).then_inc(s["ms"], 1)
            nc.vector.tensor_scalar(rs_in[0:TS, 4:5], PS[0:TS, 2, 4:5], 1.0 / n, eps, ALU.mult, ALU.add)\
                .then_inc(s["ms"], 1)
            dve.wait_ge(s["rs"], r + 1)
            nc.vector.tensor_copy(rb[:, :, 0, :], rs[:, 0:TT].unsqueeze(2).to_broadcast([P, TT, P]))\
                .then_inc(s["rb"], 1)

        def norm_pow(pool, s, n=TT, r=0):
            pool.wait_ge(s["ms"], 2 * r + 2)
            nc.gpsimd.tensor_tensor(rs[:, 0:n], rs_in[:, 0:n], minus_half[:, 0:n], ALU.pow).then_inc(s["rs"], 1)

        def norm_x_act(act, s):
            for k in range(DT):
                nc.scalar.activation(hT[:, k, :], xT[:, k, :], ACT.Square).then_inc(s["sq"], 1)

        def norm_x_pe(pe, s, r=0):
            for k in range(DT):
                pe.wait_ge(s["sq"], DT * r + k + 1)
                for h in range(2):
                    ins = nc.tensor.matmul(PS[0:1, h, 0:HALF], ones[:, 0:1], hT[:, k, h * HALF:(h + 1) * HALF],
                                           start=(k == 0), stop=(k == DT - 1))
            ins.then_inc(s["row"], 1)
            norm_cols_pe(pe, s, TP, r)
            norm_pe_tail(pe, s, r)

        def norm_x_dve(dve, s, gain, r=0):
            dve.wait_ge(s["row"], r + 1)
            for h in range(2):
                nc.vector.tensor_copy(row[0:1, 0, h * HALF:(h + 1) * HALF], PS[0:1, h, 0:HALF]).then_inc(s["srow"], 1)
            norm_cols_dve(dve, s, DM, 1e-6, r)
            dve.wait_ge(s["bc"], r + 1)
            for k in range(DT):
                nc.vector.scalar_tensor_tensor(hT[:, k, 0:TP], xT[:, k, 0:TP], gain(k, 0), PS[:, 3, :],
                                               ALU.mult, ALU.mult).then_inc(s["g"], 1)
                nc.vector.scalar_tensor_tensor(hT[:, k, TP:T], xT[:, k, TP:T], gain(k, 1), PS[:, 4, 0:TS],
                                               ALU.mult, ALU.mult).then_inc(s["g"], 1)

        def norm_shift_act(act, s, chunk, r=0):
            for k in range(DT):
                act.wait_ge(s["g"], 2 * DT * r + 2 * k + 2)
                nc.scalar.activation(hT[:, k, 0:TP], hT[:, k, 0:TP], ACT.Identity,
                                     bias=mod[:, chunk * DT + k, 0:1]).then_inc(s["out"], 1)
                nc.scalar.activation(hT[:, k, TP:T], hT[:, k, TP:T], ACT.Identity,
                                     bias=mod[:, chunk * DT + k, 1:2]).then_inc(s["out"], 1)

        def unit_wait(pe, n):
            pe.wait_ge(ring_full[n % RING], 16 * (n // RING + 1))
            return ring[:, n % RING, :].rearrange("p (k m) -> p k m", k=DT)

        def unit_mm(pe, n, pair, rows=P):
            w = unit_wait(pe, n)
            if rows < P:
                w = ring[:, n % RING, 0:DT * rows].rearrange("p (k m) -> p k m", k=DT)
            for k in range(DT):
                for h in range(2):
                    ins = nc.tensor.matmul(PS[0:rows, 2 * pair + h, 0:HALF], w[:, k, :],
                                           hT[:, k, h * HALF:(h + 1) * HALF], start=(k == 0), stop=(k == DT - 1))
            ins.then_inc(unit_done, 1)

        def ada_unit(n, bank, col):
            w = unit_wait(nc.tensor, n)
            for k in range(DT):
                ins = nc.tensor.matmul(PS[0:2, bank, col:col + P], silu_c[:, k, :], w[:, k, :],
                                       start=(k == 0), stop=(k == DT - 1))
            ins.then_inc(unit_done, 1)

        def mod_part(j, n, bank):
            o = PARAM["ada_b"][0] + j
            nc.vector.tensor_tensor(mod[:, j:j + n, :], PS[:, bank, 0:2 * n].rearrange("p (n g) -> p n g", g=2),
                                    prm[:, o:o + n].unsqueeze(2).to_broadcast([P, n, 2]), ALU.add)\
                .then_inc(mod_ready, 1)

        lay = [None]
        L_ = lambda name: lay[0](name)

        names = ("act", "gl", "sq", "n2", "cumd", "exp", "der", "bon", "bon_mm", "tp", "tpe", "gram", "gm", "x0",
                 "mo", "t", "te", "x", "xe", "nv", "nve", "wu", "wue", "lin", "line", "st_init", "st_mm", "st",
                 "y_mm", "y", "ytp", "out", "clr")
        q = {n: sem(f"q_{n}") for n in names}
        cv_done = sem("cv_done")

        def by4(v):
            return v.unsqueeze(1).to_broadcast([P, 4, P])

        def bank4(b):
            return PS[:, b, :].rearrange("p (h n) -> p h n", h=4)

        def rwkv_in_pe(pe):
            for i in range(8):
                if i < 2:
                    pe.wait_ge(cv_th, 2 * i + 2)
                elif i < 4:
                    pe.wait_ge(cv_glu, 3 * (i - 1))
                else:
                    pe.wait_ge(rw_pr, 3 * (i - 3))
                unit_mm(pe, U_RW + i, i % 4)

        def rwkv_in_act(act):
            for i in range(8):
                act.wait_ge(unit_done, U_RW + i + 1)
                b = 2 * (i % 4)
                nc.scalar.copy(pr[:, i, 1:1 + HALF], PS[:, b, 0:HALF]).then_inc(rw_pr, 1)
                nc.scalar.copy(pr[:, i, 1 + HALF:1 + TP], PS[:, b + 1, 0:TP - HALF]).then_inc(rw_pr, 1)
                nc.scalar.copy(pr[:, i, 2 + TP:2 + T], PS[:, b + 1, TP - HALF:HALF]).then_inc(rw_pr, 1)

        def rwkv_pe(pe):
            for g in range(3):
                if g == 2:
                    pe.wait_ge(ada_row, 5)
                for j in range(4):
                    ada_unit(U_AD2 + 4 * g + j, 5 + g % 2, j * P)
            pe.wait_ge(ada_row, 7)
            for j in range(12):
                ins = nc.tensor.transpose(PS[:, 7, 2 * j:2 * j + 2], ad_row[0:2, j * P:(j + 1) * P], ident[0:2, 0:2])
            ins.then_inc(ada_tp, 1)
            pe.wait_ge(cv_done, 1)
            pe.wait_ge(mod_ready, 2)
            pe.wait_ge(rw_pr, 24)
            pe.wait_ge(s_lora, 64)
            pe.wait_ge(q["act"], 1)
            for j in range(4):
                for h in range(2):
                    ins = nc.tensor.matmul(PS[:, 2 * j + h, 0:HALF], lora[:, j // 2, (j % 2) * P:(j % 2 + 1) * P],
                                           xs[:, 6, h * HALF:(h + 1) * HALF], start=True, stop=True)
                ins.then_inc(rw_lora, 1)
            pe.wait_ge(q["gl"], 1)
            pe.wait_ge(rw_wag, 4)
            for j in range(2):
                for h in range(2):
                    ins = nc.tensor.matmul(PS[:, 2 * j + h, 0:HALF], lora[:, 2, j * P:(j + 1) * P],
                                           xs[:, 7, h * HALF:(h + 1) * HALF], start=True, stop=True)
                ins.then_inc(rw_lora, 1)
            pe.wait_ge(q["sq"], 1)
            pe.wait_ge(rw_wag, 12)
            for t in range(2):
                for i in range(TT):
                    m = P if i < 4 else TS
                    ins = nc.tensor.matmul(PS[0:m, 2, 4 * i + 2 * t:4 * i + 2 * t + 2], rtmp[:, t, i * P:i * P + m],
                                           blk[:, 0:P:64], start=True, stop=True)
            ins.then_inc(q["n2"], 1)
            turn_rb(pe, nm["cv"], lambda i, t: rb[:, i, t, :], r=1)
            pe.wait_ge(q["bon"], 2)
            for t in range(2):
                for h in range(2):
                    ins = nc.tensor.matmul(PS[:, (0, 1, 2, 7)[2 * t + h], 0:HALF], blk,
                                           bonus[:, t, h * HALF:(h + 1) * HALF], start=True, stop=True)
            ins.then_inc(q["bon_mm"], 1)
            pe.wait_ge(q["der"], 8)
            for p in range(TT):
                co = slice(p * P, (p + 1) * P)
                if p:
                    pe.wait_ge(q["wue"], p)
                for t in range(2):
                    nc.tensor.transpose(PS[:, 0, t * P:(t + 1) * P], xs[:, 4 + t, co], ident)
                    nc.tensor.transpose(PS[:, 0, (2 + t) * P:(3 + t) * P], bf[:, t, co], ident)
                    nc.tensor.transpose(PS[:, 1, t * P:(t + 1) * P], kf[:, t, co], ident)
                    for e in range(2):
                        ins = nc.tensor.matmul(PS[:, 1, (2 + t) * P:(3 + t) * P], ar[:, t, e, co], ident,
                                               start=(e == 0), stop=(e == 1))
                ins.then_inc(q["tp"], 1)
                if p:
                    pe.wait_ge(q["line"], 5 * p)
                for o, src in ((2, bf), (4, kf)):
                    for t in range(2):
                        nc.tensor.matmul(PS[:, o + t, :].rearrange("p (k n) -> p k n", k=4), src[:, t, co],
                                         ar[:, t, :, co], start=True, stop=True).then_inc(q["gram"], 1)
                for h in range(4):
                    ins = nc.tensor.matmul(PS[:, 6, h * P:(h + 1) * P], ar[:, h // 2, h % 2, co], bf[:, h // 2, co],
                                           start=True, stop=True)
                ins.then_inc(q["gram"], 1)
                for lv in range(5):
                    n = 5 * p + lv
                    pe.wait_ge(q["mo"], n + 1)
                    pe.wait_ge(q["x0"], 2 * (p + 1))
                    if lv:
                        pe.wait_ge(q["xe"], 9 * p + 2 * lv - 1)
                    for h in range(4):
                        ins = nc.tensor.matmul(PS[:, 7, h * P:(h + 1) * P], mo[:, h, :], xx[:, h, :],
                                               start=True, stop=True)
                    ins.then_inc(q["t"], 1)
                    if lv < 4:
                        if lv == 0:
                            pe.wait_ge(q["tpe"], 6 * p + 3)
                        ada_unit(U_AD3 + 4 * p + lv, 0, lv * P)
                    pe.wait_ge(q["te"], n + 1)
                    if lv:
                        pe.wait_ge(q["xe"], 9 * p + 2 * lv)
                    if lv < 4:
                        for h in range(4):
                            ins = nc.tensor.matmul(PS[:, 6, h * P:(h + 1) * P], xt[:, h, :], tm[:, h, :],
                                                   start=True, stop=True)
                        ins.then_inc(q["x"], 1)
                    for h in range(4):
                        ins = nc.tensor.matmul(PS[:, 5, h * P:(h + 1) * P], tm[:, h, :], xt[:, h, :],
                                               start=True, stop=True)
                    ins.then_inc(q["x"], 1)
                pe.wait_ge(q["tpe"], 6 * (p + 1))
                pe.wait_ge(ada_row, 8 + p)
                for j in range(4):
                    ins = nc.tensor.transpose(PS[:, 1, 2 * j:2 * j + 2], ad_row2[0:2, j * P:(j + 1) * P],
                                              ident[0:2, 0:2])
                ins.then_inc(ada_tp, 1)
                for h in range(4):
                    ins = nc.tensor.matmul(PS[:, 0, h * 64:(h + 1) * 64], gk[:, 0, h, :], vtok[:, h * 64:(h + 1) * 64],
                                           start=True, stop=True)
                ins.then_inc(q["nv"], 1)
                pe.wait_ge(q["nve"], p + 1)
                pe.wait_ge(q["xe"], 9 * (p + 1))
                pe.wait_ge(mod_ready, 3 + p)
                for h in range(4):
                    ins = nc.tensor.matmul(PS[:, 1, h * P:(h + 1) * P], xt[:, h, :], wr[:, h, :],
                                           start=True, stop=True)
                ins.then_inc(q["wu"], 1)
                pe.wait_ge(q["wue"], p + 1)
                for t in range(2):
                    ins = nc.tensor.matmul(PS[:, 2, t * 256:(t + 1) * 256].rearrange("p (a n) -> p a n", a=2),
                                           wn[:, 0, 2 * t:2 * t + 2, :].rearrange("p h n -> p (h n)"),
                                           btm[:, :, t * P:(t + 1) * P],
                                           start=True, stop=True)
                ins.then_inc(q["lin"], 1)
                for t in range(2):
                    for e in range(2):
                        o = PS[:, 3, (2 * t + e) * P:(2 * t + e + 1) * P]
                        nc.tensor.matmul(o, btm[:, e, t * P:(t + 1) * P],
                                         wn[:, 1, 2 * t:2 * t + 2, :].rearrange("p h n -> p (h n)"),
                                         start=True, stop=False)
                        ins = nc.tensor.matmul(o, ktm[:, e, t * P:(t + 1) * P], vtok[:, t * P:(t + 1) * P],
                                               start=False, stop=True)
                ins.then_inc(q["lin"], 1)
                for h in range(4):
                    e = h % 2
                    ins = nc.tensor.matmul(PS[64 * e:64 * e + 64, 4, (h // 2) * P:(h // 2 + 1) * P], wn[:, 0, h, :],
                                           gb[:, 1, h, :], start=True, stop=True)
                ins.then_inc(q["lin"], 1)
                for h in range(4):
                    nc.tensor.matmul(PS[:, 5, h * 64:(h + 1) * 64], gb[:, 1, h, :], wn[:, 1, h, :],
                                     start=True, stop=False)
                    ins = nc.tensor.matmul(PS[:, 5, h * 64:(h + 1) * 64], gk[:, 1, h, :],
                                           vtok[:, h * 64:(h + 1) * 64], start=False, stop=True)
                ins.then_inc(q["lin"], 1)
            pe.wait_ge(q["st_init"], 1)
            pe.wait_ge(s_wkv, 64)
            pe.wait_ge(q["line"], 5 * TT)
            for c in range(9):
                if c and c < 8:
                    pe.wait_ge(q["st"], 2 * c)
                for t in range(2):
                    ins = nc.tensor.matmul(PS[:, 6 + c % 2, t * P:(t + 1) * P], et[:, c // 2, t, (c % 2) * P:(c % 2 + 1) * P],
                                           st[:, c if c < 8 else 9, t, :], start=True, stop=True)
                ins.then_inc(q["st_mm"], 1)
            pe.wait_ge(q["st"], 14)
            for c in range(9):
                p, e = c // 2, c % 2
                for t in range(2):
                    for r in range(2):
                        ins = nc.tensor.matmul(PS[64 * e:64 * e + 64, p, t * P:(t + 1) * P],
                                               ar[:, t, 2 + r, c * 64:(c + 1) * 64], st[:, c if c < 8 else 9, t, :],
                                               start=(r == 0), stop=(r == 1))
                ins.then_inc(q["y_mm"], 1)
            pe.wait_ge(q["st"], 18)
            unit_mm(pe, U_MLA, 3)
            pe.wait_ge(q["y"], 2)
            unit_mm(pe, U_MLA + 1, 0)
            turn_rb(pe, None, lambda i, t: ytok[:, i, 2 * t:2 * t + 2, :].rearrange("p h n -> p (h n)"),
                    (q["y"], TT + 1), q["ytp"])

        def turn_rb(pe, s, src, wait=None, done=None, r=0):
            if s is not None:
                wait, done = (s["rb"], r + 1), s["bc"]
            pe.wait_ge(*wait)
            for t in range(2):
                for i in range(4):
                    nc.tensor.transpose(PS[:, 3 + 2 * t, i * P:(i + 1) * P], src(i, t), ident)
                ins = nc.tensor.transpose(PS[:, 4, TS * t:TS * (t + 1)], src(4, t)[0:TS], ident[0:TS, 0:TS])
            ins.then_inc(done, 1)

        def rwkv_act(act):
            act.wait_ge(cv_done, 1)
            for g in range(3):
                act.wait_ge(unit_done, U_AD2 + 4 * g + 4)
                nc.scalar.copy(ad_row[0:2, 512 * g:512 * g + 512], PS[0:2, 5 + g % 2, :]).then_inc(ada_row, 1)
            act.wait_ge(rw_shift, 2)
            act.dma_start(L_("out_shift").rearrange("l p g n -> p (l g) n"), keep[:, :, :]).then_inc(rw_fin, 16)
            act.wait_ge(rw_xs, 14)
            nc.scalar.activation(xs[0:64, 6, 0:T], xs[0:64, 6, 0:T], ACT.Tanh).then_inc(q["act"], 1)
            act.wait_ge(rw_xs, 16)
            nc.scalar.activation(xs[:, 7, 0:T], xs[:, 7, 0:T], ACT.Tanh, scale=0.5).then_inc(q["act"], 1)
            act.wait_ge(rw_init, 7)
            for j in range(4):
                act.wait_ge(rw_lora, j + 1)
                dst = (logw, aa)[j // 2]
                for h in range(2):
                    nc.scalar.activation(dst[:, j % 2, h * HALF:(h + 1) * HALF], PS[:, 2 * j + h, 0:HALF], ACT.Tanh,
                                         bias=half_w0a0[:, j:j + 1], scale=0.5).then_inc(rw_wag, 1)
            for j in range(2):
                act.wait_ge(rw_lora, 5 + j)
                for h in range(2):
                    nc.scalar.copy(gg[:, j, h * HALF:(h + 1) * HALF], PS[:, 2 * j + h, 0:HALF]).then_inc(rw_wag, 1)
            act.wait_ge(q["cumd"], 2)
            nc.scalar.activation(pexp[:, :, :], cum[:, :, :], ACT.Exp).then_inc(q["exp"], 1)
            nc.scalar.activation(pneg[:, :, :], cum[:, :, :], ACT.Exp, scale=-1.0).then_inc(q["exp"], 1)
            act.wait_ge(q["cumd"], 3)
            nc.scalar.activation(pm[:, :, :], logw[:, :, :], ACT.Exp).then_inc(q["exp"], 1)
            act.wait_ge(q["clr"], 1)
            for h in range(4):
                e = h % 2
                act.dma_start(st[64 * e:64 * e + 64, 9, h // 2, 64 * e:64 * e + 64],
                              L_("wkv")[:, h].rearrange("l j i -> (l j) i")).then_inc(s_wkv, 16)
            for p in range(TT):
                act.wait_ge(q["tp"], p + 1)
                nc.scalar.copy(vtok[:, :], PS[:, 0, 0:256]).then_inc(q["tpe"], 1)
                for dst, b, o in ((btm, 0, 256), (ktm, 1, 0)):
                    for e in range(2):
                        nc.scalar.copy(dst[64 * e:64 * e + 64, e, :], PS[64 * e:64 * e + 64, b, o:o + 256])\
                            .then_inc(q["tpe"], 1)
                nc.scalar.copy(wr[:, :, 0:64], PS[:, 1, 256:512].rearrange("p (h n) -> p h n", h=4))\
                    .then_inc(q["tpe"], 1)
                for lv in range(5):
                    act.wait_ge(q["t"], 5 * p + lv + 1)
                    nc.scalar.copy(tm[:, :, :], bank4(7)).then_inc(q["te"], 1)
                    if lv == 3:
                        act.wait_ge(unit_done, U_AD3 + 4 * p + 4)
                        if p:
                            act.wait_ge(ada_tp, 2 + p)
                        nc.scalar.copy(ad_row2[0:2, :], PS[0:2, 0, :]).then_inc(ada_row, 1)
                act.wait_ge(q["nv"], p + 1)
                nc.scalar.copy(wr[:, :, 64:128], PS[:, 0, 0:256].rearrange("p (h n) -> p h n", h=4))\
                    .then_inc(q["nve"], 1)
                act.wait_ge(q["wu"], p + 1)
                nc.scalar.activation(wn[:, :, :, :].rearrange("p a h n -> p h a n"),
                                     PS[:, 1, :].rearrange("p (h a n) -> p h a n", h=4, a=2), ACT.Copy,
                                     scale=-1.0).then_inc(q["wue"], 1)
                act.wait_ge(q["lin"], 4 * p + 4)
                nc.scalar.copy(yv[:, p, :], PS[:, 5, 0:256]).then_inc(q["line"], 1)
            act.wait_ge(q["st"], 18)
            for g, c in ((0, 8), (1, 10)):
                for h in range(4):
                    e = h % 2
                    act.dma_start(L_("out_wkv")[:, g, h].rearrange("l j i -> (l j) i"),
                                  st[64 * e:64 * e + 64, c, h // 2, 64 * e:64 * e + 64]).then_inc(rw_fin, 16)
            act.wait_ge(rw_fin, 16 * 9)

        def rwkv_pool(pool):
            pool.wait_ge(cv_done, 1)
            pool.wait_ge(cv_out, 32)
            pool.wait_ge(s_lora, 64)
            nc.gpsimd.memset(pr[:, :, 0:1], 0.0).then_inc(rw_init, 1)
            nc.gpsimd.tensor_copy(pr[:, :, TP + 1:TP + 2], shift_in[:, :].unsqueeze(2)).then_inc(rw_init, 1)
            nc.gpsimd.memset(xs[:, :, T:PADT], 0.0).then_inc(rw_init, 1)
            nc.gpsimd.memset(bf[:, :, T:PADT], 0.0).then_inc(rw_init, 1)
            nc.gpsimd.memset(kf[:, :, T:PADT], 0.0).then_inc(rw_init, 1)
            pool.wait_ge(s_zero, 16 * NE)
            nc.gpsimd.memset(ar[:, :, :, :], 0.0).then_inc(rw_init, 1)
            nc.gpsimd.tensor_scalar(half_w0a0[:, :], prm[:, PARAM["w0"][0]:PARAM["w0"][0] + 4], 0.5, None, ALU.mult)\
                .then_inc(rw_init, 1)
            pool.wait_ge(rw_pr, 24)
            nc.gpsimd.tensor_copy(keep[:, 0, :], pr[:, :, TP:TP + 1].squeeze(2)).then_inc(rw_shift, 1)
            nc.gpsimd.tensor_copy(keep[:, 1, :], pr[:, :, T + 1:T + 2].squeeze(2)).then_inc(rw_shift, 1)
            norm_pow(pool, nm["cv"], 4 * TT, 1)
            pool.wait_ge(q["der"], 8)
            nc.gpsimd.memset(btm[:, :, :], 0.0).then_inc(pch, 1)
            nc.gpsimd.memset(ktm[:, :, :], 0.0).then_inc(pch, 1)
            nc.gpsimd.memset(st[:, 0, :, :], 0.0).then_inc(pch, 1)
            pool.wait_ge(pch, 3)
            nc.gpsimd.memset(st[:, 9, :, :], 0.0).then_inc(q["clr"], 1)
            pool.wait_ge(q["line"], 5 * TT)
            nc.gpsimd.memset(ytok[64:128, 4, :, :], 0.0).then_inc(q["st_init"], 1)
            norm_pow(pool, nm["cv"], 4 * TT, 2)

        def rwkv_dve(dve, ch):
            dve.wait_ge(rw_init, 3)
            dve.wait_ge(cv_out, 32)
            for i in range(8):
                dve.wait_ge(rw_pr, 3 * (i + 1))
                tmp = a_((11664, 12752)[i % 2], T + 1)
                if i >= 2:
                    dve.wait_ge(rw_xs, 2 * (i - 1))
                ch.link(nc.vector.tensor_tensor(tmp, pr[:, i, 0:T + 1], pr[:, i, 1:T + 2], ALU.subtract))
                nc.vector.scalar_tensor_tensor(xs[:, i, 0:TP], tmp[:, 0:TP], p_("mu", i), pr[:, i, 1:TP + 1],
                                               ALU.mult, ALU.add).then_inc(rw_xs, 1)
                nc.vector.scalar_tensor_tensor(xs[:, i, TP:T], tmp[:, TP + 1:T + 1], p_("mu", i),
                                               pr[:, i, TP + 2:T + 2], ALU.mult, ALU.add).then_inc(rw_xs, 1)
            dve.wait_ge(ada_tp, 2)
            mod_part(16, 12, 7)
            dve.wait_ge(rw_xs, 16)
            for t in range(2):
                ch.mark(nc.vector.tensor_scalar(kk[:, t, :], xs[:, 2 + t, 0:T], p_("k_k", t), None, ALU.mult))
            dve.wait_ge(q["act"], 2)
            nc.vector.tensor_scalar(xs[:, 7, 0:T], xs[:, 7, 0:T], 0.5, 0.5, ALU.mult, ALU.add).then_inc(q["gl"], 1)
            ch.wait(ch.n)
            nc.vector.tensor_tensor(rtmp[:, :, :], kk[:, :, :], kk[:, :, :], ALU.mult).then_inc(q["sq"], 1)
            dve.wait_ge(rw_wag, 4)
            ch.link(nc.vector.tensor_scalar(logw[:, :, :], logw[:, :, :], -0.5 * DECAY, -0.5 * DECAY,
                                            ALU.mult, ALU.add))
            for t in range(2):
                nc.vector.tensor_tensor_scan(cum[:, t, :], c_("scan"), logw[:, t, :], 0.0, ALU.mult, ALU.add)\
                    .then_inc(q["cumd"], 1)
            dve.wait_ge(q["cumd"], 2)
            nc.vector.tensor_tensor(logw[:, :, :], cum[:, :, :], logw[:, :, :], ALU.subtract).then_inc(q["cumd"], 1)
            dve.wait_ge(rw_wag, 8)
            ch.link(nc.vector.tensor_scalar(aa[:, :, :], aa[:, :, :], 0.5, 0.5, ALU.mult, ALU.add))
            s = nm["cv"]
            dve.wait_ge(q["n2"], 1)
            nc.vector.tensor_scalar(rs_in[:, 0:16], PS[:, 2, 0:16], 1e-12, None, ALU.add).then_inc(s["ms"], 1)
            nc.vector.tensor_scalar(rs_in[0:TS, 16:20], PS[0:TS, 2, 16:20], 1e-12, None, ALU.add)\
                .then_inc(s["ms"], 1)
            for t in range(2):
                ch.link(nc.vector.tensor_scalar(rtmp[:, t, :], aa[:, t, :], 1.0, p_("k_a", t),
                                                ALU.subtract, ALU.mult))
                ch.link(nc.vector.scalar_tensor_tensor(rtmp[:, t, :], rtmp[:, t, :], 1.0, xs[:, 2 + t, 0:T],
                                                       ALU.add, ALU.mult))
                nc.vector.scalar_tensor_tensor(bonus[:, t, :], xs[:, t, 0:T], p_("r_k", t), rtmp[:, t, :],
                                               ALU.mult, ALU.mult).then_inc(q["bon"], 1)
            dve.wait_ge(s["rs"], 2)
            nc.vector.tensor_copy(rb[:, :, :, :].rearrange("p i t (h n) -> p (i t h) n", h=2),
                                  rs[:, 0:20].unsqueeze(2).to_broadcast([P, 20, 64])).then_inc(s["rb"], 1)
            dve.wait_ge(q["exp"], 3)
            dve.wait_ge(rw_init, 7)
            dve.wait_ge(q["bon"], 2)
            nc.vector.tensor_tensor(kf[:, :, 0:T], rtmp[:, :, :], pneg[:, :, :], ALU.mult).then_inc(q["der"], 1)
            for e in range(2):
                r = slice(64 * e, 64 * e + 64)
                nc.vector.tensor_tensor(ar[r, :, 2 + e, 0:T], xs[r, 0:2, 0:T], pexp[r, :, :], ALU.mult)\
                    .then_inc(q["der"], 1)
            for t in range(2):
                ch.mark(nc.vector.tensor_copy(pend[:, 0:4, t, :], pexp[:, t, 63:TP:64]
                                              .rearrange("p (a b) -> p a b", b=2)))
            ch.mark(nc.vector.tensor_copy(pend[:, 4, :, 0:1], pexp[:, :, T - 1:T]))
            ch.mark(nc.vector.tensor_copy(pend[:, 4, :, 1:2], pexp[:, :, T - 1:T]))
            dve.wait_ge(s["bc"], 2)
            for t in range(2):
                ch.mark(nc.vector.tensor_tensor(kk[:, t, 0:TP], kk[:, t, 0:TP], PS[:, 3 + 2 * t, :], ALU.mult))
                ch.link(nc.vector.tensor_tensor(kk[:, t, TP:T], kk[:, t, TP:T], PS[:, 4, TS * t:TS * t + TS],
                                                ALU.mult))
            ch.link(nc.vector.tensor_tensor(aa[:, :, :], aa[:, :, :], kk[:, :, :], ALU.mult))
            nc.vector.tensor_tensor(bf[:, :, 0:T], aa[:, :, :], pneg[:, :, :], ALU.mult).then_inc(q["der"], 1)
            for e in range(2):
                r = slice(64 * e, 64 * e + 64)
                nc.vector.tensor_tensor(ar[r, :, e, 0:T], kk[r, :, :], pm[r, :, :], ALU.mult).then_inc(q["der"], 1)
            dve.wait_ge(q["bon_mm"], 1)
            for t in range(2):
                for h in range(2):
                    ins = nc.vector.tensor_tensor(bonus[:, t, h * HALF:(h + 1) * HALF],
                                                  PS[:, (0, 1, 2, 7)[2 * t + h], 0:HALF],
                                                  xs[:, 4 + t, h * HALF:(h + 1) * HALF], ALU.mult)
                    ins.then_inc(q["der"], 1) if h else ch.mark(ins)
            ch.wait(ch.n)
            dve.wait_ge(q["der"], 8)
            for p in range(TT):
                co = slice(p * P, (p + 1) * P)
                for i in range(4):
                    dve.wait_ge(q["gram"], 5 * p + i + 1)
                    dst, t = (gb, gk)[i // 2], i % 2
                    nc.vector.tensor_tensor(dst[:, :, 2 * t:2 * t + 2, :].rearrange("p k h n -> p k (h n)"),
                                            PS[:, 2 + i, :].rearrange("p (k n) -> p k n", k=2),
                                            c_("gram").rearrange("p (k n) -> p k n", k=2), ALU.mult)\
                        .then_inc(q["gm"], 1)
                dve.wait_ge(q["gram"], 5 * p + 5)
                dve.wait_ge(q["gm"], 4 * p + 4)
                ch.mark(nc.vector.scalar_tensor_tensor(xx[:, :, :], bank4(6), -1.0, by4(c_("first")),
                                                       ALU.mult, ALU.mult))
                ch.link(nc.vector.scalar_tensor_tensor(xt[:, :, :], gb[:, 0, :, :], -1.0, by4(c_("first_t")),
                                                       ALU.mult, ALU.mult))
                nc.vector.tensor_tensor(xx[:, :, :], xx[:, :, :], by4(ident), ALU.add).then_inc(q["x0"], 1)
                nc.vector.tensor_tensor(xt[:, :, :], xt[:, :, :], by4(ident), ALU.add).then_inc(q["x0"], 1)
                def level_mask(lv):
                    if 5 * p + lv:
                        dve.wait_ge(q["t"], 5 * p + lv)
                    nc.vector.tensor_tensor(mo[:, :, :], gb[:, 0, :, :], by4(c_("levels")[:, lv * P:(lv + 1) * P]),
                                            ALU.mult).then_inc(q["mo"], 1)
                level_mask(0)
                dve.wait_ge(q["x0"], 2 * p + 2)
                for lv in range(5):
                    n = 9 * p + 2 * lv
                    if lv < 4:
                        level_mask(lv + 1)
                        dve.wait_ge(q["x"], n + 1)
                        if lv:
                            dve.wait_ge(q["xe"], n - 1)
                        nc.vector.tensor_tensor(xx[:, :, :], xx[:, :, :], bank4(6), ALU.add).then_inc(q["xe"], 1)
                    dve.wait_ge(q["x"], n + 2 if lv < 4 else n + 1)
                    if lv:
                        dve.wait_ge(q["xe"], n)
                    nc.vector.tensor_tensor(xt[:, :, :], xt[:, :, :], bank4(5), ALU.add).then_inc(q["xe"], 1)
                dve.wait_ge(ada_tp, 3 + p)
                mod_part(28 + 4 * p, 4, 1)
                dve.wait_ge(q["lin"], 4 * p + 3)
                four = lambda v: v.rearrange("p (a n) -> p a n", n=P)
                e4 = et[:, p, :, :].rearrange("p t n -> p (t n)").rearrange("p (a n) -> p a n", n=P)
                ch.mark(nc.vector.tensor_tensor(e4, bank4(2), by4(blk), ALU.mult))
                ch.link(nc.vector.tensor_tensor(zp[:, p, :, :], bank4(3), by4(blk), ALU.mult))
                nc.vector.tensor_tensor(e4, e4, by4(ident), ALU.add).then_inc(q["line"], 1)
                nc.vector.tensor_tensor(zp[:, p, :, :], zp[:, p, :, :],
                                        pend[:, p, :, :].rearrange("p a b -> p (a b)").unsqueeze(2)
                                        .to_broadcast([P, 4, P]), ALU.mult).then_inc(q["line"], 1)
                for e in range(2):
                    r = slice(64 * e, 64 * e + 64)
                    ins = nc.vector.tensor_tensor(ar[r, :, 2 + e, co], ar[r, :, 2 + e, co],
                                                  PS[r, 4, 0:256].rearrange("p (t n) -> p t n", t=2), ALU.add)
                    ins.then_inc(q["line"], 1)
            dve.wait_ge(q["line"], 5 * TT)
            for c in range(9):
                dve.wait_ge(q["st_mm"], c + 1)
                p, e = c // 2, c % 2
                for t in range(2):
                    nc.vector.scalar_tensor_tensor(st[:, c + 1 if c < 8 else 10, t, :], PS[:, 6 + c % 2, t * P:(t + 1) * P],
                                                   pend[:, p, t, e:e + 1], zp[:, p, 2 * t + e, :],
                                                   ALU.mult, ALU.add).then_inc(q["st"], 1)
            dve.wait_ge(q["st_init"], 1)
            for p in range(TT):
                m = P if p < 4 else 64
                dve.wait_ge(q["y_mm"], min(2 * p + 2, 9))
                nc.vector.tensor_tensor(ytok[0:m, p, :, :].rearrange("p h n -> p (h n)"), PS[0:m, p, 0:256],
                                        yv[0:m, p, :], ALU.add).then_inc(q["y"], 1)
            dve.wait_ge(q["y"], TT)
            y20 = ytok[:, :, :, :].rearrange("p i h n -> p (i h) n")
            s20 = ysq[:, :, :, :].rearrange("p i h n -> p (i h) n")
            ch.link(nc.vector.tensor_reduce(rs_in[:, :], y20, AX_X, ALU.add))
            ch.link(nc.vector.tensor_scalar(rs[:, :], rs_in[:, :], -1.0 / 64, None, ALU.mult))
            ch.link(nc.vector.tensor_tensor(y20, y20, rs[:, :].unsqueeze(2).to_broadcast([P, 20, 64]), ALU.add))
            ch.link(nc.vector.tensor_tensor(s20, y20, y20, ALU.mult))
            ch.link(nc.vector.tensor_reduce(rs_in[:, :], s20, AX_X, ALU.add))
            nc.vector.tensor_scalar(rs_in[:, :], rs_in[:, :], 1.0 / 64, 64e-5, ALU.mult, ALU.add).then_inc(nm["cv"]["ms"], 2)
            dve.wait_ge(nm["cv"]["rs"], 3)
            nc.vector.tensor_tensor(y20, y20, rs[:, :].unsqueeze(2).to_broadcast([P, 20, 64]), ALU.mult)\
                .then_inc(q["y"], 1)
            dve.wait_ge(q["ytp"], 1)
            for t in range(2):
                ch.mark(nc.vector.tensor_scalar(yT[:, t, 0:TP], PS[:, 3 + 2 * t, :], p_("ln_g", t), p_("ln_b", t),
                                                ALU.mult, ALU.add))
                ch.mark(nc.vector.tensor_scalar(yT[:, t, TP:T], PS[:, 4, TS * t:TS * t + TS], p_("ln_g", t),
                                                p_("ln_b", t), ALU.mult, ALU.add))
            ch.wait(ch.n)
            ch.link(nc.vector.tensor_tensor(yT[:, :, :], yT[:, :, :], bonus[:, :, :], ALU.add))
            nc.vector.tensor_tensor(yT[:, :, :], yT[:, :, :], gg[:, :, :], ALU.mult).then_inc(q["out"], 1)

        at = {n: sem(f"at_{n}") for n in
              ("in", "lat_in", "pm", "sq", "kr", "row", "srow", "col", "ms", "rs", "rb", "bc", "krot", 
               "krr", "kb", "lat", "qn", "k_mm", "ka", "kd", "v_mm", "v", "q_mm", "rot", "sin", "cos",
               "q", "s", "mx", "exp", "dg", "t", "ta", "td", "o_mm", "o", "out", "init")}
        groups = [(b, g) for b in range(TT) for g in range(2)]
        extent = lambda b: (b + 1) * P if b < 4 else PAST + TS
        ktiles = [(i, k) for i, (b, g) in enumerate(groups) for k in range(-(-extent(b) // P))]
        first_tile = [next(n for n, x in enumerate(ktiles) if x[0] == i) for i in range(len(groups))] + [len(ktiles)]

        q_uses = [("up", h) for h in range(5)]
        for h in range(3):
            q_uses += [("rot", h), ("up", 5 + h)]
        q_uses += [("rot", h) for h in range(3, HEADS)]

        def q_bank(kind, h):
            u = h if kind == "" else q_uses.index((kind, h))
            return 2 * ((u + 3) % 4)

        def k_or_unit(eng, name, i, last, unit):
            if i < last:
                eng.wait_ge(at[name], i + 1)
            else:
                eng.wait_ge(unit_done, unit + 1)

        def att_sp(sp):
            sp.wait_ge(q["out"], 1)
            sp.wait_ge(rw_fin, 16 * 9)
            sp.dma_start(qup[:, :, :].rearrange("p k n -> p (k n)"), L_("qup").rearrange("l p n -> p (l n)"))\
                .then_inc(at["in"], 16)
            sp.dma_start(latT[:, :, TP:TP + PAST], L_("cache_lat").rearrange("l p k n -> p (l k) n"))\
                .then_inc(at["lat_in"], 16)
            sp.dma_start(krc[NOPE:QK, :], L_("cache_rope").rearrange("l p n -> p (l n)")).then_inc(at["lat_in"], 16)

        def att_out_sp(sp):
            sp.wait_ge(at["out"], 48)

        def att_pe(pe):
            pe.wait_ge(q["out"], 1)
            for i in range(2, 5):
                if i == 4:
                    pe.wait_ge(at["pm"], 2)
                unit_mm(pe, U_MLA + i, (i + 3) % 4)
            pe.wait_ge(at["pm"], 6)
            unit_wait(pe, U_MLA + 5)
            w = ring[:, (U_MLA + 5) % RING, 0:DT * ROPE].rearrange("p (k m) -> p k m", k=DT)
            for k in range(DT):
                for h in range(2):
                    ins = nc.tensor.matmul(PS[NOPE:QK, 2 + h, 0:HALF], w[:, k, :], hT[:, k, h * HALF:(h + 1) * HALF],
                                           start=(k == 0), stop=(k == DT - 1))
            ins.then_inc(unit_done, 1)
            pe.wait_ge(at["pm"], 10)
            pe.wait_ge(at["sq"], 10)
            for t in range(5):
                o, first, last = (4, t == 0, t == 2) if t < 3 else (6, t == 3, t == 4)
                for h in range(2):
                    ins = nc.tensor.matmul(PS[0:1, o + h, 0:HALF], ones[:, 0:1], msq[:, t, h * HALF:(h + 1) * HALF],
                                           start=first, stop=last)
            ins.then_inc(at["row"], 1)
            pe.wait_ge(at["kr"], 2)
            pe.wait_ge(at["init"], 1)
            for h in range(2):
                ins = nc.tensor.matmul(PS[NOPE:QK, h, 0:HALF], c_("rot")[0:QK], krt[0:QK, h * HALF:(h + 1) * HALF],
                                       start=True, stop=True)
            ins.then_inc(at["krot"], 1)
            pe.wait_ge(at["srow"], 4)
            for j in range(2):
                for i in range(TT):
                    m = P if i < 4 else TS
                    ins = nc.tensor.matmul(PS[0:m, 2, 5 * j + i:5 * j + i + 1], row[0:1, j, i * P:i * P + m],
                                           ones[0:1, 0:1], start=True, stop=True)
            ins.then_inc(at["col"], 1)
            turn_rb(pe, at, lambda i, t: rb[:, i, t, :])
            pe.wait_ge(at["lat"], 4)
            pe.wait_ge(at["lat_in"], 32)
            wk = unit_wait(pe, U_UK).rearrange("p k m -> p (k m)").rearrange("p (k m) -> p k m", k=2)
            for h in range(HEADS):
                b = 2 * ((h + 3) % 4)
                if h == 1:
                    pe.wait_ge(at["sin"], 2)
                if h == 2:
                    pe.wait_ge(at["qn"], 6)
                if h >= 4:
                    pe.wait_ge(at["ka"], h - 3)
                    pe.wait_ge(at["kd"], h - 3)
                for o, n, lo in ((0, TP, 0), (1, PAST + TS, TP)):
                    for k in range(2):
                        ins = nc.tensor.matmul(PS[0:NOPE, b + o, 0:n], wk[:, k, h * NOPE:(h + 1) * NOPE],
                                               latT[:, k, lo:lo + n], start=(k == 0), stop=(k == 1))
                ins.then_inc(at["k_mm"] if h < 7 else unit_done, 1)
            wv = unit_wait(pe, U_UV).rearrange("p k m -> p (k m)").rearrange("p (k m) -> p k m", k=2)
            for i in range(7):
                m = P if i < 6 else TS
                if i % 2 == 0:
                    pe.wait_ge(at["ka"], 5 + i // 2)
                    pe.wait_ge(at["kd"], 5 + i // 2)
                for k in range(2):
                    ins = nc.tensor.matmul(PS[0:m, (6 + i) % 8, :], latT[:, k, i * P:i * P + m], wv[:, k, :],
                                           start=(k == 0), stop=(k == 1))
                ins.then_inc(at["v_mm"] if i < 6 else unit_done, 1)
            pe.wait_ge(at["qn"], 6)
            pe.wait_ge(at["in"], 16)
            for u, (kind, h) in enumerate(q_uses):
                b = q_bank("", u)
                if u < 4:
                    pe.wait_ge(at["v"], min(2 * u + 2, 7))
                else:
                    was, g = q_uses[u - 4]
                    if was == "up":
                        pe.wait_ge(at["ka"], 8 + g + 1)
                        pe.wait_ge(at["kd"], 8 + g + 1)
                    else:
                        pe.wait_ge(at["sin"], 2 + 2 * (g + 1))
                if kind == "up":
                    for k in range(3):
                        for o in range(2):
                            ins = nc.tensor.matmul(PS[0:QK, b + o, 0:HALF], qup[:, k, h * QK:(h + 1) * QK],
                                                   pmT[:, k, o * HALF:(o + 1) * HALF], start=(k == 0), stop=(k == 2))
                    ins.then_inc(at["q_mm"], 1)
                else:
                    pe.wait_ge(at["ka"], 8 + h + 1)
                    pe.wait_ge(at["kd"], 8 + h + 1)
                    for o in range(2):
                        ins = nc.tensor.matmul(PS[NOPE:QK, b + o, 0:HALF], c_("rot")[0:QK],
                                               QT[0:QK, h, o * HALF:(o + 1) * HALF], start=True, stop=True)
                    ins.then_inc(at["rot"], 1)
            pe.wait_ge(at["q"], 1)
            pe.wait_ge(at["sin"], 2 + 2 * HEADS)
            pe.wait_ge(at["kb"], 5)

            def scores(i):
                b, g = groups[i]
                n, m = extent(b), (P if b < 4 else TS)
                keys, rows = (KT, QK + 4) if b < 4 else (KTs, QK)
                if i:
                    pe.wait_ge(at["exp"], 4 * i)
                if i == 1:
                    pe.wait_ge(at["q"], 2)
                for j in range(4):
                    h = 4 * g + j
                    ins = nc.tensor.matmul(PS[0:m, j, 0:n], QT[0:rows, h, b * P:b * P + m], keys[0:rows, h, 0:n],
                                           start=True, stop=True)
                ins.then_inc(at["s"], 1)

            scores(0)
            for i, (b, g) in enumerate(groups):
                m = P if b < 4 else TS
                if i + 1 < len(groups):
                    scores(i + 1)
                pe.wait_ge(at["dg"], i + 1)
                for n in range(first_tile[i], first_tile[i + 1]):
                    k = ktiles[n][1]
                    if n >= 3:
                        pe.wait_ge(at["td" if (n - 3) % 2 else "ta"], (n - 3) // 2 + 1)
                    rows = min(P, extent(b) - k * P)
                    for j in range(4):
                        ins = nc.tensor.matmul(PS[0:rows, 4 + n % 3, j * P:j * P + m],
                                               prob[i % 2][0:m, j, k * P:k * P + rows], diag[i % 2][0:m, j, 0:m],
                                               start=True, stop=True)
                    ins.then_inc(at["t"], 1)
                last = first_tile[i + 1] - 1
                for n in (last, last - 1):
                    if n >= first_tile[i]:
                        pe.wait_ge(at["td" if n % 2 else "ta"], n // 2 + 1)
                if i:
                    pe.wait_ge(at["o"], i)
                tiles = range(first_tile[i], first_tile[i + 1])
                for j in range(4):
                    h = 4 * g + j
                    for n in tiles:
                        k = ktiles[n][1]
                        rows = min(P, extent(b) - k * P)
                        o = (i % 2) * 256 + (j // 2) * P
                        ins = nc.tensor.matmul(PS[64 * (j % 2):64 * (j % 2) + 64, 7, o:o + m],
                                               vv[0:rows, k + (4 if b == 4 else 0), h * VH:(h + 1) * VH],
                                               probT[i % 2][0:rows, k, j, 0:m], start=(n == tiles[0]),
                                               stop=(n == tiles[-1]), skip_group_check=True)
                ins.then_inc(at["o_mm"], 1)

        def att_act(act):
            for t in range(5):
                act.wait_ge(at["pm"], 2 * t + 2)
                nc.scalar.activation(msq[:, t, :], pmT[:, t, :], ACT.Square).then_inc(at["sq"], 2)
            act.wait_ge(unit_done, U_MLA + 6)
            for h in range(2):
                nc.scalar.copy(krt[NOPE:QK, h * HALF:(h + 1) * HALF], PS[NOPE:QK, 2 + h, 0:HALF])\
                    .then_inc(at["kr"], 1)
            for h in range(HEADS):
                k_or_unit(act, "k_mm", h, 7, U_UK)
                nc.scalar.copy(KT[0:NOPE, h, :], PS[0:NOPE, 2 * ((h + 3) % 4), :]).then_inc(at["ka"], 1)
            act.dma_start(L_("out_lat")[:, :, :, 0:TP].rearrange("l p k n -> p (l k) n"), latT[:, :, 0:TP])\
                .then_inc(at["out"], 16)
            act.dma_start(L_("out_lat")[:, :, :, TP:T].rearrange("l p k n -> p (l k) n"),
                          latT[:, :, TP + PAST:TP + PAST + TS]).then_inc(at["out"], 16)
            act.wait_ge(at["krr"], 1)
            act.dma_start(L_("out_rope").rearrange("l p n -> p (l n)"), krr[NOPE:QK, :]).then_inc(at["out"], 16)
            for i in range(7):
                m = P if i < 6 else TS
                k_or_unit(act, "v_mm", i, 6, U_UV)
                nc.scalar.copy(vv[0:m, i, :], PS[0:m, (6 + i) % 8, :]).then_inc(at["v"], 1)
            for h in range(HEADS):
                act.wait_ge(at["q_mm"], h + 1)
                nc.scalar.copy(QT[0:QK, h, 0:HALF], PS[0:QK, q_bank("up", h), 0:HALF]).then_inc(at["ka"], 1)

            def exps(i):
                b, g = groups[i]
                n, m = extent(b), (P if b < 4 else TS)
                act.wait_ge(at["mx"], i + 1)
                if i == 1:
                    act.wait_ge(at["out"], 48)
                if i >= 2:
                    act.wait_ge(at["t"], first_tile[i - 1])
                for j in range(4):
                    nc.scalar.activation(prob[i % 2][0:m, j, 0:n], PS[0:m, j, 0:n], ACT.Exp, scale=SCALE,
                                         bias=mx[0:m, i % 2, 1, j:j + 1], accum_out=mx[0:m, i % 2, 2, j:j + 1])\
                        .then_inc(at["exp"], 1)

            exps(0)
            for i, (b, g) in enumerate(groups):
                m = P if b < 4 else TS
                if i + 1 < len(groups):
                    exps(i + 1)
                for n in range(first_tile[i], first_tile[i + 1]):
                    if n % 2 == 0:
                        turned(act, nc.scalar.copy, i, n)
                act.wait_ge(at["o_mm"], i + 1)
                nc.scalar.copy(oT[:, 2 * g:2 * g + 2, b * P:b * P + m],
                               PS[:, 7, (i % 2) * 256:(i % 2) * 256 + 256].rearrange("p (t n) -> p t n", t=2)[:, :, 0:m])\
                    .then_inc(at["o"], 1)

        def turned(eng, copy, i, n):
            b, k = groups[i][0], ktiles[n][1]
            m, rows = (P if b < 4 else TS), min(P, extent(b) - k * P)
            eng.wait_ge(at["t"], n + 1)
            if i >= 2:
                eng.wait_ge(at["o_mm"], i - 1)
            copy(probT[i % 2][0:rows, k, :, 0:m], PS[0:rows, 4 + n % 3, :].rearrange("p (j n) -> p j n", j=4)[:, :, 0:m])\
                .then_inc(at["td" if n % 2 else "ta"], 1)

        def att_pool(pool):
            pool.wait_ge(q["out"], 1)
            nc.gpsimd.memset(krt[0:NOPE, :], 0.0).then_inc(at["init"], 1)
            pool.wait_ge(at["init"], 1)
            pool.wait_ge(rw_fin, 16 * 9)
            nc.gpsimd.tensor_copy(QT[QK:QK + 4, :, 0:TP], cos[QK:QK + 4, 0:TP].unsqueeze(1).to_broadcast([4, HEADS, TP]))\
                .then_inc(at["kb"], 1)
            pool.wait_ge(at["kb"], 1)
            nc.gpsimd.tensor_copy(KT[QK:QK + 4, :, :], sin[QK:QK + 4, 0:TP].unsqueeze(1).to_broadcast([4, HEADS, TP]))\
                .then_inc(at["kb"], 1)
            pool.wait_ge(at["kb"], 2)
            pool.wait_ge(at["krot"], 1)
            nc.gpsimd.tensor_tensor(krt[NOPE:QK, :], krt[NOPE:QK, :], cos[NOPE:QK, :], ALU.mult).then_inc(at["cos"], 1)
            pool.wait_ge(at["cos"], 1)
            norm_pow(pool, at, 10)
            pool.wait_ge(at["rs"], 1)
            pool.wait_ge(at["lat_in"], 32)
            nc.gpsimd.tensor_copy(KTs[NOPE:QK, :, 0:PAST], krc[NOPE:QK, :].unsqueeze(1).to_broadcast([ROPE, HEADS, PAST]))\
                .then_inc(at["kb"], 1)
            pool.wait_ge(at["krr"], 1)
            pool.wait_ge(at["kb"], 3)
            nc.gpsimd.tensor_copy(KT[NOPE:QK, :, :], krr[NOPE:QK, 0:TP].unsqueeze(1).to_broadcast([ROPE, HEADS, TP]))\
                .then_inc(at["kb"], 1)
            pool.wait_ge(at["kb"], 4)
            nc.gpsimd.tensor_copy(KTs[NOPE:QK, :, PAST:PAST + TS],
                                  krr[NOPE:QK, TP:T].unsqueeze(1).to_broadcast([ROPE, HEADS, TS])).then_inc(at["kb"], 1)
            pool.wait_ge(at["kb"], 5)
            for g in range(2):
                pool.wait_ge(at["rot"], 4 * g + 4)
                if g:
                    pool.wait_ge(at["cos"], 2)
                nc.gpsimd.tensor_tensor(QT[NOPE:QK, 4 * g:4 * g + 4, :], QT[NOPE:QK, 4 * g:4 * g + 4, :],
                                        cos[NOPE:QK, :].unsqueeze(1).to_broadcast([ROPE, 4, T]), ALU.mult)\
                    .then_inc(at["cos"], 1)
            pool.wait_ge(at["cos"], 3)

        def att_dve(dve, ch):
            for t in range(5):
                dve.wait_ge(unit_done, U_MLA + t + 1)
                for h in range(2):
                    nc.vector.tensor_copy(pmT[:, t, h * HALF:(h + 1) * HALF], PS[:, 2 * ((t + 3) % 4) + h, 0:HALF])\
                        .then_inc(at["pm"], 1)
            dve.wait_ge(at["row"], 1)
            for j in range(2):
                for h in range(2):
                    nc.vector.tensor_copy(row[0:1, j, h * HALF:(h + 1) * HALF], PS[0:1, 4 + 2 * j + h, 0:HALF])\
                        .then_inc(at["srow"], 1)
            dve.wait_ge(at["krot"], 1)
            for h in range(2):
                nc.vector.tensor_tensor(krr[NOPE:QK, h * HALF:(h + 1) * HALF], PS[NOPE:QK, h, 0:HALF],
                                        sin[NOPE:QK, h * HALF:(h + 1) * HALF], ALU.mult).then_inc(at["sin"], 1)
            dve.wait_ge(at["col"], 1)
            for j, n in ((0, QL), (1, KVL)):
                ins = nc.vector.tensor_scalar(rs_in[:, 5 * j:5 * j + 4], PS[:, 2, 5 * j:5 * j + 4], 1.0 / n, 1e-6,
                                              ALU.mult, ALU.add)
                ch.mark(ins)
                ins = nc.vector.tensor_scalar(rs_in[0:TS, 5 * j + 4:5 * j + 5], PS[0:TS, 2, 5 * j + 4:5 * j + 5],
                                              1.0 / n, 1e-6, ALU.mult, ALU.add)
                ins.then_inc(at["ms"], 2) if j else ch.mark(ins)
            dve.wait_ge(at["cos"], 1)
            dve.wait_ge(at["sin"], 2)
            nc.vector.tensor_tensor(krr[NOPE:QK, :], krr[NOPE:QK, :], krt[NOPE:QK, :], ALU.add).then_inc(at["krr"], 1)
            dve.wait_ge(at["rs"], 1)
            for j in range(2):
                ins = nc.vector.tensor_copy(rb[:, :, j, :], rs[:, 5 * j:5 * j + 5].unsqueeze(2).to_broadcast([P, TT, P]))
                if j:
                    ins.then_inc(at["rb"], 1)
                else:
                    ch.link(ins)
            dve.wait_ge(at["bc"], 1)
            for t in range(2):
                nc.vector.scalar_tensor_tensor(latT[:, t, 0:TP], pmT[:, 3 + t, 0:TP], p_("kv_norm_g", t), PS[:, 5, :],
                                               ALU.mult, ALU.mult).then_inc(at["lat"], 1)
                nc.vector.scalar_tensor_tensor(latT[:, t, TP + PAST:], pmT[:, 3 + t, TP:T], p_("kv_norm_g", t),
                                               PS[:, 4, TS:2 * TS], ALU.mult, ALU.mult).then_inc(at["lat"], 1)
            for t in range(3):
                nc.vector.scalar_tensor_tensor(pmT[:, t, 0:TP], pmT[:, t, 0:TP], p_("q_norm_g", t), PS[:, 3, :],
                                               ALU.mult, ALU.mult).then_inc(at["qn"], 1)
                nc.vector.scalar_tensor_tensor(pmT[:, t, TP:T], pmT[:, t, TP:T], p_("q_norm_g", t), PS[:, 4, 0:TS],
                                               ALU.mult, ALU.mult).then_inc(at["qn"], 1)
            for h in range(HEADS):
                k_or_unit(dve, "k_mm", h, 7, U_UK)
                nc.vector.tensor_copy(KTs[0:NOPE, h, :], PS[0:NOPE, 2 * ((h + 3) % 4) + 1, 0:PAST + TS])\
                    .then_inc(at["kd"], 1)
            for kind, h in q_uses:
                if kind == "up":
                    dve.wait_ge(at["q_mm"], h + 1)
                    nc.vector.tensor_copy(QT[0:QK, h, HALF:T], PS[0:QK, q_bank("up", h) + 1, 0:HALF])\
                        .then_inc(at["kd"], 1)
                    continue
                dve.wait_ge(at["rot"], h + 1)
                if h == 4:
                    dve.wait_ge(at["q_mm"], HEADS)
                for o in range(2):
                    nc.vector.tensor_tensor(sin_q[h // 4][NOPE:QK, h % 4, o * HALF:(o + 1) * HALF],
                                            PS[NOPE:QK, q_bank("rot", h) + o, 0:HALF],
                                            sin[NOPE:QK, o * HALF:(o + 1) * HALF], ALU.mult).then_inc(at["sin"], 1)
                if h % 4 == 3:
                    g = h // 4
                    dve.wait_ge(at["cos"], g + 2)
                    dve.wait_ge(at["sin"], 2 + 2 * h + 2)
                    nc.vector.tensor_tensor(QT[NOPE:QK, 4 * g:4 * g + 4, :], QT[NOPE:QK, 4 * g:4 * g + 4, :],
                                            sin_q[g][NOPE:QK, :, :], ALU.add).then_inc(at["q"], 1)

            def maxima(i):
                b, g = groups[i]
                n, m = extent(b), (P if b < 4 else TS)
                dve.wait_ge(at["s"], i + 1)
                ch.link(nc.vector.tensor_reduce(mx[0:m, i % 2, 0, :], PS[0:m, 0:4, 0:n], AX_X, ALU.max))
                nc.vector.tensor_scalar(mx[0:m, i % 2, 1, :], mx[0:m, i % 2, 0, :], -SCALE, None, ALU.mult)\
                    .then_inc(at["mx"], 1)

            maxima(0)
            for i, (b, g) in enumerate(groups):
                m = P if b < 4 else TS
                dve.wait_ge(at["exp"], 4 * i + 4)
                if i >= 2:
                    dve.wait_ge(at["t"], first_tile[i - 1])
                elif i == 1:
                    dve.wait_ge(at["out"], 48)
                ch.link(nc.vector.reciprocal(mx[0:m, i % 2, 3, :], mx[0:m, i % 2, 2, :]))
                nc.vector.tensor_tensor(diag[i % 2][0:m, :, :], ident[0:m].unsqueeze(1).to_broadcast([m, 4, P]),
                                        mx[0:m, i % 2, 3, :].unsqueeze(2).to_broadcast([m, 4, P]), ALU.mult)\
                    .then_inc(at["dg"], 1)
                if i + 1 < len(groups):
                    maxima(i + 1)
                for n in range(first_tile[i], first_tile[i + 1]):
                    if n % 2:
                        turned(dve, nc.vector.tensor_copy, i, n)

        g_ = {n: sem(f"mg_{n}") for n in ("th", "o_mm", "u", "done", "out", "hi", "lo", "w_hi", "w_lo")}
        split_units = [U_MERGE + 4 * t + b for t in range(DT) for b in range(3)] + [U_OUT + t for t in range(DT)]

        def weights_hi(act, j):
            if j >= len(split_units):
                return
            w = unit_wait(act, split_units[j])
            if j >= 2:
                act.wait_ge(unit_done, split_units[j - 2] + 1)
            nc.scalar.copy(w_hi[:, j % 2], w).then_inc(g_["w_hi"], 1)

        def weights_lo(dve, j):
            if j >= len(split_units):
                return
            w = unit_wait(dve, split_units[j])
            dve.wait_ge(g_["w_hi"], j + 1)
            if j >= 2:
                dve.wait_ge(unit_done, split_units[j - 2] + 1)
            nc.vector.tensor_tensor(w_lo[:, j % 2], w, w_hi[:, j % 2], ALU.subtract).then_inc(g_["w_lo"], 1)

        def split_mm(pe, j, pair):
            pe.wait_ge(g_["w_hi"], j + 1)
            pe.wait_ge(g_["w_lo"], j + 1)
            base = 0 if j < 3 * DT else DT
            for k in range(DT):
                if j in (0, 3 * DT):
                    pe.wait_ge(g_["hi"], base + k + 1)
                    pe.wait_ge(g_["lo"], base + k + 1)
                for n, (w, v) in enumerate(((w_hi, x_hi), (w_hi, x_lo), (w_lo, x_hi))):
                    for h in range(2):
                        ins = nc.tensor.matmul(PS[:, 2 * pair + h, 0:HALF], w[:, j % 2, k, :],
                                               v[:, k, h * HALF:(h + 1) * HALF], start=(k == 0 and n == 0),
                                               stop=(k == DT - 1 and n == 2))
            ins.then_inc(unit_done, 1)
        src_k = ((0, 4), (4, 6), (6, 8))

        def branch(b, k):
            return (oT, yT, cT)[b][:, k - src_k[b][0], :]

        def freed(pe, n):
            d_, j = divmod(n, 6)
            if j < 3:
                pe.wait_ge(g_["th"], 2 * (3 * d_ + j + 1))
            else:
                pe.wait_ge(g_["u"], 2 * (3 * d_ + j - 2))

        def merge_pe(pe):
            pe.wait_ge(at["o"], len(groups))
            for t in range(DT):
                for j in range(6):
                    n = 6 * t + j
                    if n >= 4:
                        freed(pe, n - 4)
                    if j < 3:
                        split_mm(pe, 3 * t + j, n % 4)
                        continue
                    w = unit_wait(pe, U_MERGE + 4 * t + 3)
                    lo, hi = src_k[j - 3]
                    for k in range(lo, hi):
                        for h in range(2):
                            ins = nc.tensor.matmul(PS[:, 2 * (n % 4) + h, 0:HALF], w[:, k, :],
                                                   branch(j - 3, k)[:, h * HALF:(h + 1) * HALF],
                                                   start=(k == lo), stop=(k == hi - 1))
                    ins.then_inc(unit_done if j == 5 else g_["o_mm"], 1)
            for t in range(DT):
                n = 6 * DT + t
                pe.wait_ge(g_["done"], DT)
                if t >= 4:
                    pe.wait_ge(g_["out"], 3 * (t - 3))
                else:
                    freed(pe, n - 4)
                split_mm(pe, 3 * DT + t, n % 4)
            pe.wait_ge(g_["out"], 3 * DT)
            norm_x_pe(pe, nm["n1"], 1)

        def merge_act(act):
            for k in range(DT):
                nc.scalar.copy(x_hi[:, k, :], hT[:, k, :]).then_inc(g_["hi"], 1)
                if k in (0, 1):
                    weights_hi(act, k)
            for t in range(DT):
                for b in range(3):
                    n = 6 * t + b
                    act.wait_ge(unit_done, U_MERGE + 4 * t + b + 1)
                    if t >= 2:
                        act.wait_ge(g_["u"], 2 * (3 * (t - 2) + b + 1))
                    for h in range(2):
                        nc.scalar.activation(th[t % 2][:, b, h * HALF:(h + 1) * HALF], PS[:, 2 * (n % 4) + h, 0:HALF],
                                             ACT.Tanh, scale=0.5).then_inc(g_["th"], 1)
                    weights_hi(act, 3 * t + b + 2)
            act.wait_ge(unit_done, U_OUT)
            for k in range(DT):
                act.wait_ge(g_["done"], k + 1)
                nc.scalar.copy(x_hi[:, k, :], mg[:, k, :]).then_inc(g_["hi"], 1)
            for k in range(DT + 1):
                if k < DT - 2:
                    weights_hi(act, 3 * DT + k + 2)
                if k:
                    act.wait_ge(g_["out"], 3 * k)
                    nc.scalar.activation(hT[:, k - 1, :], xT[:, k - 1, :], ACT.Square).then_inc(nm["n1"]["sq"], 1)
            norm_shift_act(act, nm["n1"], 3, 1)

        def merge_pool(pool):
            norm_pow(pool, nm["n1"], r=1)

        def merge_dve(dve, ch):
            for g in range(2):
                ch.mark(nc.vector.scalar_tensor_tensor(gain2[:, :, g], mod[:, 4 * DT:5 * DT, g], 1.0, p_("norm2_g"),
                                                       ALU.add, ALU.mult))
            ch.mark(nc.vector.tensor_scalar(half_gt1[:, :, :], mod[:, 2 * DT:3 * DT, :], 0.5, None, ALU.mult))
            ch.link(nc.vector.tensor_scalar(half_gt2[:, :, :], mod[:, 5 * DT:6 * DT, :], 0.5, None, ALU.mult))
            dve.wait_ge(at["o"], len(groups))
            for k in range(DT):
                dve.wait_ge(g_["hi"], k + 1)
                nc.vector.tensor_tensor(x_lo[:, k, :], hT[:, k, :], x_hi[:, k, :], ALU.subtract).then_inc(g_["lo"], 1)
                if k in (0, 1):
                    weights_lo(dve, k)
            for t in range(DT):
                for b in range(3):
                    weights_lo(dve, 3 * t + b + 2)
                for b in range(3):
                    n = 6 * t + 3 + b
                    dve.wait_ge(g_["th"], 2 * (3 * t + b + 1))
                    if b < 2:
                        dve.wait_ge(g_["o_mm"], 2 * t + b + 1)
                    else:
                        dve.wait_ge(unit_done, U_MERGE + 4 * t + 4)
                    dst = mg[:, t, :] if b == 0 else mtmp[b - 1]
                    for h in range(2):
                        nc.vector.scalar_tensor_tensor(dst[:, h * HALF:(h + 1) * HALF],
                                                       th[t % 2][:, b, h * HALF:(h + 1) * HALF], 1.0,
                                                       PS[:, 2 * (n % 4) + h, 0:HALF], ALU.add, ALU.mult)\
                            .then_inc(g_["u"], 1)
                    dve.wait_ge(g_["u"], 2 * (3 * t + b + 1))
                    if b:
                        ins = nc.vector.tensor_tensor(mg[:, t, :], mg[:, t, :], mtmp[b - 1], ALU.add)
                        if b == 1:
                            ch.link(ins)
                        else:
                            ins.then_inc(g_["done"], 1)
            dve.wait_ge(g_["done"], DT)
            for k in range(DT):
                dve.wait_ge(g_["hi"], DT + k + 1)
                nc.vector.tensor_tensor(x_lo[:, k, :], mg[:, k, :], x_hi[:, k, :], ALU.subtract).then_inc(g_["lo"], 1)
            for t in range(DT):
                n = 6 * DT + t
                if t < DT - 2:
                    weights_lo(dve, 3 * DT + t + 2)
                dve.wait_ge(unit_done, U_OUT + t + 1)
                for bank, src, lo, hi, g in ((0, 0, 0, HALF, 0), (1, 0, HALF, TP, 0), (1, TP - HALF, TP, T, 1)):
                    nc.vector.scalar_tensor_tensor(xT[:, t, lo:hi], PS[:, 2 * (n % 4) + bank, src:src + hi - lo],
                                                   half_gt1[:, t, g:g + 1], xT[:, t, lo:hi], ALU.mult, ALU.add)\
                        .then_inc(g_["out"], 1)
            norm_x_dve(dve, nm["n1"], lambda k, g: gain2[:, k, g:g + 1], 1)

        e_ = {n: sem(f"moe_{n}") for n in ("w0", "w1", "d0", "d1", "logit", "shift", "gexp", "diff", "eexp", "comb",
                                           "both", "rank", "most", "most_row", "clr", "ht", "hte")}

        def again(names, before):
            return dict(zip(names, list(before.values())[:len(names)]))

        e_ |= again(("combT", "mm", "th", "use", "ctp"), at)
        order = [("gu", 0), ("gu", 1)]
        for e in range(2, NE, 2):
            order += [("gu", e), ("dn", e // 2 - 1), ("gu", e + 1)]
        order.append(("dn", NE // 2 - 1))
        start = {}
        _n = 0
        for kind, i in order:
            start[kind, i] = _n
            _n += 5 if kind == "gu" else DT

        def load_expert(sp, e, part):
            if part == "gu":
                sp.dma_start(gu_w[e % 2][:, :, :].rearrange("p k n -> p (k n)"),
                             L_("moe_gu")[:, e].rearrange("l p n -> p (l n)")).then_inc(e_[f"w{e % 2}"], 16)
            else:
                sp.dma_start(dn_w[e % 2][:, :, :].rearrange("p k n -> p (k n)"),
                             L_("moe_dn")[:, e].rearrange("l p n -> p (l n)")).then_inc(e_[f"d{e % 2}"], 16)

        p_s = again(("x0", "x1", "y0", "y1", "tx", "xa", "xd", "gu", "th", "act", "at", "ae", "dn", "oa", "od", "yc",
                     "yt", "yx", "y2"), q)
        s_scat, s_gath = (ctx.enter_context(nc.semaphore(n)) for n in ("scattered", "gathered"))

        def flat16(j):
            return sel[:, j, :, :, :].rearrange("p i g e -> p i (g e)")

        def route_sp(sp):
            sp.wait_ge(unit_done, UNITS)
            for e in range(2):
                load_expert(sp, e, "gu")
                load_expert(sp, e, "dn")
            for n in ("w0", "w1", "d0", "d1"):
                sp.wait_ge(e_[n], 16)
            sp.wait_ge(s_zero, 16 * NE)

        def route_pe(pe):
            pe.wait_ge(nm["n1"]["out"], 4 * DT)
            for i in range(TT):
                m = P if i < 4 else TS
                for k in range(DT):
                    ins = nc.tensor.matmul(PS[0:m, 0, 20 * i:20 * i + 20], hT[:, k, i * P:i * P + m], router_w[:, k, :],
                                           start=(k == 0), stop=(k == DT - 1))
            ins.then_inc(e_["logit"], 1)
            for n in range(2 * TT):
                i, h = divmod(n, 2)
                m = P if i < 4 else TS
                if n >= 4:
                    pe.wait_ge(e_["hte"], n - 3)
                if n == 8:
                    pe.wait_ge(e_["both"], 1)
                    for t in range(TT):
                        for j in range(t + 1):
                            ins = nc.tensor.matmul(PS[:, 1, NE * t:NE * t + NE], (before if j == t else ones_b)[:, :],
                                                   both[:, j, :], start=(j == 0), stop=(j == t))
                    ins.then_inc(e_["rank"], 1)
                for k in range(4):
                    ins = nc.tensor.transpose(PS[0:m, 4 + n % 4, k * P:(k + 1) * P], hT[:, 4 * h + k, i * P:i * P + m],
                                              ident)
                ins.then_inc(e_["ht"], 1)
            pe.wait_ge(e_["most"], 1)
            nc.tensor.transpose(PS[0:1, 2, 0:P], most[:, :], ident).then_inc(e_["most_row"], 1)

        def route_act(act):
            act.wait_ge(e_["shift"], 1)
            nc.scalar.activation(ra[:, 0, :, :], ra[:, 0, :, :], ACT.Exp).then_inc(e_["gexp"], 1)
            for n in range(2 * TT):
                i, h = divmod(n, 2)
                m = P if i < 4 else TS
                act.wait_ge(e_["ht"], n + 1)
                nc.scalar.copy(htok[0:m, i, 512 * h:512 * h + 512], PS[0:m, 4 + n % 4, :]).then_inc(e_["hte"], 1)
                if n == 4:
                    act.wait_ge(e_["diff"], 1)
                    nc.scalar.activation(rm[:, 3, :], rm[:, 3, :], ACT.Exp).then_inc(e_["eexp"], 1)

        def route_pool(pool):
            pool.wait_ge(g_["done"], DT)
            nc.gpsimd.memset(lg[:, 4, :], 0.0).then_inc(e_["clr"], 1)

        def route_dve(dve, ch):
            V = nc.vector
            A, B, C, D_ = (ra[:, i, :, :] for i in range(4))
            col = lambda i: rm[:, i, :]
            wide = lambda i: rm[:, i, :].unsqueeze(2).to_broadcast([P, TT, 4])
            fall = c_("falling").unsqueeze(1).to_broadcast([P, TT, 4])
            glog = lg[:, :, 0:4]
            dve.wait_ge(e_["logit"], 1)
            dve.wait_ge(e_["clr"], 1)
            ch.mark(V.tensor_tensor(lg[:, 0:4, :], PS[:, 0, 0:80].rearrange("p (i n) -> p i n", i=4),
                                    router_b[:, :].unsqueeze(1).to_broadcast([P, 4, 20]), ALU.add))
            ch.link(V.tensor_tensor(lg[0:TS, 4, :], PS[0:TS, 0, 80:100], router_b[0:TS, :], ALU.add))

            def first_max(src, at_col, dst):
                ch.link(V.tensor_reduce(col(at_col), src, AX_X, ALU.max))
                ch.link(V.tensor_tensor(dst, src, wide(at_col), ALU.is_equal))
                ch.link(V.tensor_tensor(dst, dst, fall, ALU.mult))
                ch.link(V.tensor_reduce(col(7), dst, AX_X, ALU.max))
                ch.link(V.tensor_tensor(dst, dst, wide(7), ALU.is_equal))
            first_max(glog, 0, B)
            ch.link(V.tensor_tensor(B, B, c_("valid").unsqueeze(2).to_broadcast([P, TT, 4]), ALU.mult))
            V.tensor_tensor(A, glog, wide(0), ALU.subtract).then_inc(e_["shift"], 1)
            ch.link(V.tensor_tensor(grp[:, :, :, :], lg[:, :, 4:20].rearrange("p i (g e) -> p i g e", g=4),
                                    B.unsqueeze(3).to_broadcast([P, TT, 4, 4]), ALU.mult))
            ch.link(V.tensor_reduce(C, grp[:, :, :, :].rearrange("p i g e -> p i e g"), AX_X, ALU.add))
            dve.wait_ge(e_["gexp"], 1)
            ch.link(V.tensor_reduce(col(1), A, AX_X, ALU.add))
            ch.link(V.reciprocal(col(1), col(1)))
            first_max(C, 2, D_)
            ch.link(V.scalar_tensor_tensor(C, D_, -1e30, C, ALU.mult, ALU.add))
            first_max(C, 4, A)
            V.tensor_tensor(col(3), col(4), col(2), ALU.subtract).then_inc(e_["diff"], 1)
            pick = lambda j: sel[:, j, :, :, :]
            for j, v in enumerate((D_, A)):
                ch.mark(V.tensor_tensor(pick(j), B.unsqueeze(3).to_broadcast([P, TT, 4, 4]),
                                        v.unsqueeze(2).to_broadcast([P, TT, 4, 4]), ALU.mult))
            ch.wait(ch.n)
            V.tensor_tensor(both[:, :, :], flat16(0), flat16(1), ALU.add).then_inc(e_["both"], 1)
            dve.wait_ge(e_["eexp"], 1)
            ch.link(V.tensor_scalar(col(5), col(3), 1.0, None, ALU.add))
            ch.link(V.reciprocal(col(5), col(5)))
            ch.link(V.tensor_tensor(col(5), col(5), col(1), ALU.mult))
            ch.link(V.tensor_tensor(col(6), col(5), col(3), ALU.mult))
            ch.link(V.tensor_tensor(D_, D_, wide(5), ALU.mult))
            ch.link(V.tensor_tensor(A, A, wide(6), ALU.mult))
            ch.link(V.tensor_tensor(A, A, D_, ALU.add))
            V.tensor_tensor(cmb[:, :, :, :], B.unsqueeze(3).to_broadcast([P, TT, 4, 4]),
                            A.unsqueeze(2).to_broadcast([P, TT, 4, 4]), ALU.mult).then_inc(e_["comb"], 1)
            dve.wait_ge(e_["rank"], 1)
            ch.link(V.tensor_tensor(pos[:, 0:4, :], PS[:, 1, 0:64].rearrange("p (i n) -> p i n", i=4),
                                    c_("slot0").unsqueeze(1).to_broadcast([P, 4, NE]), ALU.add))
            ch.link(V.tensor_tensor(pos[:, 4, :], PS[:, 1, 64:80], c_("slot0"), ALU.add))
            for j in range(2):
                ch.link(V.tensor_tensor(flat16(j), flat16(j), pos[:, :, :], ALU.mult))
                ch.link(V.tensor_reduce(slot[:, j, :], flat16(j), AX_X, ALU.add))
            ch.link(V.tensor_copy(slot_i[:, :, :], slot[:, :, :]))
            ch.link(V.tensor_tensor(pos[:, :, :], pos[:, :, :], c_("slot0").unsqueeze(1).to_broadcast([P, TT, NE]),
                                    ALU.subtract))
            ch.link(V.tensor_tensor(pos[:, :, :], pos[:, :, :], both[:, :, :], ALU.mult))
            V.tensor_reduce(most[:, :], pos[:, :, :].rearrange("p i n -> p (i n)"), AX_X, ALU.max).then_inc(e_["most"], 1)
            dve.wait_ge(e_["most_row"], 1)
            ch.link(V.tensor_reduce(most[0:1, :], PS[0:1, 2, 0:P], AX_X, ALU.max))
            ch.link(V.tensor_scalar(most[0:1, :], most[0:1, :], P - 0.5, None, ALU.is_lt))
            ch.link(V.tensor_copy(fits[:, :], most[0:1, :]))

        def dense_sp(sp, t0):
            sp.wait_ge(s_scat, t0 + 160)
            for p in range(1, NE // 2):
                for e in (2 * p, 2 * p + 1):
                    sp.wait_ge(e_["mm"], start["gu", e - 2] + 4)
                    load_expert(sp, e, "gu")
                sp.wait_ge(e_["mm"], start["dn", p - 1] + DT)
                for e in (2 * p, 2 * p + 1):
                    if e == 2:
                        sp.wait_ge(s_gath, t0 + 160)
                    load_expert(sp, e, "dn")

        def dense_pe(pe):
            for i in range(4):
                nc.tensor.transpose(PS[0:NE, 1, i * P:(i + 1) * P], cmb[:, i, :, :].rearrange("p g e -> p (g e)"), ident)
            nc.tensor.transpose(PS[0:NE, 2, 0:TS], cmb[0:TS, 4, :, :].rearrange("p g e -> p (g e)"), ident[0:TS, 0:TS])\
                .then_inc(e_["ctp"], 1)
            pe.wait_ge(e_["combT"], 2)
            for kind, i in order:
                if kind == "gu":
                    if i >= 2:
                        pe.wait_ge(e_[f"w{i % 2}"], 16 * (i // 2))
                    for j in range(4):
                        n = start[kind, i] + j
                        if n >= 4:
                            pe.wait_ge(e_["use"], n - 3)
                        o = (j % 2) * FE + (j // 2) * P
                        for k in range(DT):
                            for h in range(2):
                                ins = nc.tensor.matmul(PS[:, 2 * (n % 4) + h, 0:HALF], gu_w[i % 2][:, k, o:o + P],
                                                       hT[:, k, h * HALF:(h + 1) * HALF],
                                                       start=(k == 0), stop=(k == DT - 1))
                        ins.then_inc(e_["mm"], 1)
                    n = start[kind, i] + 4
                    pe.wait_ge(e_["use"], n - 3)
                    for h in range(2):
                        ins = nc.tensor.matmul(PS[:, 2 * (n % 4) + h, 0:HALF], ident[0:NE, i:i + 1].to_broadcast([NE, P]),
                                               cmbT[0:NE, h * HALF:(h + 1) * HALF], start=True, stop=True)
                    ins.then_inc(e_["mm"], 1)
                else:
                    pe.wait_ge(e_["use"], start["gu", 2 * i + 1] + 5)
                    if i:
                        pe.wait_ge(e_["d0"], 16 * i)
                        pe.wait_ge(e_["d1"], 16 * i)
                    for t in range(DT):
                        n = start[kind, i] + t
                        pe.wait_ge(e_["use"], n - 3)
                        for e in range(2):
                            for k in range(2):
                                for h in range(2):
                                    ins = nc.tensor.matmul(PS[:, 2 * (n % 4) + h, 0:HALF],
                                                           dn_w[e][:, k, t * P:(t + 1) * P],
                                                           eact[:, (2 * i + e) % 3, k, h * HALF:(h + 1) * HALF],
                                                           start=(e == 0 and k == 0), stop=(e == 1 and k == 1))
                        ins.then_inc(e_["mm"], 1)

        def dense_act(act):
            act.wait_ge(e_["ctp"], 1)
            nc.scalar.copy(cmbT[0:NE, 0:TP], PS[0:NE, 1, :]).then_inc(e_["combT"], 1)
            nc.scalar.copy(cmbT[0:NE, TP:T], PS[0:NE, 2, 0:TS]).then_inc(e_["combT"], 1)
            c = 0
            for i in range(NE):
                for f in range(2):
                    n = start["gu", i] + 2 * f
                    act.wait_ge(e_["mm"], n + 1)
                    for h in range(2):
                        if c >= 2:
                            pc = c - 2
                            pi, pf = pc // 4, (pc // 2) % 2
                            act.wait_ge(e_["use"], start["gu", pi] + 2 * pf + 1)
                        nc.scalar.activation(eth[c % 2], PS[:, 2 * (n % 4) + h, 0:HALF], ACT.Tanh, scale=0.5)\
                            .then_inc(e_["th"], 1)
                        c += 1

        def dense_pool(pool):
            nc.gpsimd.memset(yacc[:, :, :], 0.0).then_inc(e_["clr"], 1)
            for i in range(2 * TT):
                dst = pos if i < TT else sel[:, 0, :, :, :].rearrange("p i g e -> p i (g e)")
                nc.gpsimd.dma_start(dst[:, i % TT, :], d["xs_d"][0:P, 0:NE]).then_inc(s_scat, 16)
            for i in range(2 * TT):
                nc.gpsimd.dma_start(sel[:, 1, i % TT, :, :].rearrange("p g e -> p (g e)") if i < TT else
                                    both_f[:, i % TT, :], d["xs_d"][0:P, 0:NE]).then_inc(s_gath, 16)

        def dense_dve(dve, ch):
            V = nc.vector
            dve.wait_ge(e_["clr"], 1)
            c = 0
            for kind, i in order:
                if kind == "gu":
                    dst = eact[:, i % 3, :, :]
                    if i >= 3:
                        dve.wait_ge(e_["mm"], start["dn", (i - 3) // 2] + DT)
                    for f in range(2):
                        n = start[kind, i] + 2 * f
                        for h in range(2):
                            c += 1
                            dve.wait_ge(e_["th"], c)
                            ins = V.scalar_tensor_tensor(dst[:, f, h * HALF:(h + 1) * HALF], eth[(c - 1) % 2], 1.0,
                                                         PS[:, 2 * (n % 4) + h, 0:HALF], ALU.add, ALU.mult)
                            ins.then_inc(e_["use"], 1) if h else ch.mark(ins)
                        ch.wait(ch.n)
                        dve.wait_ge(e_["use"], n + 1)
                        dve.wait_ge(e_["mm"], n + 2)
                        for h in range(2):
                            ins = V.tensor_tensor(dst[:, f, h * HALF:(h + 1) * HALF], dst[:, f, h * HALF:(h + 1) * HALF],
                                                  PS[:, 2 * ((n + 1) % 4) + h, 0:HALF], ALU.mult)
                            ins.then_inc(e_["use"], 1) if h else ch.mark(ins)
                    n = start[kind, i] + 4
                    ch.wait(ch.n)
                    dve.wait_ge(e_["use"], n)
                    dve.wait_ge(e_["mm"], n + 1)
                    for h in range(2):
                        ins = V.tensor_tensor(dst[:, :, h * HALF:(h + 1) * HALF], dst[:, :, h * HALF:(h + 1) * HALF],
                                              PS[:, 2 * (n % 4) + h, 0:HALF].unsqueeze(1).to_broadcast([P, 2, HALF]),
                                              ALU.mult)
                        if h:
                            ins.then_inc(e_["use"], 1)
                else:
                    for t in range(DT):
                        n = start[kind, i] + t
                        dve.wait_ge(e_["mm"], n + 1)
                        for h in range(2):
                            ins = V.tensor_tensor(yacc[:, t, h * HALF:(h + 1) * HALF], yacc[:, t, h * HALF:(h + 1) * HALF],
                                                  PS[:, 2 * (n % 4) + h, 0:HALF], ALU.add)
                            ins.then_inc(e_["use"], 1) if h else ch.mark(ins)
            ch.wait(ch.n)
            dve.wait_ge(e_["use"], start["dn", NE // 2 - 1] + DT)
            for t in range(DT):
                for g, lo, hi in ((0, 0, TP), (1, TP, T)):
                    V.scalar_tensor_tensor(xT[:, t, lo:hi], yacc[:, t, lo:hi], half_gt2[:, t, g:g + 1], xT[:, t, lo:hi],
                                           ALU.mult, ALU.add)


        def sparse_pool(pool, t0):
            for i in range(TT):
                m = P if i < 4 else TS
                for j in range(2):
                    nc.gpsimd.indirect_dma_start(d["xs_d"], bass.IndirectOffsetOnAxis(ap=slot_i[0:m, j, i:i + 1], axis=0),
                                                 htok[0:m, i, :], None).then_inc(s_scat, 16)
            for b in range(2):
                pool.wait_ge(p_s[f"y{b}"], 16 * NE // 2)
            for i in range(TT):
                m = P if i < 4 else TS
                for j in range(2):
                    nc.gpsimd.indirect_dma_start(yg[j][0:m, i, :], None, d["ys_d"],
                                                 bass.IndirectOffsetOnAxis(ap=slot_i[0:m, j, i:i + 1], axis=0))\
                        .then_inc(s_gath, 16)

        def sparse_sp(sp, t0):
            sp.wait_ge(s_scat, t0 + 160)
            for e in range(NE):
                if e >= 2:
                    sp.wait_ge(p_s["tx"], e - 1)
                sp.dma_start(xe[e % 2][:, :], d["xs_d"][e * P:(e + 1) * P, :]).then_inc(p_s[f"x{e % 2}"], 16)
                if e >= 2:
                    sp.wait_ge(p_s["gu"], e - 1)
                    load_expert(sp, e, "gu")
                    sp.wait_ge(p_s["dn"], e - 1)
                    load_expert(sp, e, "dn")

        def sparse_pe(pe):
            def turn_in(e):
                pe.wait_ge(p_s[f"x{e % 2}"], 16 * (e // 2 + 1))
                if e:
                    pe.wait_ge(p_s["xa"], e)
                    pe.wait_ge(p_s["xd"], e)
                for k in range(DT):
                    ins = nc.tensor.transpose(PS[:, k // 4, (k % 4) * P:(k % 4 + 1) * P],
                                              xe[e % 2][:, k * P:(k + 1) * P], ident)
                ins.then_inc(p_s["tx"], 1)

            def gate_up(e):
                pe.wait_ge(p_s["xa"], e + 1)
                pe.wait_ge(p_s["xd"], e + 1)
                if e >= 2:
                    pe.wait_ge(e_[f"w{e % 2}"], 16 * (e // 2))
                    pe.wait_ge(p_s["act"], e - 1)
                for k in range(DT):
                    ins = nc.tensor.matmul(PS[:, 2 + e % 2, :], xeT[e % 2][:, k, :], gu_w[e % 2][:, k, :],
                                           start=(k == 0), stop=(k == DT - 1))
                ins.then_inc(p_s["gu"], 1)

            turn_in(0)
            gate_up(0)
            turn_in(1)
            for e in range(NE):
                pe.wait_ge(p_s["act"], e + 1)
                if e:
                    pe.wait_ge(p_s["ae"], e)
                for k in range(2):
                    ins = nc.tensor.transpose(PS[:, 4, k * P:(k + 1) * P], pact[e % 2][:, k * P:(k + 1) * P], ident)
                ins.then_inc(p_s["at"], 1)
                if e + 1 < NE:
                    gate_up(e + 1)
                if e + 2 < NE:
                    turn_in(e + 2)
                pe.wait_ge(p_s["ae"], e + 1)
                if e >= 2:
                    pe.wait_ge(e_[f"d{e % 2}"], 16 * (e // 2))
                if e:
                    pe.wait_ge(p_s["oa"], e)
                    pe.wait_ge(p_s["od"], e)
                for h in range(2):
                    for k in range(2):
                        ins = nc.tensor.matmul(PS[:, 5 + h, :], pactT[e % 2][:, k, :],
                                               dn_w[e % 2][:, k, 512 * h:512 * h + 512], start=(k == 0), stop=(k == 1))
                ins.then_inc(p_s["dn"], 1)
            pe.wait_ge(p_s["xa"], NE)
            for i in range(TT):
                m = P if i < 4 else TS
                pe.wait_ge(p_s["yc"], i + 1)
                if i >= 2:
                    pe.wait_ge(p_s["yx"], DT * (i - 1))
                for k in range(DT):
                    ins = nc.tensor.transpose(PS[:, 2 * (i % 2) + k // 4, (k % 4) * P:(k % 4) * P + m],
                                              yg[0][0:m, i, k * P:(k + 1) * P], ident[0:m, 0:m])
                ins.then_inc(p_s["yt"], 1)

        def sparse_act(act, t0):
            def turned_in(e):
                if e >= NE:
                    return
                act.wait_ge(p_s["tx"], e + 1)
                if e >= 2:
                    act.wait_ge(p_s["gu"], e - 1)
                nc.scalar.copy(xeT[e % 2][:, 0:4, :].rearrange("p k n -> p (k n)"), PS[:, 0, :]).then_inc(p_s["xa"], 1)

            def gate(e):
                if e >= NE:
                    return
                act.wait_ge(p_s["gu"], e + 1)
                if e >= 2:
                    act.wait_ge(p_s["act"], e - 1)
                nc.scalar.activation(pth[e % 2][:, :], PS[:, 2 + e % 2, 0:FE], ACT.Tanh, scale=0.5)\
                    .then_inc(p_s["th"], 1)

            turned_in(0)
            gate(0)
            turned_in(1)
            for e in range(NE):
                act.wait_ge(p_s["at"], e + 1)
                if e >= 2:
                    act.wait_ge(p_s["dn"], e - 1)
                nc.scalar.copy(pactT[e % 2][:, :, :].rearrange("p k n -> p (k n)"), PS[:, 4, 0:2 * P])\
                    .then_inc(p_s["ae"], 1)
                gate(e + 1)
                turned_in(e + 2)
                act.wait_ge(p_s["dn"], e + 1)
                if e >= 2:
                    act.wait_ge(p_s[f"y{e % 2}"], 16 * (e // 2))
                nc.scalar.copy(pout[e % 2][:, 0:512], PS[:, 5, :]).then_inc(p_s["oa"], 1)
                act.wait_ge(p_s["oa"], e + 1)
                act.wait_ge(p_s["od"], e + 1)
                act.dma_start(d["ys_d"][e * P:(e + 1) * P, :], pout[e % 2][:, :]).then_inc(p_s[f"y{e % 2}"], 16)
            act.wait_ge(s_gath, t0 + 160)
            for i in range(TT):
                m = P if i < 4 else TS
                nc.scalar.activation(yg[1][0:m, i, :], yg[1][0:m, i, :], ACT.Copy, scale=rm[0:m, 6, i:i + 1])\
                    .then_inc(p_s["y2"], 1)

        def sparse_dve(dve, ch, t0):
            V = nc.vector

            def turned_in(e):
                if e >= NE:
                    return
                dve.wait_ge(p_s["tx"], e + 1)
                if e >= 2:
                    dve.wait_ge(p_s["gu"], e - 1)
                V.tensor_copy(xeT[e % 2][:, 4:8, :].rearrange("p k n -> p (k n)"), PS[:, 1, :]).then_inc(p_s["xd"], 1)

            def gated(e):
                if e >= NE:
                    return
                dve.wait_ge(p_s["th"], e + 1)
                if e >= 2:
                    dve.wait_ge(p_s["at"], e - 1)
                ch.link(V.scalar_tensor_tensor(pact[e % 2][:, :], pth[e % 2][:, :], 1.0, PS[:, 2 + e % 2, 0:FE],
                                               ALU.add, ALU.mult))
                V.tensor_tensor(pact[e % 2][:, :], pact[e % 2][:, :], PS[:, 2 + e % 2, FE:2 * FE], ALU.mult)\
                    .then_inc(p_s["act"], 1)

            turned_in(0)
            gated(0)
            turned_in(1)
            for e in range(NE):
                gated(e + 1)
                turned_in(e + 2)
                dve.wait_ge(p_s["dn"], e + 1)
                if e >= 2:
                    dve.wait_ge(p_s[f"y{e % 2}"], 16 * (e // 2))
                V.tensor_copy(pout[e % 2][:, 512:1024], PS[:, 6, :]).then_inc(p_s["od"], 1)
            for i in range(TT):
                m = P if i < 4 else TS
                dve.wait_ge(p_s["y2"], i + 1)
                V.scalar_tensor_tensor(yg[0][0:m, i, :], yg[0][0:m, i, :], rm[0:m, 5, i:i + 1], yg[1][0:m, i, :],
                                       ALU.mult, ALU.add).then_inc(p_s["yc"], 1)
            for i in range(TT):
                m, g = (P, 0) if i < 4 else (TS, 1)
                dve.wait_ge(p_s["yt"], i + 1)
                for k in range(DT):
                    V.scalar_tensor_tensor(xT[:, k, i * P:i * P + m],
                                           PS[:, 2 * (i % 2) + k // 4, (k % 4) * P:(k % 4) * P + m],
                                           half_gt2[:, k, g:g + 1], xT[:, k, i * P:i * P + m], ALU.mult, ALU.add)\
                        .then_inc(p_s["yx"], 1)

        def final_norm(block):
            s = nm["n1"]

            @block.scalar
            def _(act):
                norm_x_act(act, s)
                act.wait_ge(s["g"], 2 * DT)
                act.dma_start(d["out_y"], hT[:, :, :]).then_inc(s["out"], 16)
                act.wait_ge(s["out"], 16)

            @block.tensor
            def _(pe):
                norm_x_pe(pe, s)

            @block.gpsimd
            def _(pool):
                norm_pow(pool, s)

            @block.vector
            def _(dve):
                norm_x_dve(dve, s, lambda k, g: fin_g[:, k:k + 1])

        with nc.Block() as block:
            @block.sync
            def _(sp):
                sp.dma_start(xT[:, :, :], d["x"]).then_inc(s_const, 16)
                sp.dma_start(cst[:, :], d["const"]).then_inc(s_const, 16)
                sp.dma_start(c_tmp[:, :, :], d["c"]).then_inc(s_const, 16)
                sp.dma_start(fin_g[:, :], d["final_g"]).then_inc(s_const, 16)
                sp.wait_ge(s_const, 64)

            @block.gpsimd
            def _(pool):
                nc.gpsimd.memset(minus_half[:, :], -0.5)
                nc.gpsimd.memset(rs_in[:, :], 1.0)

            @block.scalar
            def _(act):
                act.wait_ge(s_const, 64)
                nc.scalar.activation(silu_c[:, :, :], c_tmp[:, :, :], ACT.Tanh, scale=0.5).then_inc(s_c, 1)

            @block.vector
            def _(dve):
                ch = Chain(dve, dch)
                dve.wait_ge(s_const, 64)
                nc.vector.tensor_copy(ones_b[:, :], ones)
                nc.vector.tensor_tensor(before[:, :], ones, c_("before"), ALU.mult)
                dve.wait_ge(s_c, 1)
                ch.link(nc.vector.tensor_scalar(silu_c[:, :, :], silu_c[:, :, :], 0.5, 0.5, ALU.mult, ALU.add))
                ch.link(nc.vector.tensor_tensor(silu_c[:, :, :], silu_c[:, :, :], c_tmp[:, :, :], ALU.mult))

        nums = sorted(s.num for s in sems)
        assert nums[-1] - nums[0] == len(nums) - 1, "semaphores of the kernel are neighbours"
        clear = range(nums[0], nums[-1] + 1)
        nc.all_engine_barrier(sems_to_clear=clear)

        with nc.Fori(0, DEPTH) as layer:
            def L(name):
                return d[name][bass.ds(layer, 1)]

            lay[0] = L

            with nc.Block() as block:
                @block.sync
                def _(sp):
                    sp.dma_start(prm[:, :], L("params").rearrange("l p n -> p (l n)")).then_inc(s_prm, 16)
                    sp.dma_start(lora[:, :, :], L("lora").rearrange("l p a n -> p (l a) n")).then_inc(s_lora, 16)
                    sp.dma_start(shift_in[:, :], L("shift").rearrange("l p n -> p (l n)")).then_inc(s_lora, 16)
                    sp.dma_start(router_w[:, :, :], L("router").rearrange("l p k n -> p (l k) n")).then_inc(s_lora, 16)
                    sp.dma_start(router_b[:, :], L("router_b").rearrange("l p n -> p (l n)")).then_inc(s_lora, 16)
                    for n in range(UNITS):
                        if n == U_AD2:
                            sp.wait_ge(zeros_set, 1)
                            for e in range(NE):
                                sp.dma_start(d["xs_d"][e * P:(e + 1) * P, :], zeros[:, :]).then_inc(s_zero, 16)
                        if n == U_UK:
                            att_sp(sp)
                        if n >= RING:
                            sp.wait_ge(unit_done, n - RING + 1)
                        sp.dma_start(ring[:, n % RING, :], L("wstream")[:, n].rearrange("l p w -> p (l w)"))\
                            .then_inc(ring_full[n % RING], 16)
                    att_out_sp(sp)
                    route_sp(sp)

                @block.tensor
                def _(pe):
                    def turn(g):
                        pe.wait_ge(ada_row, g + 1)
                        for j in range(4 * g, 4 * g + 4):
                            ins = nc.tensor.transpose(PS[:, 4, 2 * j:2 * j + 2], mod_row[0:2, j * P:(j + 1) * P],
                                                      ident[0:2, 0:2])
                        return ins
                    for n in range(U_ADA, U_CV):
                        g, j = n // 4, n % 4
                        w = unit_wait(pe, n)
                        if j == 0 and g >= 4:
                            pe.wait_ge(ada_row, g - 3)
                        for k in range(DT):
                            ins = nc.tensor.matmul(PS[0:2, g % 4, j * P:(j + 1) * P], silu_c[:, k, :], w[:, k, :],
                                                   start=(k == 0), stop=(k == DT - 1))
                        ins.then_inc(unit_done, 1)
                        if j == 3 and g >= 1:
                            turn(g - 1)
                    turn(3).then_inc(ada_tp, 1)
                    pe.wait_ge(ada_row, 4)
                    norm_x_pe(pe, nm["n1"])
                    pe.wait_ge(mod_ready, 1)
                    pe.wait_ge(nm["n1"]["out"], 2 * DT)
                    for i in range(4):
                        unit_mm(pe, U_CV + i, i)
                    rwkv_in_pe(pe)
                    s = nm["cv"]
                    pe.wait_ge(rw_pr, 24)
                    pe.wait_ge(cv_y, 2)
                    for t in range(2):
                        for h in range(2):
                            ins = nc.tensor.matmul(PS[:, h, 0:CYW // 2], ones, cy[:, t, h * 287:(h + 1) * 287],
                                                   start=(t == 0), stop=(t == 1))
                    ins.then_inc(cv_mu, 1)
                    pe.wait_ge(s["sq"], 2)
                    for t in range(2):
                        for h in range(2):
                            ins = nc.tensor.matmul(PS[0:1, 4 + h, 0:CYW // 2], ones[:, 0:1],
                                                   csq[:, t, h * 287:(h + 1) * 287], start=(t == 0), stop=(t == 1))
                    ins.then_inc(s["row"], 1)
                    norm_cols_pe(pe, s, CYW - TS)
                    norm_pe_tail(pe, s)
                    rwkv_pe(pe)
                    att_pe(pe)
                    merge_pe(pe)
                    route_pe(pe)

                @block.scalar
                def _(act):
                    norm_x_act(act, nm["n1"])
                    act.wait_ge(mod_ready, 1)
                    act.dma_start(cb[:, :, CW - 1 + TP:CW - 1 + TP + CW - 1],
                                  L("state_conv").rearrange("l p a n -> p (l a) n")).then_inc(cv_state, 16)
                    norm_shift_act(act, nm["n1"], 0)
                    for i in range(2):
                        act.wait_ge(unit_done, U_CV + i + 1)
                        for h in range(2):
                            nc.scalar.activation(cth[:, i, h * HALF:(h + 1) * HALF], PS[:, 2 * i + h, 0:HALF],
                                                 ACT.Tanh, scale=0.5).then_inc(cv_th, 1)
                    act.wait_ge(cv_glu, 6)
                    act.wait_ge(cv_state, 16)
                    act.dma_start(L("out_conv")[:, 0].rearrange("l p a n -> p (l a) n"),
                                  cb[:, :, TP:TP + CW - 1]).then_inc(cv_out, 16)
                    act.dma_start(L("out_conv")[:, 1].rearrange("l p a n -> p (l a) n"),
                                  cb[:, :, CBW - (CW - 1):CBW]).then_inc(cv_out, 16)
                    rwkv_in_act(act)
                    act.wait_ge(cv_cent, 4)
                    for t in range(2):
                        nc.scalar.activation(csq[:, t, :], cy[:, t, :], ACT.Square).then_inc(nm["cv"]["sq"], 1)
                    act.wait_ge(cv_zh, 4)
                    nc.scalar.activation(cth[:, :, :], cT[:, :, :], ACT.Tanh).then_inc(cv_t2, 1)
                    act.wait_ge(cv_out, 32)
                    rwkv_act(act)
                    att_act(act)
                    merge_act(act)
                    route_act(act)

                @block.gpsimd
                def _(pool):
                    nc.gpsimd.memset(zeros[:, :], 0.0).then_inc(zeros_set, 1)
                    norm_pow(pool, nm["n1"])
                    pool.wait_ge(mod_ready, 1)
                    nc.gpsimd.memset(cb[:, :, 0:CW - 1], 0.0).then_inc(cv_init, 1)
                    norm_pow(pool, nm["cv"])
                    rwkv_pool(pool)
                    att_pool(pool)
                    merge_pool(pool)
                    route_pool(pool)

                @block.vector
                def _(dve):
                    ch = Chain(dve, dch)
                    for g in range(4):
                        dve.wait_ge(unit_done, 4 * g + 4)
                        nc.vector.tensor_copy(mod_row[0:2, 512 * g:512 * g + 512], PS[0:2, g % 4, :])\
                            .then_inc(ada_row, 1)
                    dve.wait_ge(ada_tp, 1)
                    dve.wait_ge(s_prm, 16)
                    mod_part(0, 16, 4)
                    dve.wait_ge(mod_ready, 1)
                    for g in range(2):
                        ch.mark(nc.vector.scalar_tensor_tensor(gain1[:, :, g], mod[:, DT:2 * DT, g], 1.0,
                                                               p_("norm1_g"), ALU.add, ALU.mult))
                    ch.wait(ch.n)
                    norm_x_dve(dve, nm["n1"], lambda k, g: gain1[:, k, g:g + 1])
                    for t in range(2):
                        dve.wait_ge(cv_th, 2 * t + 2)
                        ch.mark(nc.vector.tensor_scalar(cth[:, t, :], cth[:, t, :], 0.5, 0.5, ALU.mult, ALU.add))
                    ch.wait(ch.n)
                    for t in range(2):
                        dve.wait_ge(unit_done, U_CV + 3 + t)
                        b = 2 * (2 + t)
                        for o, lo, hi, bank in ((CW - 1, 0, HALF, b), (CW - 1 + HALF, HALF, TP, b + 1),
                                                (CBW - TS, TP, T, b + 1)):
                            src = lo - HALF * (bank - b)
                            nc.vector.tensor_tensor(cb[:, t, o:o + hi - lo], cth[:, t, lo:hi],
                                                    PS[:, bank, src:src + hi - lo], ALU.mult).then_inc(cv_glu, 1)
                    dve.wait_ge(cv_glu, 6)
                    dve.wait_ge(cv_init, 1)
                    dve.wait_ge(cv_state, 16)
                    for k in range(CW):
                        for t in range(2):
                            tap = p_("dw", t * CW + k)
                            if k == 0:
                                ins = nc.vector.tensor_scalar(cy[:, t, :], cb[:, t, 0:CYW], tap, p_("dw_b", t),
                                                              ALU.mult, ALU.add)
                            else:
                                ch.wait(ch.n if k == CW - 1 and t else ch.n - 1)
                                ins = nc.vector.scalar_tensor_tensor(cy[:, t, :], cb[:, t, k:k + CYW], tap,
                                                                     cy[:, t, :], ALU.mult, ALU.add)
                            if k == CW - 1:
                                ins.then_inc(cv_y, 1)
                            else:
                                ch.mark(ins)
                    dve.wait_ge(cv_mu, 1)
                    dve.wait_ge(cv_y, 2)
                    for t in range(2):
                        for h in range(2):
                            nc.vector.scalar_tensor_tensor(cy[:, t, h * 287:(h + 1) * 287], PS[:, h, 0:287],
                                                           -1.0 / CD, cy[:, t, h * 287:(h + 1) * 287],
                                                           ALU.mult, ALU.add).then_inc(cv_cent, 1)
                    s = nm["cv"]
                    dve.wait_ge(s["row"], 1)
                    for h in range(2):
                        nc.vector.tensor_copy(row[0:1, 0, h * 287:(h + 1) * 287], PS[0:1, 4 + h, 0:287])\
                            .then_inc(s["srow"], 1)
                    norm_cols_dve(dve, s, CD, 1e-5)
                    dve.wait_ge(s["bc"], 1)
                    dve.wait_ge(cv_cent, 4)
                    for t in range(2):
                        for src, lo, hi, bank in ((0, 0, TP, 3), (CYW - TS, TP, T, 4)):
                            ch.link(nc.vector.scalar_tensor_tensor(
                                cT[:, t, lo:hi], cy[:, t, src:src + hi - lo], p_("cln_g", t), PS[:, bank, 0:hi - lo],
                                ALU.mult, ALU.mult))
                            nc.vector.tensor_scalar(cT[:, t, lo:hi], cT[:, t, lo:hi], p_("cln_b", t), 0.5,
                                                    ALU.add, ALU.mult).then_inc(cv_zh, 1)
                    dve.wait_ge(cv_zh, 4)
                    dve.wait_ge(cv_t2, 1)
                    nc.vector.scalar_tensor_tensor(cT[:, :, :], cth[:, :, :], 1.0, cT[:, :, :],
                                                   ALU.add, ALU.mult).then_inc(cv_done, 1)
                    rwkv_dve(dve, ch)
                    att_dve(dve, ch)
                    merge_dve(dve, ch)
                    route_dve(dve, ch)

            nc.all_engine_barrier(sems_to_clear=clear)
            sp, pe, act, pool, dve = nc.sync, nc.tensor, nc.scalar, nc.gpsimd, nc.vector
            enough = nc.values_load(fits[0:1, 0:1], min_val=0, max_val=1)
            with nc.If(enough > 0):
                sparse_pool(pool, 160 * layer)
                sparse_sp(sp, 160 * layer)
                sparse_pe(pe)
                sparse_act(act, 160 * layer)
                sparse_dve(dve, Chain(dve, dch), 160 * layer)
            with nc.Else():
                dense_pool(pool)
                dense_sp(sp, 160 * layer)
                dense_pe(pe)
                dense_act(act)
                dense_dve(dve, Chain(dve, dch))
            nc.all_engine_barrier(sems_to_clear=clear)

        with nc.Block() as block:
            final_norm(block)


def const_array():
    c = np.zeros((P, NCONST), np.float32)

    def put(name, v):
        o, n = CONST[name]
        c[:, o:o + n] = np.asarray(v, np.float32).reshape(P, n)
    i, j = np.indices((P, P))
    same = (i // 64 == j // 64)
    put("ident", i == j)
    put("ones", np.ones((P, P)))
    put("blk", same)
    strict, incl = same & (i < j), same & (i <= j)
    put("gram", np.stack([strict, strict, incl, incl], 1))
    up = lambda b: (i // (2 * b) == j // (2 * b)) & (i // b < j // b)
    put("first_t", up(1))
    put("first", up(1).T)
    put("levels", np.stack([-1.0 * up(b) for b in (2, 4, 8, 16, 32)], 1))
    rot = np.zeros((P, ROPE))
    for m in range(16):
        rot[NOPE + 16 + m, m] = -1.0
        rot[NOPE + m, 16 + m] = 1.0
    put("rot", rot)
    pos = np.concatenate([np.arange(TP), PAST + np.arange(TS)]).astype(np.float32)
    inv = (np.float32(10000.0) ** (-np.arange(16, dtype=np.float32) / 16)).astype(np.float32)
    ang = pos[None, :] * inv[:, None]
    tab = np.zeros((2, P, T), np.float32)
    for q in range(2):
        tab[0, NOPE + 16 * q:NOPE + 16 * q + 16] = np.cos(ang)
        tab[1, NOPE + 16 * q:NOPE + 16 * q + 16] = np.sin(ang)
    for b in range(4):
        tab[0, QK + b, 2 * b * CHUNK:(2 * b + 1) * CHUNK] = 1.0
        tab[1, QK + b, (2 * b + 1) * CHUNK:(2 * b + 2) * CHUNK] = -1e30
    put("cos", tab[0])
    put("sin", tab[1])
    put("valid", np.arange(TT)[None, :] * P + np.arange(P)[:, None] < T)
    put("slot0", np.broadcast_to(np.arange(NE) * float(P), (P, NE)))
    put("falling", np.broadcast_to(4.0 - np.arange(4), (P, 4)))
    put("before", i < j)
    put("scan", np.broadcast_to((np.arange(T) % CHUNK != 0), (P, T)))
    return c


def host(inputs):
    g = {k: np.asarray(v) for k, v in inputs.items()}
    f32 = np.float32

    def rows(w):
        l, k, m = w.shape
        return w.reshape(l, k // P, P, m).transpose(0, 2, 1, 3)

    def cols(v):
        return v.reshape(v.shape[0], -1, P).transpose(0, 2, 1)

    units = np.zeros((DEPTH, UNITS, P, UW), f32)

    def put(n, w):
        units[:, n, :, :w.shape[2] * w.shape[3]] = w.reshape(DEPTH, P, -1)

    ada, w_in = rows(g["ada_w"]), rows(g["w_in"])
    for j in range(48):
        put(U_ADA + j if j < 16 else U_AD2 + j - 16 if j < 28 else U_AD3 + j - 28, ada[..., j * P:(j + 1) * P])
    mla, rw = QL + KVL + ROPE, QL + KVL + ROPE + 1024
    cv, gates = rw, rw + 2 * CD
    for i, o in enumerate((2, 3, 0, 1)):
        put(U_CV + i, w_in[..., cv + o * P:cv + (o + 1) * P])
    for i in range(8):
        put(U_RW + i, w_in[..., mla + i * P:mla + (i + 1) * P])
    for i in range(5):
        put(U_MLA + i, w_in[..., i * P:(i + 1) * P])
    put(U_MLA + 5, w_in[..., QL + KVL:QL + KVL + ROPE])
    put(U_UK, rows(g["w_uk"].reshape(DEPTH, KVL, -1)))
    put(U_UV, rows(g["w_uv"].reshape(DEPTH, KVL, -1)))
    w_out = rows(g["w_out"])
    proj = np.concatenate([rows(g["proj_a"]), rows(g["proj_b"]), rows(g["proj_c"])], 2)
    for i in range(DT):
        for b in range(3):
            o = gates + b * DM + i * P
            put(U_MERGE + 4 * i + b, w_in[..., o:o + P])
        put(U_MERGE + 4 * i + 3, proj[..., i * P:(i + 1) * P])
        put(U_OUT + i, w_out[..., i * P:(i + 1) * P])
    dw = g["conv_dw"].reshape(DEPTH, CW, 2, P).transpose(0, 3, 2, 1).reshape(DEPTH, P, 2 * CW)
    par = {"ada_b": cols(g["ada_b"]), "norm1_g": cols(g["norm1_g"]), "norm2_g": cols(g["norm2_g"]),
           "q_norm_g": cols(g["q_norm_g"]), "kv_norm_g": cols(g["kv_norm_g"]), "mu": cols(g["rwkv_mu"]),
           "w0": cols(g["rwkv_w0"]), "a0": cols(g["rwkv_a0"]), "k_k": cols(g["rwkv_k_k"]), "k_a": cols(g["rwkv_k_a"]),
           "r_k": cols(g["rwkv_r_k"].reshape(DEPTH, -1)), "ln_g": cols(g["rwkv_ln_g"]), "ln_b": cols(g["rwkv_ln_b"]),
           "dw": dw, "dw_b": cols(g["conv_dw_b"]), "cln_g": cols(g["conv_ln_g"]), "cln_b": cols(g["conv_ln_b"])}
    params = np.concatenate([par[n] for n in PARAM], 2)
    lora = np.zeros((DEPTH, P, 3, RH * 64), f32)
    lora[:, 0:64, 0] = g["rwkv_w2"]
    lora[:, 64:128, 1] = g["rwkv_a2"]
    lora[:, :, 2] = g["rwkv_g2"]
    x = np.concatenate([g["x_prompt"][0], g["x_sample"][0]], 0)
    feat = lambda a: a.reshape(a.shape[0], DT, P).transpose(2, 1, 0)
    c = np.concatenate([g["c_prompt"], g["c_sample"]], 0)
    moe_gu = np.concatenate([g["moe_w_gate"], g["moe_w_up"]], 3).reshape(DEPTH, NE, DT, P, 2 * FE)\
        .transpose(0, 1, 3, 2, 4).reshape(DEPTH, NE, P, DT * 2 * FE)
    moe_dn = g["moe_w_down"].reshape(DEPTH, NE, 2, P, DM).transpose(0, 1, 3, 2, 4).reshape(DEPTH, NE, P, 2 * DM)
    router = np.concatenate([g["router_group_w"], g["router_expert_w"]], 2)
    router_b = np.concatenate([g["router_group_b"], g["router_expert_b"]], 1)
    conv = g["state_conv"][:, 0].reshape(DEPTH, CW - 1, 2, P).transpose(0, 3, 2, 1)
    arrays = dict(x=feat(x), c=feat(c), const=const_array(), params=params, lora=lora, wstream=units,
                  qup=rows(g["q_up"]).reshape(DEPTH, P, -1), moe_gu=moe_gu, moe_dn=moe_dn, router=rows(router),
                  router_b=np.broadcast_to(router_b[:, None], (DEPTH, P, 20)), final_g=g["final_g"].reshape(DT, P).T,
                  cache_lat=g["cache_kv_latent"][:, 0].reshape(DEPTH, PAST, 2, P).transpose(0, 3, 2, 1),
                  cache_rope=g["cache_k_rope"][:, 0].transpose(0, 2, 1),
                  shift=cols(g["state_rwkv_shift"][:, 0]), wkv=g["state_rwkv_wkv"][:, 0].transpose(0, 1, 3, 2),
                  state_conv=conv)
    return {k: np.ascontiguousarray(v) for k, v in arrays.items()}


SCRATCH = dict(xs_d=(NE * P, DM), ys_d=(NE * P, DM))
OUTS = dict(out_y=(P, DT, T), out_lat=(DEPTH, P, 2, T), out_rope=(DEPTH, ROPE, T), out_shift=(DEPTH, P, 2, 8),
            out_wkv=(DEPTH, 2, RH, 64, 64), out_conv=(DEPTH, 2, P, 2, CW - 1))


def kernel(**inputs):
    import concourse.bacc as _bacc
    from concourse.bass_utils import run_bass_kernel_spmd as _run

    arrays = host(inputs)
    nc = _bacc.Bacc("TRN2", target_bir_lowering=False, num_devices=1)
    d = {k: nc.dram_tensor(k, v.shape, F32, kind="ExternalInput").ap() for k, v in arrays.items()}
    d |= {k: nc.dram_tensor(k, s, F32, kind="ExternalOutput").ap() for k, s in OUTS.items()}
    d |= {k: nc.dram_tensor(k, s, F32).ap() for k, s in SCRATCH.items()}
    build(nc, d)
    r = _run(nc, [arrays], core_ids=[0])
    o = {k: r.results[0][k] for k in OUTS}
    y = o["out_y"].transpose(2, 1, 0).reshape(T, DM)
    lat = o["out_lat"].transpose(0, 3, 2, 1).reshape(DEPTH, T, KVL)
    rope = o["out_rope"].transpose(0, 2, 1)
    shift = o["out_shift"].transpose(0, 2, 3, 1).reshape(DEPTH, 2, 1024)
    wkv = o["out_wkv"].transpose(0, 1, 2, 4, 3)
    conv = o["out_conv"].transpose(0, 1, 4, 3, 2).reshape(DEPTH, 2, CW - 1, CD)
    res = (y[None, :TP], y[None, TP:], lat[:, None, :TP], rope[:, None, :TP], shift[:, 0:1], wkv[:, 0:1], conv[:, 0:1],
           lat[:, None, TP:], rope[:, None, TP:], shift[:, 1:2], wkv[:, 1:2], conv[:, 1:2])
    return tuple(np.ascontiguousarray(a) for a in res)
```
